# Optimizing a Trainium2 kernel written in Bass

```python
import jax, jax.numpy as jnp
from jax import lax
import numpy as np

D_MODEL = 1024
BATCH = 1
SEQ = 1024
DEPTH = 1

N_META = 16
D_MIX = D_MODEL
RWKV_W = D_MIX // 2
RWKV_HEAD = 64
RWKV_HEADS = RWKV_W // RWKV_HEAD
DECAY_RANK = 64
AAA_RANK = 64
GATE_RANK = 160
LRU_W = D_MIX - RWKV_W
LRU_BLOCKS = 8
LRU_BLOCK = LRU_W // LRU_BLOCKS
CONV_WIDTH = 4
LRU_C = 8.0
N_GROUPS = 4
EXPERTS_PER_GROUP = 8
N_EXPERTS = N_GROUPS * EXPERTS_PER_GROUP
TOP_K = 2
D_EXPERT = 512
MOE_BLOCK = 128
LN_EPS = 1e-5
GN_EPS = 64e-5
DEEPNORM_ALPHA = (2 * DEPTH) ** 0.25
DEEPNORM_BETA = (8 * DEPTH) ** -0.25

OFF_R = 0
OFF_K = OFF_R + RWKV_W
OFF_V = OFF_K + RWKV_W
OFF_W = OFF_V + RWKV_W
OFF_A = OFF_W + DECAY_RANK
OFF_G = OFF_A + AAA_RANK
RWKV_COLS = OFF_G + GATE_RANK
OFF_LX = RWKV_COLS
OFF_LG = OFF_LX + LRU_W
N_IN = OFF_LG + LRU_W

kernel_name = "hymba_rwkv7_rglru_hmoe_deepnorm"

F32 = jnp.float32

def layer_norm(x, g, b):
    xf = x.astype(F32)
    mu = jnp.mean(xf, -1, keepdims=True)
    var = jnp.mean(jnp.square(xf - mu), -1, keepdims=True)
    return ((xf - mu) * lax.rsqrt(var + LN_EPS) * g.astype(F32) + b.astype(F32)).astype(x.dtype)

def rwkv7_recurrence(r, w, k, v, a, b):
    Bs, T, H, N = r.shape
    xs = tuple(jnp.moveaxis(t, 1, 0) for t in (r, w, k, v, a, b))

    def step(S, inp):
        r_t, w_t, k_t, v_t, a_t, b_t = inp
        sa = jnp.einsum('bhvk,bhk->bhv', S, a_t)
        S = S * w_t[:, :, None, :] + sa[..., None] * b_t[:, :, None, :] + v_t[..., None] * k_t[:, :, None, :]
        return S, jnp.einsum('bhvk,bhk->bhv', S, r_t)

    _, ys = lax.scan(step, jnp.zeros((Bs, H, N, N), F32), xs)
    return jnp.moveaxis(ys, 0, 1)

def linear_scan(a, b):
    def comb(left, right):
        al, bl = left
        ar, br = right
        return al * ar, ar * bl + br
    _, h = lax.associative_scan(comb, (a, b), axis=1)
    return h

def token_mixers(h, w_in, mu_shift, w0, w_decay_up, a0, w_a_up, w_g_up, k_k, k_a, r_k, gn_g, gn_b,
                 conv_w, conv_b, w_rg, b_rg, w_ig, b_ig, lru_lambda, w_out):
    Bs, T, _ = h.shape
    u = h @ w_in

    ur = u[..., :RWKV_COLS]
    ur_prev = jnp.pad(ur[:, :-1], ((0, 0), (1, 0), (0, 0)))
    ur = (ur + (ur_prev - ur) * mu_shift).astype(F32)
    r = ur[..., OFF_R:OFF_K]
    k = ur[..., OFF_K:OFF_V]
    v = ur[..., OFF_V:OFF_W]
    zw = ur[..., OFF_W:OFF_A]
    za = ur[..., OFF_A:OFF_G]
    zg = ur[..., OFF_G:RWKV_COLS]
    w_log = -jax.nn.softplus(-(w0.astype(F32) + jnp.tanh(zw) @ w_decay_up.astype(F32))) - 0.5
    decay = jnp.exp(-jnp.exp(w_log))
    a = jax.nn.sigmoid(a0.astype(F32) + za @ w_a_up.astype(F32))
    g = jax.nn.sigmoid(zg) @ w_g_up.astype(F32)
    hd = lambda t: t.reshape(Bs, T, RWKV_HEADS, RWKV_HEAD)
    kk = hd(k * k_k.astype(F32))
    kk = kk / jnp.maximum(jnp.sqrt(jnp.sum(kk * kk, -1, keepdims=True)), 1e-12)
    k = k * (1.0 + (a - 1.0) * k_a.astype(F32))
    rh, kh, vh = hd(r), hd(k), hd(v)
    y = rwkv7_recurrence(rh, hd(decay), kh, vh, -kk, kk * hd(a))
    ym = jnp.mean(y, -1, keepdims=True)
    yv = jnp.mean(jnp.square(y - ym), -1, keepdims=True)
    y = ((y - ym) * lax.rsqrt(yv + GN_EPS)).reshape(Bs, T, RWKV_W) * gn_g.astype(F32) + gn_b.astype(F32)
    bonus = jnp.sum(rh * kh * r_k.astype(F32), -1, keepdims=True) * vh
    y_rwkv = ((y + bonus.reshape(Bs, T, RWKV_W)) * g).astype(h.dtype)

    xl = u[..., OFF_LX:OFF_LG]
    gl = u[..., OFF_LG:N_IN]
    xc = lax.conv_general_dilated(xl, conv_w[:, None, :], window_strides=(1,),
                                  padding=[(CONV_WIDTH - 1, 0)],
                                  dimension_numbers=('NWC', 'WIO', 'NWC'),
                                  feature_group_count=LRU_W) + conv_b
    xb = xc.reshape(Bs, T, LRU_BLOCKS, LRU_BLOCK)
    gate_r = jax.nn.sigmoid((jnp.einsum('btni,nij->btnj', xb, w_rg).reshape(Bs, T, LRU_W) + b_rg).astype(F32))
    gate_i = jax.nn.sigmoid((jnp.einsum('btni,nij->btnj', xb, w_ig).reshape(Bs, T, LRU_W) + b_ig).astype(F32))
    log_a = LRU_C * gate_r * jax.nn.log_sigmoid(lru_lambda.astype(F32))
    mult = jnp.sqrt(jnp.maximum(-jnp.expm1(2.0 * log_a), 0.0))
    hs = linear_scan(jnp.exp(log_a), mult * gate_i * xc.astype(F32))
    y_lru = (hs * jax.nn.gelu(gl.astype(F32))).astype(h.dtype)

    return jnp.concatenate([y_rwkv, y_lru], axis=-1) @ w_out

def hierarchical_moe(h, w_rgrp, b_rgrp, w_rexp, b_rexp, w_gate, w_up, w_down):
    Bs, T, D = h.shape
    ht = h.reshape(-1, D)
    M = ht.shape[0]
    A = M * TOP_K
    glog = (ht @ w_rgrp + b_rgrp).astype(F32)
    gprob = jax.nn.softmax(glog, -1)
    _, g_sel = lax.top_k(glog, 1)
    p_g = jnp.take_along_axis(gprob, g_sel, 1)[:, 0]
    elog = (ht @ w_rexp + b_rexp).astype(F32).reshape(M, N_GROUPS, EXPERTS_PER_GROUP)
    elog_g = jnp.take_along_axis(elog, g_sel[:, :, None], 1)[:, 0]
    top_v, top_i = lax.top_k(elog_g, TOP_K)
    gate = (p_g[:, None] * jax.nn.softmax(top_v, -1)).reshape(-1)
    eid = (g_sel * EXPERTS_PER_GROUP + top_i).reshape(-1)
    tok = jnp.repeat(jnp.arange(M), TOP_K)
    order = jnp.argsort(eid)
    eid_s, tok_s, gate_s = eid[order], tok[order], gate[order]
    counts = jnp.bincount(eid, length=N_EXPERTS)
    starts = jnp.cumsum(counts) - counts
    pcounts = (counts + MOE_BLOCK - 1) // MOE_BLOCK * MOE_BLOCK
    pends = jnp.cumsum(pcounts)
    pstarts = pends - pcounts
    dest = pstarts[eid_s] + (jnp.arange(A) - starts[eid_s])
    P = (A + N_EXPERTS * (MOE_BLOCK - 1) + MOE_BLOCK - 1) // MOE_BLOCK * MOE_BLOCK
    nblk = P // MOE_BLOCK
    buf = jnp.zeros((P, D), h.dtype).at[dest].set(ht[tok_s])
    blk_e = jnp.minimum(jnp.searchsorted(pends, jnp.arange(nblk) * MOE_BLOCK, side='right'), N_EXPERTS - 1)

    def expert_block(args):
        xblk, e = args
        return (jax.nn.silu(xblk @ w_gate[e]) * (xblk @ w_up[e])) @ w_down[e]

    ybuf = lax.map(expert_block, (buf.reshape(nblk, MOE_BLOCK, D), blk_e)).reshape(P, D)
    y = (ybuf[dest].astype(F32) * gate_s[:, None]).astype(h.dtype)
    out = jnp.zeros((M, D), h.dtype).at[tok_s].add(y)
    return out.reshape(Bs, T, D)

def setup_inputs(seed: int = 0) -> dict:
    key = jax.random.key(seed)
    ks = jax.random.split(key, 40)
    nrm = lambda k, shape, s: jax.random.normal(k, shape, F32) * s
    L, D = DEPTH, D_MODEL
    col_scale = jnp.ones((N_IN,), F32).at[OFF_V:OFF_W].set(DEEPNORM_BETA)
    u_lam = jax.random.uniform(ks[20], (L, LRU_W), F32, 0.9, 0.999) ** (1.0 / LRU_C)
    return {
        "x": nrm(ks[0], (BATCH, SEQ, D), 1.0),
        "meta": nrm(ks[1], (N_META, D), 1.0),
        "ln0_g": 1.0 + nrm(ks[2], (D,), 0.02),
        "ln0_b": nrm(ks[3], (D,), 0.02),
        "w_in": nrm(ks[4], (L, D, N_IN), D ** -0.5) * col_scale,
        "mu_shift": jax.random.uniform(ks[5], (L, RWKV_COLS), F32),
        "w0": jnp.linspace(-6.5, -1.5, RWKV_W, dtype=F32)[None] + nrm(ks[6], (L, RWKV_W), 0.1),
        "w_decay_up": nrm(ks[7], (L, DECAY_RANK, RWKV_W), 0.1 * DECAY_RANK ** -0.5),
        "a0": nrm(ks[8], (L, RWKV_W), 0.1),
        "w_a_up": nrm(ks[9], (L, AAA_RANK, RWKV_W), 0.1 * AAA_RANK ** -0.5),
        "w_g_up": nrm(ks[10], (L, GATE_RANK, RWKV_W), GATE_RANK ** -0.5),
        "k_k": 0.85 + nrm(ks[11], (L, RWKV_W), 0.02),
        "k_a": 1.0 + nrm(ks[12], (L, RWKV_W), 0.02),
        "r_k": nrm(ks[13], (L, RWKV_HEADS, RWKV_HEAD), 0.1),
        "gn_g": 1.0 + nrm(ks[14], (L, RWKV_W), 0.02),
        "gn_b": nrm(ks[15], (L, RWKV_W), 0.02),
        "conv_w": nrm(ks[16], (L, CONV_WIDTH, LRU_W), CONV_WIDTH ** -0.5),
        "conv_b": nrm(ks[17], (L, LRU_W), 0.02),
        "w_rg": nrm(ks[18], (L, LRU_BLOCKS, LRU_BLOCK, LRU_BLOCK), LRU_BLOCK ** -0.5),
        "b_rg": nrm(ks[19], (L, LRU_W), 0.02),
        "w_ig": nrm(ks[21], (L, LRU_BLOCKS, LRU_BLOCK, LRU_BLOCK), LRU_BLOCK ** -0.5),
        "b_ig": nrm(ks[22], (L, LRU_W), 0.02),
        "lru_lambda": jnp.log(u_lam) - jnp.log1p(-u_lam),
        "w_out": nrm(ks[23], (L, D_MIX, D), D_MIX ** -0.5 * DEEPNORM_BETA),
        "ln1_g": 1.0 + nrm(ks[24], (L, D), 0.02),
        "ln1_b": nrm(ks[25], (L, D), 0.02),
        "w_router_grp": nrm(ks[26], (L, D, N_GROUPS), D ** -0.5),
        "b_router_grp": nrm(ks[27], (L, N_GROUPS), 0.01),
        "w_router_exp": nrm(ks[28], (L, D, N_EXPERTS), D ** -0.5),
        "b_router_exp": nrm(ks[29], (L, N_EXPERTS), 0.01),
        "w_exp_gate": nrm(ks[30], (L, N_EXPERTS, D, D_EXPERT), D ** -0.5),
        "w_exp_up": nrm(ks[31], (L, N_EXPERTS, D, D_EXPERT), D ** -0.5),
        "w_exp_down": nrm(ks[32], (L, N_EXPERTS, D_EXPERT, D), D_EXPERT ** -0.5 * DEEPNORM_BETA),
        "ln2_g": 1.0 + nrm(ks[33], (L, D), 0.02),
        "ln2_b": nrm(ks[34], (L, D), 0.02),
    }

def reference(x, meta, ln0_g, ln0_b, w_in, mu_shift, w0, w_decay_up, a0, w_a_up, w_g_up, k_k, k_a, r_k,
              gn_g, gn_b, conv_w, conv_b, w_rg, b_rg, w_ig, b_ig, lru_lambda, w_out, ln1_g, ln1_b,
              w_router_grp, b_router_grp, w_router_exp, b_router_exp, w_exp_gate, w_exp_up, w_exp_down,
              ln2_g, ln2_b):
    Bs = x.shape[0]
    h = jnp.concatenate([jnp.broadcast_to(meta[None].astype(x.dtype), (Bs, N_META, D_MODEL)), x], axis=1)
    h = layer_norm(h, ln0_g, ln0_b)
    for l in range(DEPTH):
        mix = token_mixers(h, w_in[l], mu_shift[l], w0[l], w_decay_up[l], a0[l], w_a_up[l], w_g_up[l],
                           k_k[l], k_a[l], r_k[l], gn_g[l], gn_b[l], conv_w[l], conv_b[l], w_rg[l], b_rg[l],
                           w_ig[l], b_ig[l], lru_lambda[l], w_out[l])
        h = layer_norm(DEEPNORM_ALPHA * h + mix, ln1_g[l], ln1_b[l])
        ffn = hierarchical_moe(h, w_router_grp[l], b_router_grp[l], w_router_exp[l], b_router_exp[l],
                               w_exp_gate[l], w_exp_up[l], w_exp_down[l])
        h = layer_norm(DEEPNORM_ALPHA * h + ffn, ln2_g[l], ln2_b[l])
    return h[:, N_META:]


_drawn_inputs = setup_inputs


def setup_inputs(seed=0):
    import zlib

    import numpy as np

    out = dict(_drawn_inputs(seed))
    spreads = {}
    factors = {'w_decay_up': 8.0,
     'a0': 4.956,
     'w_a_up': 4.738,
     'k_k': 65.867,
     'k_a': 8.0,
     'gn_g': 8.0,
     'gn_b': 7.863,
     'b_rg': 64.0,
     'b_ig': 50.625,
     'b_router_grp': 20.434,
     'b_router_exp': 17.717,
     'ln2_g': 22.861,
     'ln2_b': 22.987,
     'conv_b': 3.35}
    for name, (base, spread) in spreads.items():
        noise = np.random.default_rng([zlib.crc32(name.encode()), seed]).standard_normal(out[name].shape)
        drawn = base * np.exp(spread * noise) if base else spread * noise
        out[name] = __import__('jax').numpy.asarray(drawn.astype(out[name].dtype))
    for name, factor in factors.items():
        out[name] = (out[name] * factor).astype(out[name].dtype)
    return out
```

```python
from contextlib import ExitStack

import concourse.bass as bass
from concourse import mybir

F32 = mybir.dt.float32
BF16 = mybir.dt.bfloat16
I32 = mybir.dt.int32
U32 = mybir.dt.uint32
ALU = mybir.AluOpType
ACT = mybir.ActivationFunctionType
AXX = mybir.AxisListType.X

D = 1024
SEQ = 1024
META = 16
P = 128
KD = D // P
NT = SEQ // P
HEAD = 64
PAIRS = 4
CH = 64
NCH = 17
TP = NCH * CH
PAD = TP - SEQ - META
TQ = SEQ + META + 1
Q0 = PAD - 1
SEG = TQ // 3
XQ = META + 1
DECAY = 0.6065306597126334
N_RWKV = 1824
GATE = 160
NG, EPG = 4, 8
NE = NG * EPG
FE = 512
KF = FE // P
CAP = P
OVER = 16
NBLK = NE + OVER
ALPHA = 2.0 ** 0.25
LN_EPS, GN_EPS = 1e-5, 64e-5


class Steps:

    def __init__(self, sem, names):
        self.sem, self.names = sem, list(names)

    def at(self, turn, name):
        return turn * len(self.names) + (self.names.index(name) + 1)


def build(nc, a, out, scratch):
    ctx = ExitStack()
    with ctx:
        def sem(name):
            return ctx.enter_context(nc.semaphore(name))

        WORDS = 53000
        big = ctx.enter_context(nc.sbuf_tensor("big", [P, WORDS], F32))
        ps = ctx.enter_context(nc.psum_tensor("ps", [P, 8, 512], F32))

        class Region:
            def __init__(self, at):
                self.at = at

            def take(self, *shape):
                n = 1
                for s in shape:
                    n *= s
                v = big[:, self.at:self.at + n]
                self.at += n
                assert self.at <= WORDS, self.at
                if len(shape) == 2:
                    v = v.rearrange("p (a b) -> p a b", b=shape[1])
                elif len(shape) == 3:
                    v = v.rearrange("p (a b c) -> p a b c", b=shape[1], c=shape[2])
                return v

        R = Region(0)
        ident = R.take(P)
        blk = R.take(2, HEAD)
        ident2 = R.take(HEAD)
        m_strict = R.take(2, HEAD)
        m_incl = R.take(HEAD)
        m_sub = R.take(6, HEAD)
        m_supT = R.take(2, HEAD)
        ones = R.take(P)
        ltri = R.take(P)
        lng = R.take(D)
        lnb = R.take(D)
        mu = R.take(15)
        prm = R.take(12, 4)
        (P_W0, P_A0, P_KK, P_KA, P_RK, P_GG, P_GB, P_CB, P_BR, P_BI, P_LAM, P_K1) = range(12)
        cw = R.take(4, 4)
        c8 = R.take(2, 4)
        lamt = R.take(6, 4)
        hprm = R.take(4, 4)
        eps = R.take(2)
        st6 = R.take(2, 6)
        mv = R.take(2)
        rstd = R.take(2)
        wc = R.take(PAIRS, NCH)
        wlr = R.take(512)
        BASE = R.at

        AR = R.take(PAIRS, 2, TP)
        BT = R.take(PAIRS, TP)
        KT = R.take(PAIRS, TP)
        VT = R.take(PAIRS, TP)
        BON = R.take(PAIRS, TQ)
        ZG = R.take(2, SEQ)
        AFTER = R.at

        hT = R.take(KD, TQ)
        wbuf = [R.take(KD, P) for _ in range(2)]
        rst = R.take(TQ // 2 + 1)
        reset = rst.bitcast(BF16)[:, 0:TQ]
        UB = R.take(2, TQ)
        Z0 = R.take(TQ)
        TM = [R.take(TQ) for _ in range(6)]
        SG, CS, E1, AA, KK, T7 = TM
        ZG0, XC, GR, GI, GS, LD = TM

        RA = Region(AFTER + KD * TQ + 2 * KD * P + TQ // 2 + 1)
        xb = [RA.take(D) for _ in range(2)]
        xh = [RA.take(D) for _ in range(2)]

        GG = BT
        wrg = VT[:, 0, 0:512].rearrange("p (j c) -> p j c", c=P)
        wig = VT[:, 0, 512:1024].rearrange("p (j c) -> p j c", c=P)
        LA = VT[:, 1, 0:TQ]
        YL = VT[:, 2, 0:SEQ]
        YZ = KT[:, 0, 0:D]
        XL = VT[:, 3, 0:1044]

        (meta_d, x_d) = (a["meta"], a["x"])
        h_dram, ylru_dram, h1_dram, tok_dram, y_dram = (
            scratch[n] for n in ("h", "ylru", "h1", "tok", "y"))

        s_const = sem("s_const")
        s_prm = sem("s_prm")
        s_gate_w = sem("s_gate_w")
        s_const_done = sem("s_const_done")
        s_lnp = sem("s_lnp")
        s_xin = [sem(f"s_xin{i}") for i in range(2)]
        s_ln = Steps(sem("s_ln"), ["st0", "st1", "agg", "rstd", "xhat"])
        s_std = sem("s_std")
        s_h = Steps(sem("s_h"), ["gain", "bias"])
        s_tp = sem("s_tp")
        s_ht = sem("s_ht")
        s_hst = [sem(f"s_hst{i}") for i in range(2)]
        s_yz, s_yzd = sem("s_yz"), sem("s_yzd")
        s_zcol = sem("s_zcol")
        s_setup = sem("s_setup")
        s_hp, s_absl, s_expl, s_c8 = sem("s_hp"), sem("s_absl"), sem("s_expl"), sem("s_c8")

        def cols(kind, j):
            base = {"r": 0, "k": 512, "v": 1024, "lx": N_RWKV, "gl": N_RWKV + 512}
            if kind == "z":
                return (1536 + P * j, P if j < 2 else 32)
            return base[kind] + P * j, P

        JOBS = ([("gl", j) for j in range(4)]
                + [("lx", 0), ("lx", 1), ("gr", 0), ("gi", 0), ("lx", 2), ("gr", 1), ("gi", 1), ("lx", 3),
                   ("gr", 2), ("gi", 2), ("z", 0), ("z", 1), ("gr", 3), ("gi", 3), ("z", 2)]
                + [("r", 0), ("k", 0), ("v", 0)])
        for p in range(PAIRS):
            nxt = [("r", p + 1), ("k", p + 1), ("v", p + 1)] if p + 1 < PAIRS else []
            JOBS += [("dec", p), ("aa", p)] + nxt[0:1] + [("ss", p)] + nxt[1:2] + [("bon", p)] + nxt[2:]
        J = {j: n for n, j in enumerate(JOBS)}
        WTILES = [j for j in JOBS if j[0] in ("gl", "lx", "z", "r", "k", "v")]
        s_w = [sem(f"s_w{i}") for i in range(2)]
        s_job = sem("s_job")
        SHIFTED = [j for j in JOBS if j[0] in ("z", "r", "k", "v")]

        def bank(job, rows=P):
            s = J[job] % 2
            return ps[0:rows, 3 * s:3 * s + 3, 0:SEG]

        def seg3(v):
            return v.rearrange("p (s c) -> p s c", c=SEG)

        s_gelu = sem("s_gelu")
        s_uev = sem("s_uev")
        s_udif = sem("s_udif")
        s_ush = sem("s_ush")
        s_zact = sem("s_zact")
        s_zg = sem("s_zg")
        LRU_D = Steps(sem("s_lrud"), ["c0", "c1", "c2", "c3", "gr", "d1", "rec", "m2", "gi", "ga", "gb", "scan", "y"])
        s_lx = sem("s_lx")
        LRU_A = Steps(sem("s_lrua"), ["gr", "gi", "la", "gs", "sq"])
        s_yst = sem("s_yst")
        PR_D = Steps(sem("s_prd"), ["sg", "cs", "csx", "a", "kk", "ssm", "rec", "kkn", "kc", "k2", "q", "bon",
                                    "b0", "b", "k", "r", "at"])
        PR_A = Steps(sem("s_pra"), ["sg", "a", "sq", "iw", "rt", "w63", "wx", "w"])
        s_z0 = sem("s_z0")

        RC = Region(AFTER)
        slot = []
        for s in range(2):
            d = {}
            for n in ("Ab", "Bb", "Kb", "Vb", "Mb", "Nb", "Db", "Pb", "Btb", "Ktb", "Vtb"):
                d[n] = RC.take(PAIRS, 2, HEAD)
            for n in ("Mr", "Mk", "Ds", "Ps", "Vs", "Zs", "Qs"):
                d[n] = RC.take(PAIRS, HEAD)
            d["AN"] = RC.take(PAIRS, 2, HEAD)
            d["Xb"], d["Zb"], d["Gb"] = d["Ab"], d["Bb"], d["Kb"]
            slot.append(d)
        SS = [RC.take(PAIRS, HEAD) for _ in range(2)]
        SB = [RC.take(PAIRS, 2, HEAD) for _ in range(2)]

        LV = range(5)
        CP = [Steps(sem(f"s_cp{s}"), ["A", "B", "K", "V", "P0", "P1", "P2", "P3", "P4", "Z", "S"]) for s in range(2)]
        CE_NAMES = (["MA", "MB", "VT", "MK", "NV", "P0", "BT", "DP0", "PD0", "P1", "KT", "DP1", "PD1", "P2", "VV", "DP2", "PD2",
                     "P3", "DP3", "PD3", "P4", "PD4", "XZ", "GT", "Q", "S", "Y"])
        CE = [Steps(sem(f"s_ce{s}"), CE_NAMES) for s in range(2)]
        CD = [Steps(sem(f"s_cd{s}"),
                    ["D0a", "D0", "Mb", "T0a", "T0", "Nb", "Mr", "Mk", "P0", "D1", "T1", "P1", "D2", "T2", "P2", "D3", "T3",
                     "P3", "D4", "T4", "P4", "T5", "X", "G", "Q", "S"]) for s in range(2)]
        CA = [Steps(sem(f"s_ca{s}"), ["At", "Vs", "NV", "Bt", "Kt", "Vv", "Z", "Y"]) for s in range(2)]

        RE = Region(AFTER)
        yl = RE.take(4, SEQ)
        wo = RE.take(KD, D)
        gsq = [RE.take(512) for _ in range(2)]
        gsd = [RE.take(512) for _ in range(2)]
        wgu = RE.take(2, 512)
        GN_D = Steps(sem("s_gnd"), ["c", "rec", "n", "aff", "bon", "g"])
        GN_A = Steps(sem("s_gna"), ["sq", "sd"])
        GN_E = Steps(sem("s_gne"), ["mean", "g", "var"])
        s_wo, s_yl, s_wgu = sem("s_wo"), sem("s_yl"), sem("s_wgu")

        RF = Region(BASE + PAIRS * 2 * TP)
        hb = [RF.take(D) for _ in range(2)]
        zb = [RF.take(D) for _ in range(2)]
        h1 = [RF.take(D) for _ in range(2)]
        h1T = [RF.take(KD, P) for _ in range(2)]
        wr = RF.take(KD, NG + NE)
        br = RF.take(NG + NE)
        lg = RF.take(NT, NG + NE)
        F_D = Steps(sem("s_fd"), ["res0", "res1", "st0", "st1", "agg", "rstd", "xhat"])
        F_L = sem("s_fl")
        F_P = Steps(sem("s_fp"), ["gain", "bias"])
        F_A = sem("s_fa")
        F_C = Steps(sem("s_fc"), ["t0", "t1"])
        F_O = Steps(sem("s_fo"), ["o0", "o1"])
        F_E = Steps(sem("s_fe"), ["t0", "t1", "lg"])
        s_hin = [sem(f"s_hin{i}") for i in range(2)]
        s_h1st = [sem(f"s_h1st{i}") for i in range(2)]
        s_wr, s_ln1 = sem("s_wr"), sem("s_ln1")

        g8 = RF.take(8)
        i4 = RF.take(NE)
        e8 = RF.take(EPG)
        gm8, gi8f = RF.take(8), RF.take(8)
        gi8 = RF.take(8).bitcast(U32)
        ti8 = RF.take(8).bitcast(U32)
        ti8f = RF.take(8)
        ohg = RF.take(NG)
        esel = RF.take(NG, EPG)
        tm8 = RF.take(8)
        sm = RF.take(16)
        OH = [RF.take(NT, NE) for _ in range(2)]
        OS = RF.take(NT, NE)
        OP = RF.take(NT + 1, NE)
        RK = RF.take(NT, NE)
        t32 = RF.take(NT, NE)
        eidf = RF.take(2, NT)
        rk = RF.take(2, NT)
        ovs = RF.take(2, NT)
        qk = RF.take(2, NT)
        q7 = RF.take(2 * NT, 7)
        th7 = RF.take(7)
        cnt = RF.take(NE)
        c7 = RF.take(NE, 7)
        ovb, ovi, ove = RF.take(NE), RF.take(NE), RF.take(NE)
        j16 = RF.take(OVER)
        o16 = RF.take(OVER, NE)
        oef = RF.take(OVER)
        s1t = RF.take(2, NT)
        ztab = RF.take(NBLK * CAP // P)
        KEEP = 49500
        RK2 = Region(KEEP)
        gates = RK2.take(2, NT)
        slots = RK2.take(2, NT).bitcast(I32)
        oei = RK2.take(OVER).bitcast(I32)
        novi = RK2.take(1).bitcast(I32)
        tokid = RK2.take(NT).bitcast(I32)
        idx = RK2.take(NBLK).bitcast(I32)
        s_rt = sem("s_rt")
        s_rt_arg, s_rt_oh, s_rt_done = sem("s_rt_arg"), sem("s_rt_oh"), sem("s_rt_done")
        s_rta = sem("s_rta")
        s_rte = sem("s_rte")
        s_rtc = sem("s_rtc")
        s_zt, s_sc, s_idx = sem("s_zt"), sem("s_sc"), sem("s_idx")

        RM = Region(BASE)
        we = []
        for s in range(2):
            we.append((RM.take(KD, FE), RM.take(KD, FE), RM.take(KF, D)))
        xg = [RM.take(D) for _ in range(2)]
        xT = [RM.take(KD, P) for _ in range(2)]
        hs = [RM.take(FE) for _ in range(2)]
        hd = [RM.take(FE) for _ in range(2)]
        hTe = [RM.take(KF, P) for _ in range(2)]
        yb = [RM.take(D) for _ in range(2)]
        assert RM.at <= KEEP
        s_wg = [[sem(f"s_we{k}{i}") for i in range(2)] for k in range(3)]
        s_xg = [sem(f"s_xg{i}") for i in range(2)]
        M_X, M_XA, M_XD = sem("s_mx"), sem("s_mxa"), sem("s_mxd")
        M_E = Steps(sem("s_me"), ["g", "u", "h", "y"])
        M_A = Steps(sem("s_ma"), ["silu", "h", "y"])
        M_D = Steps(sem("s_md"), ["hid", "y"])
        s_yo = [sem(f"s_yo{i}") for i in range(2)]

        RO = Region(BASE)
        y1 = [RO.take(D) for _ in range(2)]
        y2 = [RO.take(D) for _ in range(2)]
        hr = [RO.take(D) for _ in range(2)]
        o_x = [RO.take(D) for _ in range(2)]
        s_y1 = [sem(f"s_y1{i}") for i in range(2)]
        s_y2 = [sem(f"s_y2{i}") for i in range(2)]
        s_hr = [sem(f"s_hr{i}") for i in range(2)]
        s_ln2 = sem("s_ln2")
        O_D = Steps(sem("s_od"), ["y1", "y2", "res", "st0", "st1", "agg", "rstd", "xhat"])
        O_A = sem("s_oa")
        O_P = Steps(sem("s_op"), ["gain", "bias"])
        s_out = [sem(f"s_out{i}") for i in range(2)]

        block = ctx.enter_context(nc.Block())

        def rows(ti):
            return META if ti == 0 else P

        def first(n):
            return isinstance(n, int) and n == 0

        def shifted(kind, j):
            if kind == "r":
                return AR[:, j, 1, PAD:TP]
            if kind == "k":
                return KT[:, j, PAD:TP]
            if kind == "v":
                return VT[:, j, PAD:TP]
            return (Z0[:, 1:TQ], TM[0][:, 1:TQ], TM[1][0:32, 1:TQ])[j]

        def finish(pl, g, ti):
            b = ti % 2
            pl.wait_ge(O_D.sem, O_D.at(ti, "xhat"))
            g.tensor_tensor(o_x[b], o_x[b], lng, ALU.mult).then_inc(O_P.sem, 1)
            pl.wait_ge(O_P.sem, O_P.at(ti, "gain"))
            g.tensor_tensor(o_x[b], o_x[b], lnb, ALU.add).then_inc(O_P.sem, 1)

        @block.sync
        def _(sp):
            sp.dma_start(lng, a["ln0_g"].rearrange("(o n) -> o n", o=1).to_broadcast([P, D])).then_inc(s_lnp, 16)
            sp.dma_start(lnb, a["ln0_b"].rearrange("(o n) -> o n", o=1).to_broadcast([P, D])).then_inc(s_lnp, 16)
            for ti in range(NT + 1):
                b = ti % 2
                if ti >= 2:
                    sp.wait_ge(s_ln.sem, s_ln.at(ti - 2, "xhat"))
                src = meta_d if ti == 0 else x_d[0, (ti - 1) * P:ti * P, :]
                sp.dma_start(xb[b][0:rows(ti), :], src).then_inc(s_xin[b], 16)
                if ti == 1:
                    for n, j in enumerate(WTILES[0:2]):
                        c0, w = cols(*j)
                        sp.dma_start(wbuf[n][:, :, 0:w],
                                     a["w_in"][0, :, c0:c0 + w].rearrange("(k p) c -> p k c", p=P)).then_inc(s_w[n], 16)
            for n, j in enumerate(WTILES[2:], 2):
                sp.wait_ge(s_job, J[WTILES[n - 2]] + 1)
                c0, w = cols(*j)
                sp.dma_start(wbuf[n % 2][:, :, 0:w],
                             a["w_in"][0, :, c0:c0 + w].rearrange("(k p) c -> p k c", p=P)).then_inc(s_w[n % 2], 16)
            for s in range(2):
                last = (NCH - 1 - s) // 2
                sp.wait_ge(CE[s].sem, CE[s].at(last, "Y"))
                sp.wait_ge(CD[s].sem, CD[s].at(last, "S"))
                sp.wait_ge(CA[s].sem, CA[s].at(last, "Y"))
                sp.wait_ge(CP[s].sem, CP[s].at(last, "S"))
            sp.wait_ge(s_yst, 16 * 4)
            sp.dma_start(wgu[:, 0, :], a["w_g_up"][0, 0:P, :]).then_inc(s_wgu, 16)
            sp.dma_start(wgu[0:32, 1, :], a["w_g_up"][0, P:GATE, :]).then_inc(s_wgu, 16)
            sp.dma_start(yl, ylru_dram.rearrange("(j p) t -> p j t", p=P)).then_inc(s_yl, 16)
            sp.dma_start(wo, a["w_out"][0].rearrange("(k p) n -> p k n", p=P)).then_inc(s_wo, 16)
            sp.wait_ge(GN_D.sem, GN_D.at(2 * PAIRS - 1, "g"))
            sp.dma_start(wr[:, :, 0:NG], a["w_router_grp"][0].rearrange("(k p) n -> p k n", p=P)).then_inc(s_wr, 16)
            sp.dma_start(wr[:, :, NG:NG + NE], a["w_router_exp"][0].rearrange("(k p) n -> p k n", p=P)).then_inc(s_wr, 16)
            sp.dma_start(br[:, 0:NG], a["b_router_grp"].to_broadcast([P, NG])).then_inc(s_wr, 16)
            sp.dma_start(br[:, NG:NG + NE], a["b_router_exp"].to_broadcast([P, NE])).then_inc(s_wr, 16)
            for b in range(2):
                sp.wait_ge(s_hst[b], 16 * 4)
            for ti in range(NT):
                b = ti % 2
                if ti >= 2:
                    sp.wait_ge(F_D.sem, F_D.at(ti - 2, "res1"))
                sp.dma_start(hb[b], h_dram[ti * P:(ti + 1) * P, :]).then_inc(s_hin[b], 16)
            sp.wait_ge(F_L, NT)
            sp.wait_ge(s_rt_done, 1)
            sp.wait_ge(s_sc, 16 * 2 * NT)
            for b in range(2):
                sp.wait_ge(s_h1st[b], 16 * 4)

            def weights(s, e, first, turn):
                wg, wu, wd = we[s]
                if not first:
                    sp.wait_ge(M_E.sem, M_E.at(turn, "u"))
                dyn = bass.ds(e, 1)
                sp.dma_start(wg, a["w_exp_gate"][0, dyn].rearrange("o (p k) n -> p (o k) n", k=KD)).then_inc(s_wg[0][s], 16)
                sp.dma_start(wu, a["w_exp_up"][0, dyn].rearrange("o (p k) n -> p (o k) n", k=KD)).then_inc(s_wg[1][s], 16)
                if not first:
                    sp.wait_ge(M_E.sem, M_E.at(turn, "y"))
                sp.dma_start(wd, a["w_exp_down"][0, dyn].rearrange("o (p k) n -> p (o k) n", k=KF)).then_inc(s_wg[2][s], 16)

            def store(s, n, row):
                sp.wait_ge(M_D.sem, M_D.at(n, "y"))
                sp.wait_ge(M_A.sem, M_A.at(n, "y"))
                sp.dma_start(y_dram[bass.ds(row, P), :], yb[s]).then_inc(s_yo[s], 16)

            for s in range(2):
                weights(s, s, True, 0)
            with sp.Fori(0, NE // 2 - 1) as i:
                for s in range(2):
                    weights(s, i * 2 + (2 + s), False, i * 2 + s)
                    store(s, i * 2 + s, i * (2 * P) + s * P)
            for s in range(2):
                store(s, NE - 2 + s, (NE - 2 + s) * P)
            n_over = sp.value_load(novi[0:1, 0:1], min_val=0, max_val=OVER)
            for j in range(OVER):
                with sp.If(n_over > j):
                    e = sp.value_load(oei[0:1, j:j + 1], min_val=0, max_val=NE - 1)
                    weights(j % 2, e, False, NE + j - 2)
                    store(j % 2, NE + j, (NE + j) * P)
            for s in range(2):
                sp.wait_ge(s_yo[s], 16 * (NE // 2))
            for ti in range(NT):
                b = ti % 2
                if ti >= 2:
                    sp.wait_ge(O_D.sem, O_D.at(ti - 2, "xhat"))
                sp.dma_start(hr[b], h1_dram[ti * P:(ti + 1) * P, :]).then_inc(s_hr[b], 16)
                if ti >= 1:
                    sp.wait_ge(O_P.sem, O_P.at(ti - 1, "bias"))
                    sp.dma_start(out[0, (ti - 1) * P:ti * P, :], o_x[1 - b]).then_inc(s_out[1 - b], 16)
            sp.wait_ge(O_P.sem, O_P.at(NT - 1, "bias"))
            sp.dma_start(out[0, (NT - 1) * P:NT * P, :], o_x[(NT - 1) % 2]).then_inc(s_out[(NT - 1) % 2], 16)
            for b in range(2):
                sp.wait_ge(s_out[b], 16 * (NT // 2))

        @block.gpsimd
        def _(pl):
            g = nc.gpsimd
            count = [0]

            def const(ins):
                count[0] += 1
                ins.then_inc(s_const, 1)
                pl.wait_ge(s_const, count[0])

            names = ["w0", "a0", "k_k", "k_a", None, "gn_g", "gn_b", "conv_b", "b_rg", "b_ig", "lru_lambda"]
            with nc.allow_non_contiguous_dma(reason="parameters to columns"):
                for n, name in enumerate(names):
                    src = a["r_k"].rearrange("o h n -> o (h n)") if name is None else a[name]
                    pl.dma_start(prm[:, n, :], src[0].rearrange("(j p) -> p j", p=P)).then_inc(s_prm, 16)
                pl.dma_start(cw, a["conv_w"][0].rearrange("w (j p) -> p w j", p=P)).then_inc(s_prm, 16)
                pl.dma_start(mu[:, 0:14], a["mu_shift"][0, 0:14 * P].rearrange("(j p) -> p j", p=P)).then_inc(s_prm, 16)
                pl.dma_start(mu[0:32, 14:15], a["mu_shift"][0, 14 * P:N_RWKV].rearrange("(p j) -> p j", j=1)).then_inc(s_prm, 16)
            pl.dma_start(wlr[0:64, :], a["w_decay_up"][0]).then_inc(s_prm, 16)
            pl.dma_start(wlr[64:128, :], a["w_a_up"][0]).then_inc(s_prm, 16)
            const(g.memset(ident, 0.0))
            const(g.affine_select(out=ident, in_=ident, compare_op=ALU.not_equal, fill=1.0, base=0,
                                  pattern=[[-1, P]], channel_multiplier=1))
            const(g.memset(eps[:, 0:1], LN_EPS))
            const(g.memset(eps[:, 1:2], GN_EPS))
            const(g.memset(VT[:, 0, 0:1024], 0.0))
            for dst, name in ((wrg, "w_rg"), (wig, "w_ig")):
                for h in range(2):
                    pl.dma_start(dst[h * HEAD:(h + 1) * HEAD, :, h * HEAD:(h + 1) * HEAD],
                                 a[name][0].rearrange("(j h) i c -> h i j c", h=2)[h]).then_inc(s_gate_w, 16)

            def masks():
                const(g.memset(ones, 1.0))
                const(g.affine_select(out=ltri, in_=ones, compare_op=ALU.is_gt, fill=0.0, base=0,
                                      pattern=[[1, P]], channel_multiplier=-1))
                const(g.memset(XL[:, 0:3], 0.0))
                const(g.memset(reset, 1.0))
                const(g.memset(reset[:, CH - Q0:CH - Q0 + CH * (NCH - 2) + 1:CH], 0.0))
                for m in (blk, m_strict, m_supT, ident2, m_sub):
                    const(g.memset(m, 0.0))
                for h in range(2):
                    rws = slice(h * HEAD, (h + 1) * HEAD)
                    const(g.memset(blk[rws, h, :], 1.0))
                    const(g.affine_select(out=m_incl[rws, :], in_=ones[rws, 0:HEAD], compare_op=ALU.is_ge, fill=0.0,
                                          base=0, pattern=[[1, HEAD]], channel_multiplier=-1))
                    const(g.affine_select(out=m_strict[rws, h, :], in_=ones[rws, 0:HEAD], compare_op=ALU.is_gt, fill=0.0,
                                          base=0, pattern=[[1, HEAD]], channel_multiplier=-1))
                    const(g.affine_select(out=ident2[rws, :], in_=ident2[rws, :], compare_op=ALU.not_equal, fill=1.0,
                                          base=0, pattern=[[-1, HEAD]], channel_multiplier=1))
                    odd = m_supT[rws, h, :].rearrange("p (a b) -> p a b", b=2)[:, :, 1]
                    const(g.affine_select(out=odd, in_=odd, compare_op=ALU.not_equal, fill=1.0,
                                          base=0, pattern=[[-2, HEAD // 2]], channel_multiplier=1))
                for l in range(6):
                    w = 1 << l
                    n = HEAD // (2 * w)
                    for h in range(2):
                        rws = slice(h * HEAD, (h + 1) * HEAD)
                        even = m_sub[rws, l, :].rearrange("p (a b c) -> p a b c", b=2, c=w)[:, :, 0, :]
                        const(g.memset(even, 1.0))
                        const(g.affine_select(out=even, in_=even, compare_op=ALU.is_ge, fill=0.0, base=-w,
                                              pattern=[[-2 * w, n], [0, w]], channel_multiplier=1))
                        const(g.affine_select(out=even, in_=even, compare_op=ALU.is_ge, fill=0.0, base=2 * w - 1,
                                              pattern=[[2 * w, n], [0, w]], channel_multiplier=-1))
                g.memset(lamt[:, 4, :], 1.0 / 19).then_inc(s_const_done, 1)

            pl.wait_ge(s_lnp, 32)
            for ti in range(NT + 1):
                b, r = ti % 2, rows(ti)
                pl.wait_ge(s_ln.sem, s_ln.at(ti, "xhat"))
                g.tensor_tensor(xh[b][0:r, :], xh[b][0:r, :], lng[0:r, :], ALU.mult).then_inc(s_h.sem, 1)
                pl.wait_ge(s_h.sem, s_h.at(ti, "gain"))
                g.tensor_tensor(xh[b][0:r, :], xh[b][0:r, :], lnb[0:r, :], ALU.add).then_inc(s_h.sem, 1)
                if ti:
                    pl.wait_ge(s_h.sem, s_h.at(ti, "bias"))
                    pl.dma_start(h_dram[(ti - 1) * P:ti * P, :], xh[b]).then_inc(s_hst[b], 16)
            masks()
            pl.wait_ge(s_h.sem, s_h.at(NT, "bias"))
            pl.dma_start(lng, a["ln1_g"].to_broadcast([P, D])).then_inc(s_ln1, 16)
            pl.dma_start(lnb, a["ln1_b"].to_broadcast([P, D])).then_inc(s_ln1, 16)

            def lru_store(j):
                pl.wait_ge(LRU_D.sem, LRU_D.at(j, "y"))
                pl.dma_start(ylru_dram[j * P:(j + 1) * P, :], YL).then_inc(s_yst, 16)

            g.memset(YZ, 0.0).then_inc(s_yz, 1)
            pl.wait_ge(s_yz, 1)
            pl.dma_start(y_dram[NE * P:NBLK * P, :].rearrange("(b p) n -> p b n", p=P),
                         YZ.rearrange("p (o n) -> p o n", o=1).to_broadcast([P, OVER, D])).then_inc(s_yzd, 16)
            for j in range(3):
                lru_store(j)
            for n, (kind, j) in enumerate(SHIFTED):
                pl.wait_ge(s_uev, n + 1)
                r = cols(kind, j)[1]
                if (kind, j) == ("z", 2):
                    lru_store(3)
                if (kind, j) == ("r", 0):
                    pl.wait_ge(s_yst, 16 * 4)
                    pl.wait_ge(s_yzd, 16)
                    for arr in (AR[:, :, 0, 0:PAD], AR[:, :, 1, 0:PAD], BT[:, :, 0:PAD], KT[:, :, 0:PAD], VT[:, :, 0:PAD]):
                        g.memset(arr, 0.0).then_inc(s_z0, 1)
                dst = shifted(kind, j)
                g.tensor_tensor(dst, UB[0:r, n % 2, 0:TQ - 1], UB[0:r, n % 2, 1:TQ], ALU.subtract).then_inc(s_udif, 1)

            def blocks(dst, src):
                return g.tensor_tensor(dst, src.rearrange("p a (o c) -> p a o c", o=1).to_broadcast([P, PAIRS, 2, HEAD]),
                                       blk.rearrange("p (o h) c -> p o h c", o=1).to_broadcast([P, PAIRS, 2, HEAD]), ALU.mult)

            def prep(s, n, c):
                d = slot[s]
                if not first(n):
                    pl.wait_ge(CE[s].sem, CE[s].at(n - 1, "Y"))
                for name, src in (("A", AR[:, :, 0, :]), ("B", BT), ("K", KT), ("V", VT)):
                    blocks(d[name + "b"], src[:, :, bass.ds(c * CH, CH)]).then_inc(CP[s].sem, 1)

            def level(s, n, l):
                d = slot[s]
                pl.wait_ge(CD[s].sem, CD[s].at(n, f"P{l}"))
                if l:
                    pl.wait_ge(CE[s].sem, CE[s].at(n, f"PD{l - 1}"))
                blocks(d["Pb"], d["Ps"]).then_inc(CP[s].sem, 1)

            def tail_z(s, n):
                d = slot[s]
                pl.wait_ge(CA[s].sem, CA[s].at(n, "Z"))
                pl.wait_ge(CE[s].sem, CE[s].at(n, "BT"))
                blocks(d["Zb"], d["Zs"]).then_inc(CP[s].sem, 1)

            def tail_s(s, n):
                pl.wait_ge(CD[s].sem, CD[s].at(n, "S"))
                if s == 0:
                    if not first(n):
                        pl.wait_ge(CE[1].sem, CE[1].at(n - 1, "Y"))
                else:
                    pl.wait_ge(CE[0].sem, CE[0].at(n, "Y"))
                blocks(SB[1 - s], SS[1 - s]).then_inc(CP[s].sem, 1)

            pl.wait_ge(PR_D.sem, PR_D.at(PAIRS - 1, "at"))
            g.memset(SS[0], 0.0).then_inc(s_z0, 1)
            g.memset(SB[0], 0.0).then_inc(s_z0, 1)
            pl.wait_ge(s_z0, 7)

            def turn(slots_, n, c):
                for k, s in enumerate(slots_):
                    prep(s, n, c + k)
                for l in LV:
                    for s in slots_:
                        level(s, n, l)
                for s in slots_:
                    tail_z(s, n)
                for s in slots_:
                    tail_s(s, n)

            turn((0, 1), 0, 0)
            with pl.Fori(1, (NCH - 1) // 2) as i:
                turn((0, 1), i, i * 2)
            turn((0,), (NCH - 1) // 2, NCH - 1)

            pl.wait_ge(s_ln1, 32)
            for ti in range(NT):
                b = ti % 2
                pl.wait_ge(F_D.sem, F_D.at(ti, "xhat"))
                g.tensor_tensor(h1[b], h1[b], lng, ALU.mult).then_inc(F_P.sem, 1)
                pl.wait_ge(F_P.sem, F_P.at(ti, "gain"))
                g.tensor_tensor(h1[b], h1[b], lnb, ALU.add).then_inc(F_P.sem, 1)
                pl.wait_ge(F_P.sem, F_P.at(ti, "bias"))
                pl.dma_start(h1_dram[ti * P:(ti + 1) * P, :], h1[b]).then_inc(s_h1st[b], 16)
            g.iota(i4, pattern=[[1, NE]], base=0, channel_multiplier=0, allow_small_or_imprecise_dtypes=True).then_inc(s_rtc, 1)
            g.iota(th7, pattern=[[P, 7]], base=P, channel_multiplier=0, allow_small_or_imprecise_dtypes=True).then_inc(s_rtc, 1)
            g.iota(j16, pattern=[[1, OVER]], base=0, channel_multiplier=0, allow_small_or_imprecise_dtypes=True).then_inc(s_rtc, 1)
            g.iota(tokid, pattern=[[P, NT]], base=0, channel_multiplier=1).then_inc(s_rtc, 1)
            g.memset(ztab, 0.0).then_inc(s_rtc, 1)
            pl.wait_ge(s_rtc, 5)
            pl.dma_start(tok_dram.rearrange("(p b) o -> p (b o)", p=P), ztab.bitcast(I32)).then_inc(s_zt, 16)
            pl.wait_ge(s_zt, 16)
            pl.wait_ge(s_rt_done, 1)
            pl.dma_start(lng, a["ln2_g"].to_broadcast([P, D])).then_inc(s_ln2, 16)
            pl.dma_start(lnb, a["ln2_b"].to_broadcast([P, D])).then_inc(s_ln2, 16)
            for k in range(2):
                for ti in range(NT):
                    g.indirect_dma_start(out=tok_dram, out_offset=bass.IndirectOffsetOnAxis(ap=slots[:, k, ti:ti + 1], axis=0),
                                         in_=tokid[:, ti:ti + 1], in_offset=None).then_inc(s_sc, 16)
            pl.wait_ge(s_sc, 16 * 2 * NT)
            with nc.allow_non_contiguous_dma(reason="slot table to columns"):
                pl.dma_start(idx, tok_dram.rearrange("(b p) o -> p (b o)", p=P)).then_inc(s_idx, 16)
            pl.wait_ge(s_idx, 16)
            for b in range(2):
                pl.wait_ge(s_h1st[b], 16 * 4)

            def gather(s, n):
                if n >= 2:
                    pl.wait_ge(M_X, n - 1)
                g.indirect_dma_start(out=xg[s], out_offset=None, in_=h1_dram,
                                     in_offset=bass.IndirectOffsetOnAxis(ap=idx[:, n:n + 1], axis=0)).then_inc(s_xg[s], 16)

            for n in range(NE):
                gather(n % 2, n)
            n_over = pl.value_load(novi[0:1, 0:1], min_val=0, max_val=OVER)
            for j in range(OVER):
                with pl.If(n_over > j):
                    gather(j % 2, NE + j)
            for s in range(2):
                pl.wait_ge(s_yo[s], 16 * (NE // 2))
            for j in range(OVER):
                with pl.If(n_over > j):
                    pl.wait_ge(s_yo[j % 2], 16 * (NE // 2 + j // 2 + 1))
            pl.wait_ge(s_ln2, 32)
            for ti in range(NT):
                b = ti % 2
                if ti >= 2:
                    pl.wait_ge(O_D.sem, O_D.at(ti - 2, "y2"))
                g.indirect_dma_start(out=y1[b], out_offset=None, in_=y_dram,
                                     in_offset=bass.IndirectOffsetOnAxis(ap=slots[:, 0, ti:ti + 1], axis=0)).then_inc(s_y1[b], 16)
                g.indirect_dma_start(out=y2[b], out_offset=None, in_=y_dram,
                                     in_offset=bass.IndirectOffsetOnAxis(ap=slots[:, 1, ti:ti + 1], axis=0)).then_inc(s_y2[b], 16)
                if ti >= 1:
                    finish(pl, g, ti - 1)
            finish(pl, g, NT - 1)

        @block.vector
        def _(dv):
            v = nc.vector

            def own(st, n, name, ins):
                ins.then_inc(st.sem, 1)
                dv.wait_ge(st.sem, st.at(n, name))

            v.memset(hT[:, :, 0:1], 0.0).then_inc(s_zcol, 1)
            setup = [0]

            def once(ins):
                setup[0] += 1
                ins.then_inc(s_setup, 1)
                dv.wait_ge(s_setup, setup[0])

            for ti in range(NT + 1):
                b, r = ti % 2, rows(ti)
                dv.wait_ge(s_xin[b], 16 * (ti // 2 + 1))
                for hf in range(2):
                    own(s_ln, ti, f"st{hf}", v.bn_stats(out=st6[0:r, hf, :], in_=xb[b][0:r, hf * 512:(hf + 1) * 512]))
                v.bn_aggr(out=mv[0:r, :], in_=st6[0:r, :, :].rearrange("p a b -> p (a b)")).then_inc(s_ln.sem, 1)
                dv.wait_ge(s_std, ti + 1)
                own(s_ln, ti, "rstd", v.reciprocal(rstd[0:r, 1:2], rstd[0:r, 0:1]))
                if ti >= 2:
                    dv.wait_ge(s_tp, 2 * (ti - 1))
                    if ti >= 3:
                        dv.wait_ge(s_hst[b], 16 * ((ti - 1) // 2))
                own(s_ln, ti, "xhat", v.tensor_scalar(xh[b][0:r, :], xb[b][0:r, :], mv[0:r, 0:1], rstd[0:r, 1:2],
                                                      ALU.subtract, ALU.mult))

            dv.wait_ge(s_tp, 2 * (NT + 1))
            for b in range(2):
                dv.wait_ge(s_hst[b], 16 * (NT // 2))
            v.memset(Z0[:, 0:1], 0.0).then_inc(s_zcol, 1)
            dv.wait_ge(s_prm, 16 * 15)
            dv.wait_ge(s_const_done, 1)
            for q, n in enumerate((P_W0, P_A0, P_BR, P_BI)):
                once(v.tensor_scalar(hprm[:, q, :], prm[:, n, :], 0.5, None, ALU.mult))
            once(v.tensor_scalar(prm[:, P_K1, :], prm[:, P_KA, :], -1.0, 1.0, ALU.mult, ALU.add))
            once(v.tensor_scalar(lamt[:, 0, :], prm[:, P_LAM, :], -1.0, None, ALU.mult))
            once(v.tensor_tensor(lamt[:, 0, :], lamt[:, 0, :], prm[:, P_LAM, :], ALU.min))
            v.tensor_scalar(lamt[:, 5, :], prm[:, P_LAM, :], 0.0, None, ALU.min).then_inc(s_absl, 1)
            dv.wait_ge(s_absl, 1)
            dv.wait_ge(s_expl, 1)
            once(v.tensor_scalar(lamt[:, 2, :], lamt[:, 1, :], 2.0, None, ALU.add))
            once(v.reciprocal(lamt[:, 3, :], lamt[:, 2, :]))
            once(v.tensor_tensor(lamt[:, 2, :], lamt[:, 1, :], lamt[:, 3, :], ALU.mult))
            once(v.tensor_tensor(lamt[:, 3, :], lamt[:, 2, :], lamt[:, 2, :], ALU.mult))
            for q in range(8, -1, -1):
                once(v.tensor_tensor(lamt[:, 4, :], lamt[:, 4, :], lamt[:, 3, :], ALU.mult))
                once(v.tensor_scalar(lamt[:, 4, :], lamt[:, 4, :], 1.0 / (2 * q + 1), None, ALU.add))
            once(v.tensor_tensor(lamt[:, 4, :], lamt[:, 4, :], lamt[:, 2, :], ALU.mult))
            once(v.tensor_scalar(lamt[:, 4, :], lamt[:, 4, :], -2.0, None, ALU.mult))
            once(v.tensor_tensor(lamt[:, 4, :], lamt[:, 4, :], lamt[:, 5, :], ALU.add))
            once(v.tensor_scalar(c8[:, 0, :], lamt[:, 4, :], 8.0, None, ALU.mult))
            v.tensor_scalar(c8[:, 1, :], lamt[:, 4, :], -8.0, None, ALU.mult).then_inc(s_c8, 1)

            def conv(j):
                dv.wait_ge(s_lx, j + 1)
                own(LRU_D, j, "c0", v.tensor_scalar(XC, XL[:, 0:TQ], cw[:, 0, j:j + 1], prm[:, P_CB, j:j + 1], ALU.mult, ALU.add))
                for w in range(1, 4):
                    own(LRU_D, j, f"c{w}", v.scalar_tensor_tensor(out=XC, in0=XL[:, w:w + TQ], scalar=cw[:, w, j:j + 1], in1=XC,
                                                                  op0=ALU.mult, op1=ALU.add))

            def lru(j):
                dv.wait_ge(LRU_A.sem, LRU_A.at(j, "gr"))
                own(LRU_D, j, "gr", v.tensor_scalar(GR, GR, 0.5, 0.5, ALU.mult, ALU.add))
                dv.wait_ge(LRU_A.sem, LRU_A.at(j, "gs"))
                own(LRU_D, j, "d1", v.tensor_scalar(LD, GS, 1.0, None, ALU.add))
                own(LRU_D, j, "rec", v.reciprocal(LD, LD))
                own(LRU_D, j, "m2", v.scalar_tensor_tensor(out=GS, in0=GS, scalar=2.0, in1=LD, op0=ALU.mult, op1=ALU.mult))
                own(LRU_D, j, "gi", v.tensor_scalar(GI, GI, 0.5, 0.5, ALU.mult, ALU.add))
                own(LRU_D, j, "ga", v.tensor_tensor(GI, GI, XC, ALU.mult))
                dv.wait_ge(LRU_A.sem, LRU_A.at(j, "sq"))
                own(LRU_D, j, "gb", v.tensor_tensor(GI, GI, GS, ALU.mult))
                own(LRU_D, j, "scan", v.tensor_tensor_scan(out=LD[:, 1:TQ], data0=LA[:, 1:TQ], data1=GI[:, 1:TQ], initial=0.0,
                                                           op0=ALU.mult, op1=ALU.add))
                if j:
                    dv.wait_ge(s_yst, 16 * j)
                own(LRU_D, j, "y", v.tensor_tensor(YL, LD[:, XQ:TQ], GG[:, j, 64:TP], ALU.mult))

            nsh = [0]

            def shift(kind, j):
                n = nsh[0]
                nsh[0] += 1
                r = cols(kind, j)[1]
                q = {"r": j, "k": 4 + j, "v": 8 + j, "z": 12 + j}[kind]
                dv.wait_ge(s_udif, n + 1)
                dst = shifted(kind, j)
                v.scalar_tensor_tensor(out=dst, in0=dst, scalar=mu[0:r, q:q + 1], in1=UB[0:r, n % 2, 1:TQ],
                                       op0=ALU.mult, op1=ALU.add).then_inc(s_ush, 1)
                dv.wait_ge(s_ush, n + 1)

            def pair(p, part):
                jb = J
                kt = KT[:, p, Q0:TP]
                if part == 0:
                    dv.wait_ge(PR_A.sem, PR_A.at(p, "sg"))
                    own(PR_D, p, "sg", v.tensor_scalar(SG, SG, 0.5, 0.5, ALU.mult, ALU.add))
                    own(PR_D, p, "cs", v.tensor_tensor_scan(out=CS, data0=reset, data1=SG, initial=0.0, op0=ALU.mult, op1=ALU.add))
                    own(PR_D, p, "csx", v.tensor_tensor(SG, CS, SG, ALU.subtract))
                    dv.wait_ge(PR_A.sem, PR_A.at(p, "a"))
                    own(PR_D, p, "a", v.tensor_scalar(AA, AA, 0.5, 0.5, ALU.mult, ALU.add))
                    dv.wait_ge(s_z0, 5)
                    own(PR_D, p, "kk", v.tensor_scalar(KK, kt, prm[:, P_KK, p:p + 1], None, ALU.mult))
                if part == 1:
                    dv.wait_ge(s_job, jb[("ss", p)] + 1)
                    own(PR_D, p, "ssm", v.tensor_scalar(seg3(T7), bank(("ss", p)), 1e-24, None, ALU.max))
                    dv.wait_ge(PR_A.sem, PR_A.at(p, "rt"))
                    own(PR_D, p, "rec", v.reciprocal(T7, T7))
                    own(PR_D, p, "kkn", v.tensor_tensor(KK, KK, T7, ALU.mult))
                    own(PR_D, p, "kc", v.tensor_scalar(T7, AA, prm[:, P_KA, p:p + 1], prm[:, P_K1, p:p + 1], ALU.mult, ALU.add))
                    own(PR_D, p, "k2", v.tensor_tensor(kt, kt, T7, ALU.mult))
                    own(PR_D, p, "q", v.scalar_tensor_tensor(out=T7, in0=AR[:, p, 1, Q0:TP], scalar=prm[:, P_RK, p:p + 1], in1=kt,
                                                             op0=ALU.mult, op1=ALU.mult))
                if part == 2:
                    dv.wait_ge(s_job, jb[("bon", p)] + 1)
                    own(PR_D, p, "bon", v.tensor_tensor(seg3(BON[:, p, :]), bank(("bon", p)), seg3(VT[:, p, Q0:TP]), ALU.mult))
                    own(PR_D, p, "b0", v.tensor_tensor(AA, AA, KK, ALU.mult))
                    dv.wait_ge(PR_A.sem, PR_A.at(p, "iw"))
                    own(PR_D, p, "b", v.tensor_tensor(BT[:, p, Q0:TP], AA, E1, ALU.mult))
                    own(PR_D, p, "k", v.tensor_tensor(kt, kt, E1, ALU.mult))
                    dv.wait_ge(PR_A.sem, PR_A.at(p, "w"))
                    own(PR_D, p, "r", v.tensor_tensor(AR[:, p, 1, Q0:TP], AR[:, p, 1, Q0:TP], E1, ALU.mult))
                    dv.wait_ge(PR_A.sem, PR_A.at(p, "wx"))
                    own(PR_D, p, "at", v.scalar_tensor_tensor(out=AR[:, p, 0, Q0:TP], in0=KK, scalar=-1.0, in1=SG,
                                                              op0=ALU.mult, op1=ALU.mult))
            for job in JOBS:
                kind, j = job
                if kind == "lx" and j == 0:
                    conv(0)
                if kind == "gi":
                    lru(j)
                    if j < 3:
                        conv(j + 1)
                if kind in ("r", "k", "v", "z"):
                    shift(kind, j)
                    if job == ("z", 2):
                        for q, r in ((0, P), (1, 32)):
                            dv.wait_ge(s_zact, 2 + q)
                            v.tensor_scalar(ZG[0:r, q, :], ZG[0:r, q, :], 0.5, 0.5, ALU.mult, ALU.add).then_inc(s_zg, 1)
                if kind == "aa":
                    pair(j, 0)
                if kind == "ss":
                    pair(j, 1)
                if kind == "bon":
                    pair(j, 2)

            def masked(out_, in_, mask):
                return v.tensor_tensor(out_, in_, mask, ALU.mult)

            def pb(b0, lo, hi):
                return ps[:, b0, lo:hi]

            def st(m):
                return m.rearrange("p (o c) -> p o c", o=1).to_broadcast([P, PAIRS, HEAD])

            def bd(m):
                return m.rearrange("p (o h) c -> p o h c", o=1).to_broadcast([P, PAIRS, 2, HEAD])

            def dup(x4):
                return x4.rearrange("p a (o c) -> p a o c", o=1).to_broadcast([P, PAIRS, 2, HEAD])

            def quad(b0):
                return ps[:, b0, 0:512].rearrange("p (a h c) -> p a h c", h=2, c=HEAD)

            def half(b0, k):
                return ps[:, b0, 256 * k:256 * k + 256].rearrange("p (a c) -> p a c", c=HEAD)

            def first_part(s, n):
                d, B, cd = slot[s], 4 * s, CD[s]
                dv.wait_ge(CE[s].sem, CE[s].at(n, "MA"))
                own(cd, n, "D0a", masked(d["Ds"], half(B + 2, 0), st(m_sub[:, 0, :])))
                own(cd, n, "D0", v.tensor_tensor(d["Ds"], d["Ds"], st(ident2), ALU.add))
                dv.wait_ge(CE[s].sem, CE[s].at(n, "MB"))
                own(cd, n, "Mb", masked(d["Mb"], dup(quad(B)[:, :, 0, :]), bd(m_strict)))
                own(cd, n, "T0a", masked(d["Db"], dup(quad(B)[:, :, 0, :]), bd(m_supT)))
                own(cd, n, "T0", v.tensor_tensor(d["Db"], d["Db"], bd(ident.rearrange("p (h c) -> p h c", c=HEAD)), ALU.add))
                dv.wait_ge(CE[s].sem, CE[s].at(n, "MK"))
                own(cd, n, "Nb", masked(d["Nb"], dup(quad(B + 1)[:, :, 0, :]), bd(m_strict)))
                own(cd, n, "Mr", masked(d["Mr"], quad(B)[:, :, 1, :], st(m_incl)))
                own(cd, n, "Mk", masked(d["Mk"], quad(B + 1)[:, :, 1, :], st(m_incl)))

            def level_p(s, n, l):
                d, B, cd = slot[s], 4 * s, CD[s]
                dv.wait_ge(CE[s].sem, CE[s].at(n, f"P{l}"))
                if l:
                    dv.wait_ge(CP[s].sem, CP[s].at(n, f"P{l - 1}"))
                own(cd, n, f"P{l}", masked(d["Ps"], half(B, 0), st(m_sub[:, l + 1, :])))

            def level_d(s, n, l):
                d, B, cd = slot[s], 4 * s, CD[s]
                if l < 4:
                    dv.wait_ge(CE[s].sem, CE[s].at(n, f"DP{l}"))
                    own(cd, n, f"D{l + 1}", v.tensor_tensor(d["Ds"], d["Ds"], half(B, 1), ALU.add))
                dv.wait_ge(CE[s].sem, CE[s].at(n, f"PD{l}"))
                own(cd, n, f"T{l + 1}", v.tensor_tensor(d["Db"], d["Db"], quad(B + 1), ALU.add))

            def part_x(s, n):
                d, B, cd = slot[s], 4 * s, CD[s]
                dv.wait_ge(CE[s].sem, CE[s].at(n, "XZ"))
                own(cd, n, "X", masked(d["Xb"], dup(quad(B)[:, :, 0, :]), bd(blk)))

            def part_g(s, n, c):
                d, B, cd = slot[s], 4 * s, CD[s]
                dv.wait_ge(CE[s].sem, CE[s].at(n, "GT"))
                own(cd, n, "G", v.tensor_tensor(d["Gb"], quad(B + 1), bd(ident.rearrange("p (h c) -> p h c", c=HEAD)), ALU.add))
                dv.wait_ge(CE[s].sem, CE[s].at(n, "Q"))
                own(cd, n, "Q", v.tensor_tensor(d["Qs"], half(B + 2, 0), AR[:, :, 1, bass.ds(c * CH, CH)], ALU.add))

            def part_s(s, n, c):
                B, cd = 4 * s, CD[s]
                dv.wait_ge(CE[s].sem, CE[s].at(n, "S"))
                own(cd, n, "S", v.tensor_tensor(SS[1 - s], half(B + 3, 0),
                                                wc[:, :, bass.ds(c, 1)].to_broadcast([P, PAIRS, HEAD]), ALU.mult))

            def turn(slots_, n, c):
                for s in slots_:
                    first_part(s, n)
                for l in LV:
                    for s in slots_:
                        level_p(s, n, l)
                    for s in slots_:
                        level_d(s, n, l)
                for s in slots_:
                    part_x(s, n)
                for k, s in enumerate(slots_):
                    part_g(s, n, c + k)
                for k, s in enumerate(slots_):
                    part_s(s, n, c + k)

            turn((0, 1), 0, 0)
            with dv.Fori(1, (NCH - 1) // 2) as i:
                turn((0, 1), i, i * 2)
            turn((0,), (NCH - 1) // 2, NCH - 1)

            dv.wait_ge(CA[0].sem, CA[0].at((NCH - 1) // 2, "Y"))
            dv.wait_ge(CA[1].sem, CA[1].at((NCH - 1) // 2 - 1, "Y"))
            for n in range(2 * PAIRS):
                p, hf = n // 2, n % 2
                y = AR[:, p, 1, CH + hf * 512:CH + hf * 512 + 512]
                sd = gsd[n % 2]
                B = 4 * (n % 2)
                dv.wait_ge(GN_E.sem, GN_E.at(n, "mean"))
                own(GN_D, n, "c", v.scalar_tensor_tensor(out=y, in0=ps[:, B, :], scalar=-1.0 / HEAD, in1=y,
                                                         op0=ALU.mult, op1=ALU.add))
                dv.wait_ge(GN_A.sem, GN_A.at(n, "sd"))
                own(GN_D, n, "rec", v.reciprocal(sd, sd))
                own(GN_D, n, "n", v.tensor_tensor(y, y, sd, ALU.mult))
                own(GN_D, n, "aff", v.tensor_scalar(y, y, prm[:, P_GG, p:p + 1], prm[:, P_GB, p:p + 1], ALU.mult, ALU.add))
                own(GN_D, n, "bon", v.tensor_tensor(y, y, BON[:, p, XQ + hf * 512:XQ + hf * 512 + 512], ALU.add))
                dv.wait_ge(GN_E.sem, GN_E.at(n, "g"))
                own(GN_D, n, "g", v.tensor_tensor(y, y, ps[:, B + 2, :], ALU.mult))

            def logits(ti):
                dv.wait_ge(F_E.sem, F_E.at(ti, "lg"))
                v.tensor_tensor(lg[:, ti, :], ps[:, 6, 0:NG + NE], br, ALU.add).then_inc(F_L, 1)

            for ti in range(NT):
                b = ti % 2
                dv.wait_ge(s_hin[b], 16 * (ti // 2 + 1))
                for hf in range(2):
                    dv.wait_ge(F_O.sem, F_O.at(ti, f"o{hf}"))
                    cs = slice(hf * 512, (hf + 1) * 512)
                    own(F_D, ti, f"res{hf}", v.scalar_tensor_tensor(out=zb[b][:, cs], in0=hb[b][:, cs], scalar=ALPHA,
                                                                    in1=ps[:, 2 * b + hf, :], op0=ALU.mult, op1=ALU.add))
                for hf in range(2):
                    own(F_D, ti, f"st{hf}", v.bn_stats(out=st6[:, hf, :], in_=zb[b][:, hf * 512:(hf + 1) * 512]))
                v.bn_aggr(out=mv, in_=st6.rearrange("p a b -> p (a b)")).then_inc(F_D.sem, 1)
                dv.wait_ge(F_A, ti + 1)
                own(F_D, ti, "rstd", v.reciprocal(rstd[:, 1:2], rstd[:, 0:1]))
                if ti >= 2:
                    dv.wait_ge(s_h1st[b], 16 * (ti // 2))
                    dv.wait_ge(F_E.sem, F_E.at(ti - 2, "t1"))
                own(F_D, ti, "xhat", v.tensor_scalar(h1[b], zb[b], mv[:, 0:1], rstd[:, 1:2], ALU.subtract, ALU.mult))
                if ti:
                    logits(ti - 1)
            logits(NT - 1)

            rt = [0]

            def r_(ins):
                rt[0] += 1
                ins.then_inc(s_rt, 1)
                dv.wait_ge(s_rt, rt[0])

            dv.wait_ge(F_L, NT)

            dv.wait_ge(s_rtc, 5)
            r_(v.memset(g8, -3.0e38))
            for ti in range(NT):
                r_(v.tensor_copy(g8[:, 0:NG], lg[:, ti, 0:NG]))
                r_(v.max(gm8, g8))
                r_(v.max_index(gi8, gm8, g8))
                r_(v.tensor_copy(gi8f, gi8))
                r_(v.tensor_scalar(ohg, i4[:, 0:NG], gi8f[:, 0:1], None, ALU.is_equal))
                r_(v.tensor_tensor(esel, lg[:, ti, NG:NG + NE].rearrange("p (g e) -> p g e", e=EPG),
                                   ohg.rearrange("p (g o) -> p g o", o=1).to_broadcast([P, NG, EPG]), ALU.mult))
                r_(v.tensor_tensor(e8, esel[:, 0, :], esel[:, 1, :], ALU.add))
                r_(v.tensor_tensor(e8, e8, esel[:, 2, :], ALU.add))
                r_(v.tensor_tensor(e8, e8, esel[:, 3, :], ALU.add))
                r_(v.max(tm8, e8))
                r_(v.max_index(ti8, tm8, e8))
                r_(v.tensor_copy(ti8f, ti8))
                r_(v.tensor_scalar(sm[:, 0:1], gi8f[:, 0:1], float(EPG), None, ALU.mult))
                for k in range(2):
                    r_(v.tensor_tensor(eidf[:, k, ti:ti + 1], sm[:, 0:1], ti8f[:, k:k + 1], ALU.add))
                    r_(v.tensor_scalar(OH[k][:, ti, :], i4, eidf[:, k, ti:ti + 1], None, ALU.is_equal))
                r_(v.tensor_scalar(lg[:, ti, 0:NG], lg[:, ti, 0:NG], gm8[:, 0:1], None, ALU.subtract))
                arg = v.tensor_tensor(lg[:, ti, NG:NG + 1], tm8[:, 1:2], tm8[:, 0:1], ALU.subtract)
                if ti < NT - 1:
                    r_(arg)
            arg.then_inc(s_rt_arg, 1)
            r_(v.tensor_tensor(OS, OH[0], OH[1], ALU.add))
            r_(v.memset(OP[:, 0, :], 0.0))
            for ti in range(NT - 1):
                r_(v.tensor_tensor(OP[:, ti + 1, :], OP[:, ti, :], OS[:, ti, :], ALU.add))
            v.tensor_tensor(OP[:, NT, :], OP[:, NT - 1, :], OS[:, NT - 1, :], ALU.add).then_inc(s_rt_oh, 1)
            dv.wait_ge(s_rta, 1)
            r_(v.reduce_sum(s1t[:, 0, :], lg[:, :, 0:NG], axis=AXX))
            r_(v.tensor_scalar(s1t[:, 1, :], lg[:, :, NG], 1.0, None, ALU.add))
            r_(v.tensor_tensor(s1t[:, 0, :], s1t[:, 0, :], s1t[:, 1, :], ALU.mult))
            r_(v.reciprocal(gates[:, 0, :], s1t[:, 0, :]))
            r_(v.tensor_tensor(gates[:, 1, :], gates[:, 0, :], lg[:, :, NG], ALU.mult))
            dv.wait_ge(s_rte, 1)
            r_(v.tensor_copy(RK.rearrange("p a b -> p (a b)"), ps[:, 0, 0:NT * NE]))
            r_(v.tensor_copy(cnt, ps[:, 1, 0:NE]))
            r_(v.tensor_tensor(c7, cnt.rearrange("p (e o) -> p e o", o=1).to_broadcast([P, NE, 7]),
                               th7.rearrange("p (o m) -> p o m", o=1).to_broadcast([P, NE, 7]), ALU.is_gt))
            r_(v.reduce_sum(ovb, c7, axis=AXX))
            r_(v.tensor_tensor_scan(out=ovi, data0=ones[:, 0:NE], data1=ovb, initial=0.0, op0=ALU.mult, op1=ALU.add))
            r_(v.tensor_tensor(ove, ovi, ovb, ALU.subtract))
            for k in range(2):
                r_(v.tensor_tensor(t32, OH[k], RK, ALU.mult))
                r_(v.reduce_sum(rk[:, k, :], t32, axis=AXX))
                r_(v.tensor_tensor(t32, OH[k], ove.rearrange("p (o e) -> p o e", o=1).to_broadcast([P, NT, NE]), ALU.mult))
                r_(v.reduce_sum(ovs[:, k, :], t32, axis=AXX))
            rkf, qf = rk.rearrange("p k t -> p (k t)"), qk.rearrange("p k t -> p (k t)")
            ovf, ef = ovs.rearrange("p k t -> p (k t)"), eidf.rearrange("p k t -> p (k t)")
            r_(v.tensor_tensor(q7, rkf.rearrange("p (n o) -> p n o", o=1).to_broadcast([P, 2 * NT, 7]),
                               th7.rearrange("p (o m) -> p o m", o=1).to_broadcast([P, 2 * NT, 7]), ALU.is_ge))
            r_(v.reduce_sum(qf, q7, axis=AXX))
            r_(v.tensor_tensor(ovf, ovf, qf, ALU.add))
            r_(v.tensor_scalar(ovf, ovf, float(NE - 1), None, ALU.add))
            r_(v.tensor_tensor(ovf, ovf, ef, ALU.subtract))
            s1f = s1t.rearrange("p k t -> p (k t)")
            r_(v.tensor_scalar(s1f, qf, 0.0, None, ALU.is_gt))
            r_(v.tensor_tensor(ovf, ovf, s1f, ALU.mult))
            r_(v.tensor_tensor(ovf, ovf, ef, ALU.add))
            r_(v.tensor_tensor(ovf, ovf, qf, ALU.subtract))
            r_(v.scalar_tensor_tensor(out=ovf, in0=ovf, scalar=float(P), in1=rkf, op0=ALU.mult, op1=ALU.add))
            r_(v.tensor_copy(slots.rearrange("p k t -> p (k t)"), ovf))
            r_(v.tensor_tensor(o16, ovi.rearrange("p (o e) -> p o e", o=1).to_broadcast([P, OVER, NE]),
                               j16.rearrange("p (j o) -> p j o", o=1).to_broadcast([P, OVER, NE]), ALU.is_le))
            r_(v.reduce_sum(oef, o16, axis=AXX))
            r_(v.tensor_scalar(oef, oef, float(NE - 1), None, ALU.min))
            r_(v.tensor_copy(oei, oef))
            v.tensor_copy(novi, ovi[:, NE - 1:NE]).then_inc(s_rt_done, 1)

            def rows_in(s, n):
                dv.wait_ge(M_X, n + 1)
                v.tensor_copy(xT[s][:, 4:8, :], ps[:, 1, :].rearrange("p (k c) -> p k c", c=P)).then_inc(M_XD, 1)

            def hidden(s, n):
                dv.wait_ge(M_A.sem, M_A.at(n, "silu"))
                dv.wait_ge(M_E.sem, M_E.at(n, "u"))
                v.tensor_tensor(hd[s], hs[s], ps[:, 3, :], ALU.mult).then_inc(M_D.sem, 1)

            def yout(s, n):
                dv.wait_ge(M_E.sem, M_E.at(n, "y"))
                if not (isinstance(n, int) and n < 2):
                    dv.wait_ge(s_yo[s], (n - s) * 8)
                v.tensor_copy(yb[s][:, 512:1024], ps[:, 6, :]).then_inc(M_D.sem, 1)

            def pair_of_blocks(n, more):
                for s in range(2):
                    hidden(s, n + s)
                    if s == 0 or more:
                        rows_in(1 - s, n + s + 1)
                    yout(s, n + s)

            dv.wait_ge(s_sc, 16 * 2 * NT)
            rows_in(0, 0)
            pair_of_blocks(0, True)
            with dv.Fori(1, NE // 2 - 1) as i:
                pair_of_blocks(i * 2, True)
            pair_of_blocks(NE - 2, False)
            n_over = dv.value_load(novi[0:1, 0:1], min_val=0, max_val=OVER)
            for j in range(OVER):
                with dv.If(n_over > j):
                    rows_in(j % 2, NE + j)
                    hidden(j % 2, NE + j)
                    yout(j % 2, NE + j)

            for ti in range(NT):
                b = ti % 2
                dv.wait_ge(s_y1[b], 16 * (ti // 2 + 1))
                dv.wait_ge(s_hr[b], 16 * (ti // 2 + 1))
                own(O_D, ti, "y1", v.tensor_scalar(y1[b], y1[b], gates[:, 0, ti:ti + 1], None, ALU.mult))
                dv.wait_ge(s_y2[b], 16 * (ti // 2 + 1))
                own(O_D, ti, "y2", v.scalar_tensor_tensor(out=y1[b], in0=y2[b], scalar=gates[:, 1, ti:ti + 1], in1=y1[b],
                                                          op0=ALU.mult, op1=ALU.add))
                own(O_D, ti, "res", v.scalar_tensor_tensor(out=hr[b], in0=hr[b], scalar=ALPHA, in1=y1[b], op0=ALU.mult, op1=ALU.add))
                for hf in range(2):
                    own(O_D, ti, f"st{hf}", v.bn_stats(out=st6[:, hf, :], in_=hr[b][:, hf * 512:(hf + 1) * 512]))
                v.bn_aggr(out=mv, in_=st6.rearrange("p a b -> p (a b)")).then_inc(O_D.sem, 1)
                dv.wait_ge(O_A, ti + 1)
                own(O_D, ti, "rstd", v.reciprocal(rstd[:, 1:2], rstd[:, 0:1]))
                if ti >= 2:
                    dv.wait_ge(s_out[b], 16 * (ti // 2))
                own(O_D, ti, "xhat", v.tensor_scalar(o_x[b], hr[b], mv[:, 0:1], rstd[:, 1:2], ALU.subtract, ALU.mult))

        @block.scalar
        def _(ac):
            f = nc.scalar.activation

            def copy_t(ti):
                r = rows(ti)
                c0 = 1 if ti == 0 else XQ + (ti - 1) * P
                for hf in range(2):
                    ac.wait_ge(s_tp, 2 * ti + hf + 1)
                    f(hT[:, 4 * hf:4 * hf + 4, c0:c0 + r],
                      ps[:, 2 * (ti % 2) + hf, :].rearrange("p (k c) -> p k c", c=P)[:, :, 0:r], ACT.Copy).then_inc(s_ht, 1)

            for ti in range(NT + 1):
                r = rows(ti)
                ac.wait_ge(s_ln.sem, s_ln.at(ti, "agg"))
                if ti == 0:
                    ac.wait_ge(s_const, 4)
                f(rstd[0:r, 0:1], mv[0:r, 1:2], ACT.Sqrt, bias=eps[0:r, 0:1]).then_inc(s_std, 1)
                if ti:
                    copy_t(ti - 1)
            copy_t(NT)
            ac.wait_ge(s_absl, 1)
            f(lamt[:, 1, :], lamt[:, 0, :], ACT.Exp).then_inc(s_expl, 1)

            nsh = [0]
            for job in JOBS:
                kind, j = job
                if kind in ("ss", "bon"):
                    continue
                ac.wait_ge(s_job, J[job] + 1)
                if kind == "gl":
                    f(seg3(GG[:, j, Q0:TP]), bank(job), ACT.Gelu_apprx_tanh).then_inc(s_gelu, 1)
                if kind == "lx":
                    if j == 0:
                        ac.wait_ge(s_const_done, 1)
                    if j:
                        ac.wait_ge(LRU_D.sem, LRU_D.at(j - 1, "c3"))
                    f(seg3(XL[:, 3:3 + TQ]), bank(job), ACT.Copy).then_inc(s_lx, 1)
                if kind == "gr":
                    if j:
                        ac.wait_ge(LRU_D.sem, LRU_D.at(j - 1, "scan"))
                    f(seg3(GR), bank(job), ACT.Tanh, bias=hprm[:, 2, j:j + 1], scale=0.5).then_inc(LRU_A.sem, 1)
                if kind == "gi":
                    f(seg3(GI), bank(job), ACT.Tanh, bias=hprm[:, 3, j:j + 1], scale=0.5).then_inc(LRU_A.sem, 1)
                    ac.wait_ge(LRU_D.sem, LRU_D.at(j, "gr"))
                    ac.wait_ge(s_c8, 1)
                    f(LA, GR, ACT.Exp, scale=c8[:, 0, j:j + 1]).then_inc(LRU_A.sem, 1)
                    f(GS, GR, ACT.Tanh, scale=c8[:, 1, j:j + 1]).then_inc(LRU_A.sem, 1)
                    ac.wait_ge(LRU_D.sem, LRU_D.at(j, "m2"))
                    f(GS, GS, ACT.Sqrt).then_inc(LRU_A.sem, 1)
                if kind in ("z", "r", "k", "v"):
                    n = nsh[0]
                    nsh[0] += 1
                    r = cols(kind, j)[1]
                    if n >= 2:
                        ac.wait_ge(s_ush, n - 1)
                    f(seg3(UB[0:r, n % 2, :]), bank(job, r), ACT.Copy).then_inc(s_uev, 1)
                    if kind == "z":
                        ac.wait_ge(s_ush, n + 1)
                        if j == 0:
                            ac.wait_ge(s_zcol, 2)
                            f(Z0[0:64, :], Z0[0:64, :], ACT.Tanh).then_inc(s_zact, 1)
                        if j == 1:
                            f(ZG[:, 0, :], ZG0[:, XQ:TQ], ACT.Tanh, scale=0.5).then_inc(s_zact, 1)
                        if j == 2:
                            f(ZG[0:32, 1, :], XC[0:32, XQ:TQ], ACT.Tanh, scale=0.5).then_inc(s_zact, 1)
                if kind == "dec":
                    if j:
                        ac.wait_ge(PR_D.sem, PR_D.at(j - 1, "at"))
                    f(seg3(SG), bank(job), ACT.Tanh, bias=hprm[:, 0, j:j + 1], scale=0.5).then_inc(PR_A.sem, 1)
                if kind == "aa":
                    f(seg3(AA), bank(job), ACT.Tanh, bias=hprm[:, 1, j:j + 1], scale=0.5).then_inc(PR_A.sem, 1)
                    ac.wait_ge(PR_D.sem, PR_D.at(j, "kk"))
                    f(T7, KK, ACT.Square).then_inc(PR_A.sem, 1)
                    f(E1, CS, ACT.Exp, scale=DECAY).then_inc(PR_A.sem, 1)
                nxt = JOBS[J[job] + 1] if J[job] + 1 < len(JOBS) else None
                while nxt and nxt[0] in ("ss", "bon"):
                    p = nxt[1]
                    if nxt[0] == "ss":
                        ac.wait_ge(PR_D.sem, PR_D.at(p, "ssm"))
                        f(T7, T7, ACT.Sqrt).then_inc(PR_A.sem, 1)
                    else:
                        f(wc[:, p, :], CS[:, HEAD - 1 - Q0:TQ:CH], ACT.Exp, scale=-DECAY).then_inc(PR_A.sem, 1)
                        f(SG, SG, ACT.Exp, scale=-DECAY).then_inc(PR_A.sem, 1)
                        ac.wait_ge(PR_D.sem, PR_D.at(p, "k"))
                        f(E1, CS, ACT.Exp, scale=-DECAY).then_inc(PR_A.sem, 1)
                    nxt = JOBS[J[nxt] + 1] if J[nxt] + 1 < len(JOBS) else None

            def half(b0, k):
                return ps[:, b0, 256 * k:256 * k + 256].rearrange("p (a c) -> p a c", c=HEAD)

            def quad(b0):
                return ps[:, b0, :].rearrange("p (a h c) -> p a h c", h=2, c=HEAD)

            def turn(slots_, n, c):
                def take(s, src, step, dst, shared=None):
                    ac.wait_ge(CE[s].sem, CE[s].at(n, step))
                    if shared:
                        ac.wait_ge(CD[s].sem, CD[s].at(n, shared))
                    f(dst, src, ACT.Copy).then_inc(CA[s].sem, 1)

                for s in slots_:
                    take(s, half(4 * s + 2, 1), "MA", slot[s]["AN"][:, :, 0, :], "D0a")
                    take(s, half(4 * s + 3, 0), "VT", slot[s]["Vs"])
                for s in slots_:
                    take(s, half(4 * s + 3, 1), "NV", slot[s]["AN"][:, :, 1, :])
                for s in slots_:
                    take(s, quad(4 * s + 2), "BT", slot[s]["Btb"])
                for s in slots_:
                    take(s, quad(4 * s + 3), "KT", slot[s]["Ktb"])
                for s in slots_:
                    take(s, quad(4 * s + 2), "VV", slot[s]["Vtb"])
                for s in slots_:
                    take(s, quad(4 * s)[:, :, 1, :], "XZ", slot[s]["Zs"], "X")
                for k, s in enumerate(slots_):
                    take(s, half(4 * s + 2, 1), "Y", AR[:, :, 1, bass.ds((c + k) * CH, CH)])

            turn((0, 1), 0, 0)
            with ac.Fori(1, (NCH - 1) // 2) as i:
                turn((0, 1), i, i * 2)
            turn((0,), (NCH - 1) // 2, NCH - 1)

            for n in range(2 * PAIRS):
                p, hf = n // 2, n % 2
                y = AR[:, p, 1, CH + hf * 512:CH + hf * 512 + 512]
                ac.wait_ge(GN_D.sem, GN_D.at(n, "c"))
                f(gsq[n % 2], y, ACT.Square).then_inc(GN_A.sem, 1)
                ac.wait_ge(GN_E.sem, GN_E.at(n, "var"))
                f(gsd[n % 2], ps[:, 4 * (n % 2) + 1, :], ACT.Sqrt, scale=1.0 / HEAD, bias=eps[:, 1:2]).then_inc(GN_A.sem, 1)

            def copy_h(ti):
                for hf in range(2):
                    ac.wait_ge(F_E.sem, F_E.at(ti, f"t{hf}"))
                    f(h1T[ti % 2][:, 4 * hf:4 * hf + 4, :], ps[:, 4 + hf, :].rearrange("p (k c) -> p k c", c=P),
                      ACT.Copy).then_inc(F_C.sem, 1)

            for ti in range(NT):
                if ti:
                    copy_h(ti - 1)
                ac.wait_ge(F_D.sem, F_D.at(ti, "agg"))
                f(rstd[:, 0:1], mv[:, 1:2], ACT.Sqrt, bias=eps[:, 0:1]).then_inc(F_A, 1)
            copy_h(NT - 1)
            ac.wait_ge(s_rt_arg, 1)
            f(lg[:, :, 0:NG + 1], lg[:, :, 0:NG + 1], ACT.Exp).then_inc(s_rta, 1)

            def rows_in(s, n):
                ac.wait_ge(M_X, n + 1)
                f(xT[s][:, 0:4, :], ps[:, 0, :].rearrange("p (k c) -> p k c", c=P), ACT.Copy).then_inc(M_XA, 1)

            def gate(s, n):
                ac.wait_ge(M_E.sem, M_E.at(n, "g"))
                f(hs[s], ps[:, 2, :], ACT.Silu).then_inc(M_A.sem, 1)

            def hid(s, n):
                ac.wait_ge(M_E.sem, M_E.at(n, "h"))
                f(hTe[s], ps[:, 4, :].rearrange("p (k c) -> p k c", c=P), ACT.Copy).then_inc(M_A.sem, 1)

            def yout(s, n):
                ac.wait_ge(M_E.sem, M_E.at(n, "y"))
                if not (isinstance(n, int) and n < 2):
                    ac.wait_ge(s_yo[s], (n - s) * 8)
                f(yb[s][:, 0:512], ps[:, 5, :], ACT.Copy).then_inc(M_A.sem, 1)

            def pair_of_blocks(n, more):
                for s in range(2):
                    gate(s, n + s)
                    if s == 0 or more:
                        rows_in(1 - s, n + s + 1)
                    hid(s, n + s)
                    yout(s, n + s)

            ac.wait_ge(s_sc, 16 * 2 * NT)
            rows_in(0, 0)
            pair_of_blocks(0, True)
            with ac.Fori(1, NE // 2 - 1) as i:
                pair_of_blocks(i * 2, True)
            pair_of_blocks(NE - 2, False)
            n_over = ac.value_load(novi[0:1, 0:1], min_val=0, max_val=OVER)
            for j in range(OVER):
                with ac.If(n_over > j):
                    rows_in(j % 2, NE + j)
                    gate(j % 2, NE + j)
                    hid(j % 2, NE + j)
                    yout(j % 2, NE + j)

            for ti in range(NT):
                ac.wait_ge(O_D.sem, O_D.at(ti, "agg"))
                f(rstd[:, 0:1], mv[:, 1:2], ACT.Sqrt, bias=eps[:, 0:1]).then_inc(O_A, 1)

        @block.tensor
        def _(pe):
            mm, tr = nc.tensor.matmul, nc.tensor.transpose

            pe.wait_ge(s_const, 2)
            for ti in range(NT + 1):
                b, r = ti % 2, rows(ti)
                pe.wait_ge(s_h.sem, s_h.at(ti, "bias"))
                if ti >= 2:
                    pe.wait_ge(s_ht, 2 * (ti - 1))
                for hf in range(2):
                    for k in range(4):
                        last = tr(ps[:, 2 * b + hf, k * P:k * P + r], xh[b][0:r, (4 * hf + k) * P:(4 * hf + k + 1) * P],
                                  ident[0:r, 0:r])
                    last.then_inc(s_tp, 1)

            def emptied(job):
                kind, j = job
                if kind == "gl":
                    pe.wait_ge(s_gelu, j + 1)
                elif kind == "lx":
                    pe.wait_ge(s_lx, j + 1)
                elif kind in ("gr", "gi"):
                    pe.wait_ge(LRU_A.sem, LRU_A.at(j, kind))
                elif kind in ("z", "r", "k", "v"):
                    pe.wait_ge(s_uev, SHIFTED.index(job) + 1)
                elif kind == "dec":
                    pe.wait_ge(PR_A.sem, PR_A.at(j, "sg"))
                elif kind == "aa":
                    pe.wait_ge(PR_A.sem, PR_A.at(j, "a"))
                elif kind == "ss":
                    pe.wait_ge(PR_D.sem, PR_D.at(j, "ssm"))
                else:
                    pe.wait_ge(PR_D.sem, PR_D.at(j, "bon"))

            pe.wait_ge(s_ht, 2 * (NT + 1))
            pe.wait_ge(s_zcol, 1)
            for n, job in enumerate(JOBS):
                kind, j = job
                if n >= 2:
                    emptied(JOBS[n - 2])
                if job in WTILES:
                    w = WTILES.index(job)
                    width = cols(kind, j)[1]
                    pe.wait_ge(s_w[w % 2], 16 * (w // 2 + 1))
                    for k in range(KD):
                        for q in range(3):
                            last = mm(bank(job, width)[:, q, :], wbuf[w % 2][:, k, 0:width], hT[:, k, q * SEG:(q + 1) * SEG],
                                      start=k == 0, stop=k == KD - 1)
                else:
                    if kind in ("gr", "gi"):
                        pe.wait_ge(s_gate_w, 64)
                        pe.wait_ge(LRU_D.sem, LRU_D.at(j, "c3"))
                        lhs, rhs = (wrg if kind == "gr" else wig)[:, j, :], XC
                    elif kind in ("dec", "aa"):
                        pe.wait_ge(s_zact, 1)
                        pe.wait_ge(s_prm, 16 * 15)
                        h = slice(0, 64) if kind == "dec" else slice(64, 128)
                        lhs, rhs = wlr[h, j * P:(j + 1) * P], Z0[h, :]
                    elif kind == "ss":
                        pe.wait_ge(PR_A.sem, PR_A.at(j, "sq"))
                        pe.wait_ge(s_const_done, 1)
                        lhs, rhs = blk.rearrange("p h c -> p (h c)"), T7
                    else:
                        pe.wait_ge(PR_D.sem, PR_D.at(j, "q"))
                        lhs, rhs = blk.rearrange("p h c -> p (h c)"), T7
                    for q in range(3):
                        last = mm(bank(job)[:, q, :], lhs, rhs[:, q * SEG:(q + 1) * SEG], start=True, stop=True)
                last.then_inc(s_job, 1)

            def L(m):
                return lambda p: m[:, p, :, :].rearrange("p h c -> p (h c)")

            def group(s, out_, pairs_of):
                for p in range(PAIRS):
                    ops = pairs_of(p)
                    for q, (lh, rh) in enumerate(ops):
                        last = mm(out_(p), lh, rh, start=q == 0, stop=q == len(ops) - 1)
                last.then_inc(CE[s].sem, 1)

            def half(b0, k):
                return lambda p: ps[:, b0, 256 * k + p * HEAD:256 * k + (p + 1) * HEAD]

            def whole(b0):
                return lambda p: ps[:, b0, p * P:(p + 1) * P]

            def turn(slots_, n, c):
                def W(st_, name, m=None):
                    pe.wait_ge(st_.sem, st_.at(n if m is None else m, name))

                for k, s in enumerate(slots_):
                    d, B = slot[s], 4 * s
                    at = bass.ds((c + k) * CH, CH)
                    W(CP[s], "A")
                    if not first(n):
                        W(CA[s], "Y", n - 1)
                        W(CD[s], "S", n - 1)
                    for p in range(PAIRS):
                        mm(half(B + 2, 0)(p), L(d["Ab"])(p), BT[:, p, at], start=True, stop=True)
                        last = mm(half(B + 2, 1)(p), L(d["Ab"])(p), ident2, start=True, stop=True)
                    last.then_inc(CE[s].sem, 1)
                    W(CP[s], "B")
                    group(s, whole(B), lambda p: [(L(d["Bb"])(p), AR[:, p, :, at])])
                    W(CP[s], "V")
                    group(s, half(B + 3, 0), lambda p: [(L(d["Vb"])(p), ident2)])
                    group(s, whole(B + 1), lambda p: [(L(d["Kb"])(p), AR[:, p, :, at])])
                for s in slots_:
                    d, B = slot[s], 4 * s
                    W(CD[s], "Nb")
                    W(CA[s], "Vs")
                    group(s, half(B + 3, 1), lambda p: [(L(d["Nb"])(p), d["Vs"][:, p, :])])
                for l in LV:
                    for s in slots_:
                        d, B = slot[s], 4 * s
                        W(CD[s], "Mr" if l == 0 else f"D{l}")
                        group(s, half(B, 0), lambda p: [(L(d["Mb"])(p), d["Ds"][:, p, :])])
                    if l < 3:
                        for s in slots_:
                            d, B = slot[s], 4 * s
                            if l == 0:
                                W(CA[s], "At")
                            else:
                                W(CA[s], "NV" if l == 1 else "Bt")
                            b0, src = ((B + 2, "Bb"), (B + 3, "Kb"), (B + 2, "Vb"))[l]
                            for p in range(PAIRS):
                                last = tr(whole(b0)(p), L(d[src])(p), ident)
                            last.then_inc(CE[s].sem, 1)
                    for s in slots_:
                        d, B = slot[s], 4 * s
                        W(CD[s], f"P{l}")
                        if l < 4:
                            group(s, half(B, 1), lambda p: [(L(d["Db"])(p), d["Ps"][:, p, :])])
                        if l == 0:
                            W(CD[s], "Mk")
                        W(CP[s], f"P{l}")
                        group(s, whole(B + 1), lambda p: [(L(d["Pb"])(p), L(d["Db"])(p))])
                for s in slots_:
                    d, B = slot[s], 4 * s
                    W(CD[s], "T5")
                    group(s, whole(B), lambda p: [(L(d["Db"])(p), L(d["AN"])(p))])
                for s in slots_:
                    d, B = slot[s], 4 * s
                    W(CD[s], "X")
                    W(CA[s], "Vv")
                    group(s, whole(B + 1), lambda p: [(L(d["Xb"])(p), L(d["Btb"])(p))])
                    group(s, half(B + 2, 0), lambda p: [(L(d["Xb"])(p), d["Mr"][:, p, :])])
                for s in slots_:
                    d, B = slot[s], 4 * s
                    W(CA[s], "Z")
                    W(CD[s], "Q")
                    if s == 1:
                        W(CD[0], "S")
                    elif not first(n):
                        W(CD[1], "S", n - 1)
                    group(s, half(B + 3, 0), lambda p: [(L(d["Btb"])(p), d["Zs"][:, p, :]), (L(d["Ktb"])(p), d["Vs"][:, p, :]),
                                                        (L(d["Gb"])(p), SS[s][:, p, :])])
                    W(CP[s], "Z")
                    if s == 1:
                        W(CP[0], "S")
                    elif not first(n):
                        W(CP[1], "S", n - 1)
                    group(s, half(B + 2, 1), lambda p: [(L(d["Zb"])(p), d["Mr"][:, p, :]), (L(d["Vtb"])(p), d["Mk"][:, p, :]),
                                                        (L(SB[s])(p), d["Qs"][:, p, :])])

            pe.wait_ge(s_z0, 7)
            pe.wait_ge(PR_D.sem, PR_D.at(PAIRS - 1, "at"))
            turn((0, 1), 0, 0)
            with pe.Fori(1, (NCH - 1) // 2) as i:
                turn((0, 1), i, i * 2)
            turn((0,), (NCH - 1) // 2, NCH - 1)

            pe.wait_ge(s_wgu, 32)
            pe.wait_ge(s_zg, 2)
            for s in range(2):
                pe.wait_ge(CA[s].sem, CA[s].at((NCH - 1) // 2 - s, "Y"))
                pe.wait_ge(CD[s].sem, CD[s].at((NCH - 1) // 2 - s, "S"))
            sums = blk.rearrange("p h c -> p (h c)")
            for n in range(2 * PAIRS):
                p, hf = n // 2, n % 2
                B = 4 * (n % 2)
                cs = slice(hf * 512, hf * 512 + 512)
                if n >= 2:
                    pe.wait_ge(GN_D.sem, GN_D.at(n - 2, "g"))
                mm(ps[:, B, :], sums, AR[:, p, 1, CH + hf * 512:CH + hf * 512 + 512], start=True, stop=True).then_inc(GN_E.sem, 1)
                mm(ps[:, B + 2, :], wgu[:, 0, p * P:(p + 1) * P], ZG[:, 0, cs], start=True, stop=False)
                mm(ps[:, B + 2, :], wgu[0:32, 1, p * P:(p + 1) * P], ZG[0:32, 1, cs], start=False, stop=True).then_inc(GN_E.sem, 1)
                pe.wait_ge(GN_A.sem, GN_A.at(n, "sq"))
                mm(ps[:, B + 1, :], sums, gsq[n % 2], start=True, stop=True).then_inc(GN_E.sem, 1)

            def router(ti):
                b = ti % 2
                pe.wait_ge(F_P.sem, F_P.at(ti, "bias"))
                if ti:
                    pe.wait_ge(F_C.sem, F_C.at(ti - 1, "t1"))
                    pe.wait_ge(F_L, ti)
                for hf in range(2):
                    for k in range(4):
                        last = tr(ps[:, 4 + hf, k * P:(k + 1) * P], h1[b][:, (4 * hf + k) * P:(4 * hf + k + 1) * P], ident)
                    last.then_inc(F_E.sem, 1)
                pe.wait_ge(F_C.sem, F_C.at(ti, "t1"))
                for k in range(KD):
                    last = mm(ps[:, 6, 0:NG + NE], h1T[b][:, k, :], wr[:, k, :], start=k == 0, stop=k == KD - 1)
                last.then_inc(F_E.sem, 1)

            pe.wait_ge(GN_D.sem, GN_D.at(2 * PAIRS - 1, "g"))
            pe.wait_ge(s_wo, 16)
            pe.wait_ge(s_yl, 16)
            pe.wait_ge(s_wr, 64)
            for ti in range(NT):
                b = ti % 2
                if ti >= 2:
                    pe.wait_ge(F_D.sem, F_D.at(ti - 2, "res1"))
                for hf in range(2):
                    for k in range(KD):
                        y = AR[:, k, 1, CH + ti * P:CH + (ti + 1) * P] if k < PAIRS else yl[:, k - PAIRS, ti * P:(ti + 1) * P]
                        last = mm(ps[:, 2 * b + hf, :], y, wo[:, k, hf * 512:(hf + 1) * 512], start=k == 0, stop=k == KD - 1)
                    last.then_inc(F_O.sem, 1)
                if ti:
                    router(ti - 1)
            router(NT - 1)
            pe.wait_ge(s_rt_oh, 1)
            mm(ps[:, 0, 0:NT * NE], ltri, OS.rearrange("p a b -> p (a b)"), start=True, stop=False)
            mm(ps[:, 0, 0:NT * NE], ones, OP[:, 0:NT, :].rearrange("p a b -> p (a b)"), start=False, stop=True)
            mm(ps[:, 1, 0:NE], ones, OP[:, NT, :], start=True, stop=True).then_inc(s_rte, 1)

            def rows_in(s, n):
                pe.wait_ge(s_xg[s], (n - s) * 8 + 16)
                if not first(n):
                    pe.wait_ge(M_XA, n)
                    pe.wait_ge(M_XD, n)
                xv = xg[s].rearrange("p (c k) -> p k c", k=KD)
                for k in range(KD):
                    last = tr(ps[:, k // 4, (k % 4) * P:(k % 4 + 1) * P], xv[:, k, :], ident)
                last.then_inc(M_X, 1)

            def up(s, n):
                wg, wu, wd = we[s]
                pe.wait_ge(M_XA, n + 1)
                pe.wait_ge(M_XD, n + 1)
                if not first(n):
                    pe.wait_ge(M_A.sem, M_A.at(n - 1, "silu"))
                pe.wait_ge(s_wg[0][s], (n - s) * 8 + 16)
                for k in range(KD):
                    last = mm(ps[:, 2, :], xT[s][:, k, :], wg[:, k, :], start=k == 0, stop=k == KD - 1)
                last.then_inc(M_E.sem, 1)
                if not first(n):
                    pe.wait_ge(M_D.sem, M_D.at(n - 1, "hid"))
                pe.wait_ge(s_wg[1][s], (n - s) * 8 + 16)
                for k in range(KD):
                    last = mm(ps[:, 3, :], xT[s][:, k, :], wu[:, k, :], start=k == 0, stop=k == KD - 1)
                last.then_inc(M_E.sem, 1)

            def down(s, n):
                wg, wu, wd = we[s]
                pe.wait_ge(M_D.sem, M_D.at(n, "hid"))
                if not first(n):
                    pe.wait_ge(M_A.sem, M_A.at(n - 1, "y"))
                    pe.wait_ge(M_D.sem, M_D.at(n - 1, "y"))
                hv = hd[s].rearrange("p (c k) -> p k c", k=KF)
                for k in range(KF):
                    last = tr(ps[:, 4, k * P:(k + 1) * P], hv[:, k, :], ident)
                last.then_inc(M_E.sem, 1)
                pe.wait_ge(M_A.sem, M_A.at(n, "h"))
                pe.wait_ge(s_wg[2][s], (n - s) * 8 + 16)
                for hf in range(2):
                    for k in range(KF):
                        last = mm(ps[:, 5 + hf, :], hTe[s][:, k, :], wd[:, k, hf * 512:(hf + 1) * 512],
                                  start=k == 0, stop=k == KF - 1)
                last.then_inc(M_E.sem, 1)

            def pair_of_blocks(n, more):
                for s in range(2):
                    up(s, n + s)
                    if s == 0 or more:
                        rows_in(1 - s, n + s + 1)
                    down(s, n + s)

            rows_in(0, 0)
            pair_of_blocks(0, True)
            with pe.Fori(1, NE // 2 - 1) as i:
                pair_of_blocks(i * 2, True)
            pair_of_blocks(NE - 2, False)
            n_over = pe.value_load(novi[0:1, 0:1], min_val=0, max_val=OVER)
            for j in range(OVER):
                with pe.If(n_over > j):
                    rows_in(j % 2, NE + j)
                    up(j % 2, NE + j)
                    down(j % 2, NE + j)


_INS = ["x", "meta", "ln0_g", "ln0_b", "w_in", "mu_shift", "w0", "w_decay_up", "a0", "w_a_up", "w_g_up", "k_k", "k_a", "r_k",
        "gn_g", "gn_b", "conv_w", "conv_b", "w_rg", "b_rg", "w_ig", "b_ig", "lru_lambda", "w_out", "ln1_g", "ln1_b",
        "w_router_grp", "b_router_grp", "w_router_exp", "b_router_exp", "w_exp_gate", "w_exp_up", "w_exp_down",
        "ln2_g", "ln2_b"]


def kernel(**inputs):
    import numpy as _np
    import concourse.bacc as _bacc
    from concourse import mybir as _mybir
    from concourse.bass_utils import run_bass_kernel_spmd as _run

    nc = _bacc.Bacc("TRN2", target_bir_lowering=False, num_devices=1)
    f32, i32 = _mybir.dt.float32, _mybir.dt.int32
    arrays, args = {}, {}
    for name in _INS:
        v = _np.ascontiguousarray(inputs[name])
        arrays[f"in_{name}_dram"] = v
        args[name] = nc.dram_tensor(f"in_{name}_dram", v.shape, _mybir.dt.from_np(v.dtype), kind="ExternalInput").ap()
    out = nc.dram_tensor("out_dram", (1, SEQ, D), f32, kind="ExternalOutput").ap()
    scratch = {
        "h": nc.dram_tensor("scr_h", (SEQ, D), f32).ap(),
        "ylru": nc.dram_tensor("scr_ylru", (4 * P, SEQ), f32).ap(),
        "h1": nc.dram_tensor("scr_h1", (SEQ, D), f32).ap(),
        "tok": nc.dram_tensor("scr_tok", (NBLK * CAP, 1), i32).ap(),
        "y": nc.dram_tensor("scr_y", (NBLK * CAP, D), f32).ap(),
    }
    build(nc, args, out, scratch)
    r = _run(nc, [arrays], core_ids=[0])
    return r.results[0]["out_dram"]
```

```python
from contextlib import ExitStack

import concourse.bass as bass
from concourse import mybir

F32 = mybir.dt.float32
BF16 = mybir.dt.bfloat16
I32 = mybir.dt.int32
U32 = mybir.dt.uint32
ALU = mybir.AluOpType
ACT = mybir.ActivationFunctionType
AXX = mybir.AxisListType.X

D = 1024
SEQ = 1024
META = 16
P = 128
KD = D // P
NT = SEQ // P
HEAD = 64
PAIRS = 4
CH = 64
NCH = 17
TP = NCH * CH
PAD = TP - SEQ - META
TQ = SEQ + META + 1
Q0 = PAD - 1
SEG = TQ // 3
XQ = META + 1
DECAY = 0.6065306597126334
N_RWKV = 1824
GATE = 160
NG, EPG = 4, 8
NE = NG * EPG
FE = 512
KF = FE // P
CAP = P
OVER = 16
NBLK = NE + OVER
ALPHA = 2.0 ** 0.25
LN_EPS, GN_EPS = 1e-5, 64e-5


class Steps:

    def __init__(self, sem, names):
        self.sem, self.names = sem, list(names)

    def at(self, turn, name):
        return turn * len(self.names) + (self.names.index(name) + 1)


def build(nc, a, out, scratch):
    ctx = ExitStack()
    with ctx:
        def sem(name):
            return ctx.enter_context(nc.semaphore(name))

        WORDS = 53000
        big = ctx.enter_context(nc.sbuf_tensor("big", [P, WORDS], F32))
        ps = ctx.enter_context(nc.psum_tensor("ps", [P, 8, 512], F32))

        class Region:
            def __init__(self, at):
                self.at = at

            def take(self, *shape):
                n = 1
                for s in shape:
                    n *= s
                v = big[:, self.at:self.at + n]
                self.at += n
                assert self.at <= WORDS, self.at
                if len(shape) == 2:
                    v = v.rearrange("p (a b) -> p a b", b=shape[1])
                elif len(shape) == 3:
                    v = v.rearrange("p (a b c) -> p a b c", b=shape[1], c=shape[2])
                return v

        R = Region(0)
        ident = R.take(P)
        blk = R.take(2, HEAD)
        ident2 = R.take(HEAD)
        m_strict = R.take(2, HEAD)
        m_incl = R.take(HEAD)
        m_sub = R.take(5, 2 * HEAD).rearrange("p l (h c) -> p l h c", c=HEAD)
        m_supT = R.take(2, HEAD)
        ones = R.take(P)
        ltri = R.take(P)
        lng = R.take(D)
        lnb = R.take(D)
        mu = R.take(15)
        prm = R.take(12, 4)
        (P_W0, P_A0, P_KK, P_KA, P_RK, P_GG, P_GB, P_CB, P_BR, P_BI, P_LAM, P_K1) = range(12)
        cw = R.take(4, 4)
        c8 = R.take(2, 4)
        lamt = R.take(6, 4)
        hprm = R.take(4, 4)
        eps = R.take(2)
        st6 = R.take(2, 6)
        mv = R.take(2)
        rstd = R.take(2)
        wc = R.take(PAIRS, NCH)
        wlr = R.take(512)
        BASE = R.at

        AR = R.take(PAIRS, 2, TP)
        BT = R.take(PAIRS, TP)
        KT = R.take(PAIRS, TP)
        VT = R.take(PAIRS, TP)
        BON = R.take(PAIRS, TQ)
        ZG = R.take(2, SEQ)
        AFTER = R.at

        hT = R.take(KD, TQ)
        wbuf = [R.take(KD, P) for _ in range(2)]
        rst = R.take(TQ // 2 + 1)
        reset = rst.bitcast(BF16)[:, 0:TQ]
        UB = R.take(2, TQ)
        Z0 = R.take(TQ)
        TM = [R.take(TQ) for _ in range(6)]
        SG, CS, E1, AA, KK, T7 = TM
        ZG0, XC, GR, GI, GS, LD = TM

        RA = Region(AFTER + KD * TQ + 2 * KD * P + TQ // 2 + 1)
        xb = [RA.take(D) for _ in range(2)]
        xh = [RA.take(D) for _ in range(2)]

        GG = BT
        wrg = VT[:, 0, 0:512].rearrange("p (j c) -> p j c", c=P)
        wig = VT[:, 0, 512:1024].rearrange("p (j c) -> p j c", c=P)
        LA = VT[:, 1, 0:TQ]
        YL = VT[:, 2, 0:SEQ]
        YZ = KT[:, 0, 0:D]
        XL = VT[:, 3, 0:1044]

        (meta_d, x_d) = (a["meta"], a["x"])
        h_dram, ylru_dram, h1_dram, tok_dram, y_dram = (
            scratch[n] for n in ("h", "ylru", "h1", "tok", "y"))

        s_const = sem("s_const")
        s_prm = sem("s_prm")
        s_gate_w = sem("s_gate_w")
        s_const_done = sem("s_const_done")
        s_lnp = sem("s_lnp")
        s_xin = [sem(f"s_xin{i}") for i in range(2)]
        s_ln = Steps(sem("s_ln"), ["st0", "st1", "agg", "rstd", "xhat"])
        s_std = sem("s_std")
        s_h = Steps(sem("s_h"), ["gain", "bias"])
        s_tp = sem("s_tp")
        s_ht = sem("s_ht")
        s_hst = [sem(f"s_hst{i}") for i in range(2)]
        s_yz, s_yzd = sem("s_yz"), sem("s_yzd")
        s_zcol = sem("s_zcol")
        s_setup = sem("s_setup")
        s_hp, s_absl, s_expl, s_c8 = sem("s_hp"), sem("s_absl"), sem("s_expl"), sem("s_c8")

        def cols(kind, j):
            base = {"r": 0, "k": 512, "v": 1024, "lx": N_RWKV, "gl": N_RWKV + 512}
            if kind == "z":
                return (1536 + P * j, P if j < 2 else 32)
            return base[kind] + P * j, P

        JOBS = ([("gl", j) for j in range(4)]
                + [("lx", 0), ("lx", 1), ("gr", 0), ("gi", 0), ("lx", 2), ("gr", 1), ("gi", 1), ("lx", 3),
                   ("gr", 2), ("gi", 2), ("z", 0), ("z", 1), ("gr", 3), ("gi", 3), ("z", 2)]
                + [("r", 0), ("k", 0), ("v", 0)])
        for p in range(PAIRS):
            nxt = [("r", p + 1), ("k", p + 1), ("v", p + 1)] if p + 1 < PAIRS else []
            JOBS += [("dec", p), ("aa", p)] + nxt[0:1] + [("ss", p)] + nxt[1:2] + [("bon", p)] + nxt[2:]
        J = {j: n for n, j in enumerate(JOBS)}
        WTILES = [j for j in JOBS if j[0] in ("gl", "lx", "z", "r", "k", "v")]
        s_w = [sem(f"s_w{i}") for i in range(2)]
        s_job = sem("s_job")
        SHIFTED = [j for j in JOBS if j[0] in ("z", "r", "k", "v")]

        def bank(job, rows=P):
            s = J[job] % 2
            return ps[0:rows, 3 * s:3 * s + 3, 0:SEG]

        def seg3(v):
            return v.rearrange("p (s c) -> p s c", c=SEG)

        s_gelu = sem("s_gelu")
        s_uev = sem("s_uev")
        s_udif = sem("s_udif")
        s_ush = sem("s_ush")
        s_zact = sem("s_zact")
        s_zg = sem("s_zg")
        LRU_D = Steps(sem("s_lrud"), ["c0", "c1", "c2", "c3", "gr", "d1", "rec", "m2", "gi", "ga", "gb", "scan", "y"])
        s_lx = sem("s_lx")
        LRU_A = Steps(sem("s_lrua"), ["gr", "gi", "la", "gs", "sq"])
        s_yst = sem("s_yst")
        PR_D = Steps(sem("s_prd"), ["sg", "cs", "csx", "a", "kk", "ssm", "rec", "kkn", "kc", "k2", "q", "bon",
                                    "b0", "b", "k", "r", "at"])
        PR_A = Steps(sem("s_pra"), ["sg", "a", "sq", "iw", "rt", "w63", "wx", "w"])
        s_z0 = sem("s_z0")

        RC = Region(AFTER)
        slot = []
        for s in range(2):
            d = {n: RC.take(PAIRS, 2, HEAD) for n in
                 ("Ab", "Bb", "Kb", "Vb",
                  "Mb", "Nb",
                  "Db", "Tb", "Pb",
                  "Vtb", "Xb", "Zb",
                  "AN",
                  "RB", "RK",
                  "QG",
                  "Sb")}
            slot.append(d)
        SB = [RC.take(PAIRS, 2, HEAD) for _ in range(2)]

        LV = range(5)
        CP = [Steps(sem(f"s_cp{s}"), ["B", "K", "V", "A"]) for s in range(2)]
        CM = [Steps(sem(f"s_cs{s}"), ["MB", "MK"]) for s in range(2)]
        CE = [Steps(sem(f"s_ce{s}"), ["D0", "P0", "Vt", "DP0", "P1", "T1", "Bt", "DP1", "P2", "T2", "NV", "DP2", "P3",
                                      "T3", "Kt", "DP3", "P4", "T4", "At", "PD", "XZ", "QG", "YS", "St"])
              for s in range(2)]
        CD = [Steps(sem(f"s_cd{s}"), ["T0a", "T0", "Mb", "Mr", "Nb", "Mk", "P0", "D1", "P1", "D2", "P2", "D3", "P3",
                                      "D4", "P4", "T5", "G", "Q", "S"]) for s in range(2)]
        CB = [Steps(sem(f"s_cb{s}"), ["SB"]) for s in range(2)]
        CA = [Steps(sem(f"s_ca{s}"), ["D0", "Vt", "T1", "Bt", "T2", "NV", "T3", "Kt", "T4", "At", "X", "Z", "Y"])
              for s in range(2)]

        RE = Region(AFTER)
        yl = RE.take(4, SEQ)
        wo = RE.take(KD, D)
        gsq = [RE.take(512) for _ in range(2)]
        gsd = [RE.take(512) for _ in range(2)]
        wgu = RE.take(2, 512)
        GN_D = Steps(sem("s_gnd"), ["c", "rec", "n", "aff", "bon", "g"])
        GN_A = Steps(sem("s_gna"), ["sq", "sd"])
        GN_E = Steps(sem("s_gne"), ["mean", "g", "var"])
        s_wo, s_yl, s_wgu = sem("s_wo"), sem("s_yl"), sem("s_wgu")

        RF = Region(BASE + PAIRS * 2 * TP)
        hb = [RF.take(D) for _ in range(2)]
        zb = [RF.take(D) for _ in range(2)]
        h1 = [RF.take(D) for _ in range(2)]
        h1T = [RF.take(KD, P) for _ in range(2)]
        RF = Region(BASE + 6 * KD * FE)
        wr = RF.take(KD, NG + NE)
        br = RF.take(NG + NE)
        lg = RF.take(NT, NG + NE)
        F_D = Steps(sem("s_fd"), ["res0", "res1", "st0", "st1", "agg", "rstd", "xhat"])
        F_L = sem("s_fl")
        F_P = Steps(sem("s_fp"), ["gain", "bias"])
        F_A = sem("s_fa")
        F_C = Steps(sem("s_fc"), ["t0", "t1"])
        F_O = Steps(sem("s_fo"), ["o0", "o1"])
        F_E = Steps(sem("s_fe"), ["t0", "t1", "lg"])
        s_hin = [sem(f"s_hin{i}") for i in range(2)]
        s_h1st = [sem(f"s_h1st{i}") for i in range(2)]
        s_wr, s_ln1 = sem("s_wr"), sem("s_ln1")

        g8 = RF.take(8)
        i4 = RF.take(NE)
        e8 = RF.take(EPG)
        gm8, gi8f = RF.take(8), RF.take(8)
        gi8 = RF.take(8).bitcast(U32)
        ti8 = RF.take(8).bitcast(U32)
        ti8f = RF.take(8)
        ohg = RF.take(NG)
        esel = RF.take(NG, EPG)
        tm8 = RF.take(8)
        sm = RF.take(16)
        oh_at = RF.at
        OH = [RF.take(NT, NE) for _ in range(2)]
        OS = RF.take(NT, NE)
        OP = RF.take(NT + 1, NE)
        RK = RF.take(NT, NE)
        t32 = RF.take(NT, NE)
        eidf = RF.take(2, NT)
        rk = RF.take(2, NT)
        ovs = RF.take(2, NT)
        qk = RF.take(2, NT)
        q7 = RF.take(2 * NT, 7)
        th7 = RF.take(7)
        cnt = RF.take(NE)
        c7 = RF.take(NE, 7)
        ovb, ovi, ove = RF.take(NE), RF.take(NE), RF.take(NE)
        j16 = RF.take(OVER)
        o16 = big[:, oh_at:oh_at + OVER * NE].rearrange("p (j e) -> p j e", e=NE)
        oef = RF.take(OVER)
        s1t = RF.take(2, NT)
        ztab = RF.take(NBLK * CAP // P)
        assert RF.at <= AFTER, RF.at
        KEEP = 52800
        RK2 = Region(KEEP)
        gates = RK2.take(2, NT)
        slots = RK2.take(2, NT).bitcast(I32)
        oei = RK2.take(OVER).bitcast(I32)
        novi = RK2.take(1).bitcast(I32)
        tokid = RK2.take(NT).bitcast(I32)
        idx = RK2.take(NBLK).bitcast(I32)
        s_rt = sem("s_rt")
        s_rt_arg, s_rt_oh, s_rt_done = sem("s_rt_arg"), sem("s_rt_oh"), sem("s_rt_done")
        s_rta = sem("s_rta")
        s_rte = sem("s_rte")
        s_rtc = sem("s_rtc")
        s_zt, s_sc, s_idx = sem("s_zt"), sem("s_sc"), sem("s_idx")

        RM = Region(BASE)

        def halves(*shape):
            n = 1
            for x in shape:
                n *= x
            out_ = []
            for _ in range(2):
                v = RM.take(n // 2).bitcast(BF16)
                if len(shape) == 2:
                    v = v.rearrange("p (a b) -> p a b", b=shape[1])
                out_.append(v)
            return out_

        raw = [RM.take(KD, FE), RM.take(KD, FE), RM.take(KF, D)]
        wsp = [[halves(KD, FE), halves(KD, FE), halves(KF, D)] for _ in range(2)]
        xg = [RM.take(D) for _ in range(2)]
        xT = [halves(KD, P) for _ in range(2)]
        hs = [RM.take(FE) for _ in range(2)]
        hd = [RM.take(FE) for _ in range(2)]
        hTe = [halves(KF, P) for _ in range(2)]
        yb = [RM.take(D) for _ in range(2)]
        assert RM.at <= KEEP, RM.at
        s_we = [sem(f"s_we{k}") for k in range(3)]
        s_hi = [sem(f"s_hi{k}") for k in range(3)]
        s_lo = [sem(f"s_lo{k}") for k in range(3)]
        s_xg = [sem(f"s_xg{i}") for i in range(2)]
        E_X, E_G, E_U, E_H, E_Y = (sem(f"s_e{n}") for n in "xguhy")
        A_X, A_S, A_H, A_Y = (sem(f"s_a{n}") for n in "xshy")
        V_X, V_M, V_H, V_Y = (sem(f"s_v{n}") for n in "xmhy")
        s_yo = [sem(f"s_yo{i}") for i in range(2)]

        RO = Region(BASE)
        y1 = [RO.take(D) for _ in range(2)]
        y2 = [RO.take(D) for _ in range(2)]
        hr = [RO.take(D) for _ in range(2)]
        o_x = [RO.take(D) for _ in range(2)]
        s_y1 = [sem(f"s_y1{i}") for i in range(2)]
        s_y2 = [sem(f"s_y2{i}") for i in range(2)]
        s_hr = [sem(f"s_hr{i}") for i in range(2)]
        s_ln2 = sem("s_ln2")
        O_D = Steps(sem("s_od"), ["y1", "y2", "res", "st0", "st1", "agg", "rstd", "xhat"])
        O_A = sem("s_oa")
        O_P = Steps(sem("s_op"), ["gain", "bias"])
        s_out = [sem(f"s_out{i}") for i in range(2)]

        block = ctx.enter_context(nc.Block())

        def rows(ti):
            return META if ti == 0 else P

        def first(n):
            return isinstance(n, int) and n == 0

        def shifted(kind, j):
            if kind == "r":
                return AR[:, j, 1, PAD:TP]
            if kind == "k":
                return KT[:, j, PAD:TP]
            if kind == "v":
                return VT[:, j, PAD:TP]
            return (Z0[:, 1:TQ], TM[0][:, 1:TQ], TM[1][0:32, 1:TQ])[j]

        def finish(pl, g, ti):
            b = ti % 2
            pl.wait_ge(O_D.sem, O_D.at(ti, "xhat"))
            g.tensor_tensor(o_x[b], o_x[b], lng, ALU.mult).then_inc(O_P.sem, 1)
            pl.wait_ge(O_P.sem, O_P.at(ti, "gain"))
            g.tensor_tensor(o_x[b], o_x[b], lnb, ALU.add).then_inc(O_P.sem, 1)

        @block.sync
        def _(sp):
            sp.dma_start(lng, a["ln0_g"].rearrange("(o n) -> o n", o=1).to_broadcast([P, D])).then_inc(s_lnp, 16)
            sp.dma_start(lnb, a["ln0_b"].rearrange("(o n) -> o n", o=1).to_broadcast([P, D])).then_inc(s_lnp, 16)
            for ti in range(NT + 1):
                b = ti % 2
                if ti >= 2:
                    sp.wait_ge(s_ln.sem, s_ln.at(ti - 2, "xhat"))
                src = meta_d if ti == 0 else x_d[0, (ti - 1) * P:ti * P, :]
                sp.dma_start(xb[b][0:rows(ti), :], src).then_inc(s_xin[b], 16)
                if ti == 1:
                    for n, j in enumerate(WTILES[0:2]):
                        c0, w = cols(*j)
                        sp.dma_start(wbuf[n][:, :, 0:w],
                                     a["w_in"][0, :, c0:c0 + w].rearrange("(k p) c -> p k c", p=P)).then_inc(s_w[n], 16)
            for n, j in enumerate(WTILES[2:], 2):
                sp.wait_ge(s_job, J[WTILES[n - 2]] + 1)
                c0, w = cols(*j)
                sp.dma_start(wbuf[n % 2][:, :, 0:w],
                             a["w_in"][0, :, c0:c0 + w].rearrange("(k p) c -> p k c", p=P)).then_inc(s_w[n % 2], 16)
            for s in range(2):
                last = (NCH - 1 - s) // 2
                sp.wait_ge(CE[s].sem, CE[s].at(last, "YS"))
                sp.wait_ge(CA[s].sem, CA[s].at(last, "Y"))
            sp.wait_ge(CD[0].sem, CD[0].at((NCH - 1) // 2, "Q"))
            sp.wait_ge(CB[1].sem, CB[1].at((NCH - 1) // 2 - 1, "SB"))
            sp.wait_ge(s_yst, 16 * 4)
            sp.dma_start(wgu[:, 0, :], a["w_g_up"][0, 0:P, :]).then_inc(s_wgu, 16)
            sp.dma_start(wgu[0:32, 1, :], a["w_g_up"][0, P:GATE, :]).then_inc(s_wgu, 16)
            sp.dma_start(yl, ylru_dram.rearrange("(j p) t -> p j t", p=P)).then_inc(s_yl, 16)
            sp.dma_start(wo, a["w_out"][0].rearrange("(k p) n -> p k n", p=P)).then_inc(s_wo, 16)
            sp.wait_ge(GN_D.sem, GN_D.at(2 * PAIRS - 1, "g"))
            sp.dma_start(wr[:, :, 0:NG], a["w_router_grp"][0].rearrange("(k p) n -> p k n", p=P)).then_inc(s_wr, 16)
            sp.dma_start(wr[:, :, NG:NG + NE], a["w_router_exp"][0].rearrange("(k p) n -> p k n", p=P)).then_inc(s_wr, 16)
            sp.dma_start(br[:, 0:NG], a["b_router_grp"].to_broadcast([P, NG])).then_inc(s_wr, 16)
            sp.dma_start(br[:, NG:NG + NE], a["b_router_exp"].to_broadcast([P, NE])).then_inc(s_wr, 16)
            for b in range(2):
                sp.wait_ge(s_hst[b], 16 * 4)
            for ti in range(NT):
                b = ti % 2
                if ti >= 2:
                    sp.wait_ge(F_D.sem, F_D.at(ti - 2, "res1"))
                sp.dma_start(hb[b], h_dram[ti * P:(ti + 1) * P, :]).then_inc(s_hin[b], 16)

            def weights(n, e):
                srcs = (("w_exp_gate", KD), ("w_exp_up", KD), ("w_exp_down", KF))
                for k, (name, kk) in enumerate(srcs):
                    if first(n):
                        sp.wait_ge(*((F_O.sem, F_O.at(NT - 1, "o1")) if k < 2 else (F_D.sem, F_D.at(NT - 1, "xhat"))))
                    else:
                        sp.wait_ge(s_hi[k], n)
                        sp.wait_ge(s_lo[k], n)
                    sp.dma_start(raw[k], a[name][0, bass.ds(e, 1)].rearrange("o (p k) n -> p (o k) n", k=kk)).then_inc(s_we[k], 16)

            weights(0, 0)
            with sp.Fori(1, NE) as i:
                weights(i, i)
            n_over = sp.value_load(novi[0:1, 0:1], min_val=0, max_val=OVER)
            for j in range(OVER):
                with sp.If(n_over > j):
                    e = sp.value_load(oei[0:1, j:j + 1], min_val=0, max_val=NE - 1)
                    weights(NE + j, e)
            for s in range(2):
                sp.wait_ge(s_yo[s], 16 * (NE // 2))
            for ti in range(NT):
                b = ti % 2
                if ti >= 2:
                    sp.wait_ge(O_D.sem, O_D.at(ti - 2, "xhat"))
                sp.dma_start(hr[b], h1_dram[ti * P:(ti + 1) * P, :]).then_inc(s_hr[b], 16)
                if ti >= 1:
                    sp.wait_ge(O_P.sem, O_P.at(ti - 1, "bias"))
                    sp.dma_start(out[0, (ti - 1) * P:ti * P, :], o_x[1 - b]).then_inc(s_out[1 - b], 16)
            sp.wait_ge(O_P.sem, O_P.at(NT - 1, "bias"))
            sp.dma_start(out[0, (NT - 1) * P:NT * P, :], o_x[(NT - 1) % 2]).then_inc(s_out[(NT - 1) % 2], 16)
            for b in range(2):
                sp.wait_ge(s_out[b], 16 * (NT // 2))

        @block.gpsimd
        def _(pl):
            g = nc.gpsimd
            count = [0]

            def const(ins):
                count[0] += 1
                ins.then_inc(s_const, 1)
                pl.wait_ge(s_const, count[0])

            names = ["w0", "a0", "k_k", "k_a", None, "gn_g", "gn_b", "conv_b", "b_rg", "b_ig", "lru_lambda"]
            with nc.allow_non_contiguous_dma(reason="parameters to columns"):
                for n, name in enumerate(names):
                    src = a["r_k"].rearrange("o h n -> o (h n)") if name is None else a[name]
                    pl.dma_start(prm[:, n, :], src[0].rearrange("(j p) -> p j", p=P)).then_inc(s_prm, 16)
                pl.dma_start(cw, a["conv_w"][0].rearrange("w (j p) -> p w j", p=P)).then_inc(s_prm, 16)
                pl.dma_start(mu[:, 0:14], a["mu_shift"][0, 0:14 * P].rearrange("(j p) -> p j", p=P)).then_inc(s_prm, 16)
                pl.dma_start(mu[0:32, 14:15], a["mu_shift"][0, 14 * P:N_RWKV].rearrange("(p j) -> p j", j=1)).then_inc(s_prm, 16)
            pl.dma_start(wlr[0:64, :], a["w_decay_up"][0]).then_inc(s_prm, 16)
            pl.dma_start(wlr[64:128, :], a["w_a_up"][0]).then_inc(s_prm, 16)
            const(g.memset(ident, 0.0))
            const(g.affine_select(out=ident, in_=ident, compare_op=ALU.not_equal, fill=1.0, base=0,
                                  pattern=[[-1, P]], channel_multiplier=1))
            const(g.memset(eps[:, 0:1], LN_EPS))
            const(g.memset(eps[:, 1:2], GN_EPS))
            const(g.memset(VT[:, 0, 0:1024], 0.0))
            for dst, name in ((wrg, "w_rg"), (wig, "w_ig")):
                for h in range(2):
                    pl.dma_start(dst[h * HEAD:(h + 1) * HEAD, :, h * HEAD:(h + 1) * HEAD],
                                 a[name][0].rearrange("(j h) i c -> h i j c", h=2)[h]).then_inc(s_gate_w, 16)

            def masks():
                const(g.memset(ones, 1.0))
                const(g.affine_select(out=ltri, in_=ones, compare_op=ALU.is_gt, fill=0.0, base=0,
                                      pattern=[[1, P]], channel_multiplier=-1))
                const(g.memset(XL[:, 0:3], 0.0))
                const(g.memset(reset, 1.0))
                const(g.memset(reset[:, CH - Q0:CH - Q0 + CH * (NCH - 2) + 1:CH], 0.0))
                for m in (blk, m_strict, m_supT, ident2, m_sub):
                    const(g.memset(m, 0.0))
                for h in range(2):
                    rws = slice(h * HEAD, (h + 1) * HEAD)
                    const(g.memset(blk[rws, h, :], 1.0))
                    const(g.affine_select(out=m_incl[rws, :], in_=ones[rws, 0:HEAD], compare_op=ALU.is_ge, fill=0.0,
                                          base=0, pattern=[[1, HEAD]], channel_multiplier=-1))
                    const(g.affine_select(out=m_strict[rws, h, :], in_=ones[rws, 0:HEAD], compare_op=ALU.is_gt, fill=0.0,
                                          base=0, pattern=[[1, HEAD]], channel_multiplier=-1))
                    const(g.affine_select(out=ident2[rws, :], in_=ident2[rws, :], compare_op=ALU.not_equal, fill=1.0,
                                          base=0, pattern=[[-1, HEAD]], channel_multiplier=1))
                    odd = m_supT[rws, h, :].rearrange("p (a b) -> p a b", b=2)[:, :, 1]
                    const(g.affine_select(out=odd, in_=odd, compare_op=ALU.not_equal, fill=1.0,
                                          base=0, pattern=[[-2, HEAD // 2]], channel_multiplier=1))
                for l in LV:
                    w = 2 << l
                    n = HEAD // (2 * w)
                    for h in range(2):
                        rws = slice(h * HEAD, (h + 1) * HEAD)
                        even = m_sub[rws, l, h, :].rearrange("p (a b c) -> p a b c", b=2, c=w)[:, :, 0, :]
                        const(g.memset(even, 1.0))
                        const(g.affine_select(out=even, in_=even, compare_op=ALU.is_ge, fill=0.0, base=-w,
                                              pattern=[[-2 * w, n], [0, w]], channel_multiplier=1))
                        const(g.affine_select(out=even, in_=even, compare_op=ALU.is_ge, fill=0.0, base=2 * w - 1,
                                              pattern=[[2 * w, n], [0, w]], channel_multiplier=-1))
                g.memset(lamt[:, 4, :], 1.0 / 19).then_inc(s_const_done, 1)

            pl.wait_ge(s_lnp, 32)
            for ti in range(NT + 1):
                b, r = ti % 2, rows(ti)
                pl.wait_ge(s_ln.sem, s_ln.at(ti, "xhat"))
                g.tensor_tensor(xh[b][0:r, :], xh[b][0:r, :], lng[0:r, :], ALU.mult).then_inc(s_h.sem, 1)
                pl.wait_ge(s_h.sem, s_h.at(ti, "gain"))
                g.tensor_tensor(xh[b][0:r, :], xh[b][0:r, :], lnb[0:r, :], ALU.add).then_inc(s_h.sem, 1)
                if ti:
                    pl.wait_ge(s_h.sem, s_h.at(ti, "bias"))
                    pl.dma_start(h_dram[(ti - 1) * P:ti * P, :], xh[b]).then_inc(s_hst[b], 16)
            masks()
            pl.wait_ge(s_h.sem, s_h.at(NT, "bias"))
            pl.dma_start(lng, a["ln1_g"].to_broadcast([P, D])).then_inc(s_ln1, 16)
            pl.dma_start(lnb, a["ln1_b"].to_broadcast([P, D])).then_inc(s_ln1, 16)

            def lru_store(j):
                pl.wait_ge(LRU_D.sem, LRU_D.at(j, "y"))
                pl.dma_start(ylru_dram[j * P:(j + 1) * P, :], YL).then_inc(s_yst, 16)

            g.memset(YZ, 0.0).then_inc(s_yz, 1)
            pl.wait_ge(s_yz, 1)
            pl.dma_start(y_dram[NE * P:NBLK * P, :].rearrange("(b p) n -> p b n", p=P),
                         YZ.rearrange("p (o n) -> p o n", o=1).to_broadcast([P, OVER, D])).then_inc(s_yzd, 16)
            for j in range(3):
                lru_store(j)
            for n, (kind, j) in enumerate(SHIFTED):
                pl.wait_ge(s_uev, n + 1)
                r = cols(kind, j)[1]
                if (kind, j) == ("z", 2):
                    lru_store(3)
                if (kind, j) == ("r", 0):
                    pl.wait_ge(s_yst, 16 * 4)
                    pl.wait_ge(s_yzd, 16)
                    for arr in (AR[:, :, 0, 0:PAD], AR[:, :, 1, 0:PAD], BT[:, :, 0:PAD], KT[:, :, 0:PAD], VT[:, :, 0:PAD]):
                        g.memset(arr, 0.0).then_inc(s_z0, 1)
                dst = shifted(kind, j)
                g.tensor_tensor(dst, UB[0:r, n % 2, 0:TQ - 1], UB[0:r, n % 2, 1:TQ], ALU.subtract).then_inc(s_udif, 1)

            def blocks(dst, src):
                return g.tensor_tensor(dst, src.rearrange("p a (o c) -> p a o c", o=1).to_broadcast([P, PAIRS, 2, HEAD]),
                                       blk.rearrange("p (o h) c -> p o h c", o=1).to_broadcast([P, PAIRS, 2, HEAD]), ALU.mult)

            def prep(s, n, c):
                d = slot[s]
                if not first(n):
                    pl.wait_ge(CE[s].sem, CE[s].at(n - 1, "At"))
                for name, src in (("B", BT), ("K", KT), ("V", VT), ("A", AR[:, :, 0, :])):
                    blocks(d[name + "b"], src[:, :, bass.ds(c * CH, CH)]).then_inc(CP[s].sem, 1)

            pl.wait_ge(PR_D.sem, PR_D.at(PAIRS - 1, "at"))
            for m in (SB[0], slot[0]["Xb"], slot[0]["Zb"], slot[1]["Xb"], slot[1]["Zb"]):
                g.memset(m, 0.0).then_inc(s_z0, 1)

            def turn(slots_, n, c):
                for k, s in enumerate(slots_):
                    prep(s, n, c + k)

            turn((0, 1), 0, 0)
            with pl.Fori(1, (NCH - 1) // 2) as i:
                turn((0, 1), i, i * 2)
            turn((0,), (NCH - 1) // 2, NCH - 1)

            pl.wait_ge(GN_D.sem, GN_D.at(2 * PAIRS - 1, "g"))
            g.iota(i4, pattern=[[1, NE]], base=0, channel_multiplier=0, allow_small_or_imprecise_dtypes=True).then_inc(s_rtc, 1)
            g.iota(th7, pattern=[[P, 7]], base=P, channel_multiplier=0, allow_small_or_imprecise_dtypes=True).then_inc(s_rtc, 1)
            g.iota(j16, pattern=[[1, OVER]], base=0, channel_multiplier=0, allow_small_or_imprecise_dtypes=True).then_inc(s_rtc, 1)
            g.iota(tokid, pattern=[[P, NT]], base=0, channel_multiplier=1).then_inc(s_rtc, 1)
            g.memset(ztab, 0.0).then_inc(s_rtc, 1)
            pl.wait_ge(s_rtc, 5)
            pl.dma_start(tok_dram.rearrange("(p b) o -> p (b o)", p=P), ztab.bitcast(I32)).then_inc(s_zt, 16)
            pl.wait_ge(s_ln1, 32)
            for ti in range(NT):
                b = ti % 2
                pl.wait_ge(F_D.sem, F_D.at(ti, "xhat"))
                g.tensor_tensor(h1[b], h1[b], lng, ALU.mult).then_inc(F_P.sem, 1)
                pl.wait_ge(F_P.sem, F_P.at(ti, "gain"))
                g.tensor_tensor(h1[b], h1[b], lnb, ALU.add).then_inc(F_P.sem, 1)
                pl.wait_ge(F_P.sem, F_P.at(ti, "bias"))
                pl.dma_start(h1_dram[ti * P:(ti + 1) * P, :], h1[b]).then_inc(s_h1st[b], 16)
            pl.wait_ge(s_rt_done, 1)
            pl.wait_ge(s_zt, 16)
            for k in range(2):
                for ti in range(NT):
                    g.indirect_dma_start(out=tok_dram, out_offset=bass.IndirectOffsetOnAxis(ap=slots[:, k, ti:ti + 1], axis=0),
                                         in_=tokid[:, ti:ti + 1], in_offset=None).then_inc(s_sc, 16)
            pl.wait_ge(s_sc, 16 * 2 * NT)
            with nc.allow_non_contiguous_dma(reason="slot table to columns"):
                pl.dma_start(idx, tok_dram.rearrange("(b p) o -> p (b o)", p=P)).then_inc(s_idx, 16)
            pl.wait_ge(s_idx, 16)
            for b in range(2):
                pl.wait_ge(s_h1st[b], 16 * 4)

            def gather(s, n):
                if n >= 2:
                    pl.wait_ge(E_X, n - 1)
                g.indirect_dma_start(out=xg[s], out_offset=None, in_=h1_dram,
                                     in_offset=bass.IndirectOffsetOnAxis(ap=idx[:, n:n + 1], axis=0)).then_inc(s_xg[s], 16)

            def store(s, n):
                pl.wait_ge(V_Y, n + 1)
                pl.wait_ge(A_Y, n + 1)
                pl.dma_start(y_dram[n * P:(n + 1) * P, :], yb[s]).then_inc(s_yo[s], 16)

            for n in range(NE):
                gather(n % 2, n)
                if n == 2:
                    pl.dma_start(lng, a["ln2_g"].to_broadcast([P, D])).then_inc(s_ln2, 16)
                    pl.dma_start(lnb, a["ln2_b"].to_broadcast([P, D])).then_inc(s_ln2, 16)
                if n >= 3:
                    store((n - 3) % 2, n - 3)
            for n in range(NE - 3, NE):
                store(n % 2, n)
            n_over = pl.value_load(novi[0:1, 0:1], min_val=0, max_val=OVER)
            for j in range(OVER):
                with pl.If(n_over > j):
                    gather(j % 2, NE + j)
                    store(j % 2, NE + j)
            for s in range(2):
                pl.wait_ge(s_yo[s], 16 * (NE // 2))
            for j in range(OVER):
                with pl.If(n_over > j):
                    pl.wait_ge(s_yo[j % 2], 16 * (NE // 2 + j // 2 + 1))
            pl.wait_ge(s_ln2, 32)
            for ti in range(NT):
                b = ti % 2
                if ti >= 2:
                    pl.wait_ge(O_D.sem, O_D.at(ti - 2, "y2"))
                g.indirect_dma_start(out=y1[b], out_offset=None, in_=y_dram,
                                     in_offset=bass.IndirectOffsetOnAxis(ap=slots[:, 0, ti:ti + 1], axis=0)).then_inc(s_y1[b], 16)
                g.indirect_dma_start(out=y2[b], out_offset=None, in_=y_dram,
                                     in_offset=bass.IndirectOffsetOnAxis(ap=slots[:, 1, ti:ti + 1], axis=0)).then_inc(s_y2[b], 16)
                if ti >= 1:
                    finish(pl, g, ti - 1)
            finish(pl, g, NT - 1)

        @block.vector
        def _(dv):
            v = nc.vector

            def own(st, n, name, ins):
                ins.then_inc(st.sem, 1)
                dv.wait_ge(st.sem, st.at(n, name))

            v.memset(hT[:, :, 0:1], 0.0).then_inc(s_zcol, 1)
            setup = [0]

            def once(ins):
                setup[0] += 1
                ins.then_inc(s_setup, 1)
                dv.wait_ge(s_setup, setup[0])

            for ti in range(NT + 1):
                b, r = ti % 2, rows(ti)
                dv.wait_ge(s_xin[b], 16 * (ti // 2 + 1))
                for hf in range(2):
                    own(s_ln, ti, f"st{hf}", v.bn_stats(out=st6[0:r, hf, :], in_=xb[b][0:r, hf * 512:(hf + 1) * 512]))
                v.bn_aggr(out=mv[0:r, :], in_=st6[0:r, :, :].rearrange("p a b -> p (a b)")).then_inc(s_ln.sem, 1)
                dv.wait_ge(s_std, ti + 1)
                own(s_ln, ti, "rstd", v.reciprocal(rstd[0:r, 1:2], rstd[0:r, 0:1]))
                if ti >= 2:
                    dv.wait_ge(s_tp, 2 * (ti - 1))
                    if ti >= 3:
                        dv.wait_ge(s_hst[b], 16 * ((ti - 1) // 2))
                own(s_ln, ti, "xhat", v.tensor_scalar(xh[b][0:r, :], xb[b][0:r, :], mv[0:r, 0:1], rstd[0:r, 1:2],
                                                      ALU.subtract, ALU.mult))

            dv.wait_ge(s_tp, 2 * (NT + 1))
            for b in range(2):
                dv.wait_ge(s_hst[b], 16 * (NT // 2))
            v.memset(Z0[:, 0:1], 0.0).then_inc(s_zcol, 1)
            dv.wait_ge(s_prm, 16 * 15)
            dv.wait_ge(s_const_done, 1)
            for q, n in enumerate((P_W0, P_A0, P_BR, P_BI)):
                once(v.tensor_scalar(hprm[:, q, :], prm[:, n, :], 0.5, None, ALU.mult))
            once(v.tensor_scalar(prm[:, P_K1, :], prm[:, P_KA, :], -1.0, 1.0, ALU.mult, ALU.add))
            once(v.tensor_scalar(lamt[:, 0, :], prm[:, P_LAM, :], -1.0, None, ALU.mult))
            once(v.tensor_tensor(lamt[:, 0, :], lamt[:, 0, :], prm[:, P_LAM, :], ALU.min))
            v.tensor_scalar(lamt[:, 5, :], prm[:, P_LAM, :], 0.0, None, ALU.min).then_inc(s_absl, 1)
            dv.wait_ge(s_absl, 1)
            dv.wait_ge(s_expl, 1)
            once(v.tensor_scalar(lamt[:, 2, :], lamt[:, 1, :], 2.0, None, ALU.add))
            once(v.reciprocal(lamt[:, 3, :], lamt[:, 2, :]))
            once(v.tensor_tensor(lamt[:, 2, :], lamt[:, 1, :], lamt[:, 3, :], ALU.mult))
            once(v.tensor_tensor(lamt[:, 3, :], lamt[:, 2, :], lamt[:, 2, :], ALU.mult))
            for q in range(8, -1, -1):
                once(v.tensor_tensor(lamt[:, 4, :], lamt[:, 4, :], lamt[:, 3, :], ALU.mult))
                once(v.tensor_scalar(lamt[:, 4, :], lamt[:, 4, :], 1.0 / (2 * q + 1), None, ALU.add))
            once(v.tensor_tensor(lamt[:, 4, :], lamt[:, 4, :], lamt[:, 2, :], ALU.mult))
            once(v.tensor_scalar(lamt[:, 4, :], lamt[:, 4, :], -2.0, None, ALU.mult))
            once(v.tensor_tensor(lamt[:, 4, :], lamt[:, 4, :], lamt[:, 5, :], ALU.add))
            once(v.tensor_scalar(c8[:, 0, :], lamt[:, 4, :], 8.0, None, ALU.mult))
            v.tensor_scalar(c8[:, 1, :], lamt[:, 4, :], -8.0, None, ALU.mult).then_inc(s_c8, 1)

            def conv(j):
                dv.wait_ge(s_lx, j + 1)
                own(LRU_D, j, "c0", v.tensor_scalar(XC, XL[:, 0:TQ], cw[:, 0, j:j + 1], prm[:, P_CB, j:j + 1], ALU.mult, ALU.add))
                for w in range(1, 4):
                    own(LRU_D, j, f"c{w}", v.scalar_tensor_tensor(out=XC, in0=XL[:, w:w + TQ], scalar=cw[:, w, j:j + 1], in1=XC,
                                                                  op0=ALU.mult, op1=ALU.add))

            def lru(j):
                dv.wait_ge(LRU_A.sem, LRU_A.at(j, "gr"))
                own(LRU_D, j, "gr", v.tensor_scalar(GR, GR, 0.5, 0.5, ALU.mult, ALU.add))
                dv.wait_ge(LRU_A.sem, LRU_A.at(j, "gs"))
                own(LRU_D, j, "d1", v.tensor_scalar(LD, GS, 1.0, None, ALU.add))
                own(LRU_D, j, "rec", v.reciprocal(LD, LD))
                own(LRU_D, j, "m2", v.scalar_tensor_tensor(out=GS, in0=GS, scalar=2.0, in1=LD, op0=ALU.mult, op1=ALU.mult))
                own(LRU_D, j, "gi", v.tensor_scalar(GI, GI, 0.5, 0.5, ALU.mult, ALU.add))
                own(LRU_D, j, "ga", v.tensor_tensor(GI, GI, XC, ALU.mult))
                dv.wait_ge(LRU_A.sem, LRU_A.at(j, "sq"))
                own(LRU_D, j, "gb", v.tensor_tensor(GI, GI, GS, ALU.mult))
                own(LRU_D, j, "scan", v.tensor_tensor_scan(out=LD[:, 1:TQ], data0=LA[:, 1:TQ], data1=GI[:, 1:TQ], initial=0.0,
                                                           op0=ALU.mult, op1=ALU.add))
                if j:
                    dv.wait_ge(s_yst, 16 * j)
                own(LRU_D, j, "y", v.tensor_tensor(YL, LD[:, XQ:TQ], GG[:, j, 64:TP], ALU.mult))

            nsh = [0]

            def shift(kind, j):
                n = nsh[0]
                nsh[0] += 1
                r = cols(kind, j)[1]
                q = {"r": j, "k": 4 + j, "v": 8 + j, "z": 12 + j}[kind]
                dv.wait_ge(s_udif, n + 1)
                dst = shifted(kind, j)
                v.scalar_tensor_tensor(out=dst, in0=dst, scalar=mu[0:r, q:q + 1], in1=UB[0:r, n % 2, 1:TQ],
                                       op0=ALU.mult, op1=ALU.add).then_inc(s_ush, 1)
                dv.wait_ge(s_ush, n + 1)

            def pair(p, part):
                jb = J
                kt = KT[:, p, Q0:TP]
                if part == 0:
                    dv.wait_ge(PR_A.sem, PR_A.at(p, "sg"))
                    own(PR_D, p, "sg", v.tensor_scalar(SG, SG, 0.5, 0.5, ALU.mult, ALU.add))
                    own(PR_D, p, "cs", v.tensor_tensor_scan(out=CS, data0=reset, data1=SG, initial=0.0, op0=ALU.mult, op1=ALU.add))
                    own(PR_D, p, "csx", v.tensor_tensor(SG, CS, SG, ALU.subtract))
                    dv.wait_ge(PR_A.sem, PR_A.at(p, "a"))
                    own(PR_D, p, "a", v.tensor_scalar(AA, AA, 0.5, 0.5, ALU.mult, ALU.add))
                    dv.wait_ge(s_z0, 5)
                    own(PR_D, p, "kk", v.tensor_scalar(KK, kt, prm[:, P_KK, p:p + 1], None, ALU.mult))
                if part == 1:
                    dv.wait_ge(s_job, jb[("ss", p)] + 1)
                    own(PR_D, p, "ssm", v.tensor_scalar(seg3(T7), bank(("ss", p)), 1e-24, None, ALU.max))
                    dv.wait_ge(PR_A.sem, PR_A.at(p, "rt"))
                    own(PR_D, p, "rec", v.reciprocal(T7, T7))
                    own(PR_D, p, "kkn", v.tensor_tensor(KK, KK, T7, ALU.mult))
                    own(PR_D, p, "kc", v.tensor_scalar(T7, AA, prm[:, P_KA, p:p + 1], prm[:, P_K1, p:p + 1], ALU.mult, ALU.add))
                    own(PR_D, p, "k2", v.tensor_tensor(kt, kt, T7, ALU.mult))
                    own(PR_D, p, "q", v.scalar_tensor_tensor(out=T7, in0=AR[:, p, 1, Q0:TP], scalar=prm[:, P_RK, p:p + 1], in1=kt,
                                                             op0=ALU.mult, op1=ALU.mult))
                if part == 2:
                    dv.wait_ge(s_job, jb[("bon", p)] + 1)
                    own(PR_D, p, "bon", v.tensor_tensor(seg3(BON[:, p, :]), bank(("bon", p)), seg3(VT[:, p, Q0:TP]), ALU.mult))
                    own(PR_D, p, "b0", v.tensor_tensor(AA, AA, KK, ALU.mult))
                    dv.wait_ge(PR_A.sem, PR_A.at(p, "iw"))
                    own(PR_D, p, "b", v.tensor_tensor(BT[:, p, Q0:TP], AA, E1, ALU.mult))
                    own(PR_D, p, "k", v.tensor_tensor(kt, kt, E1, ALU.mult))
                    dv.wait_ge(PR_A.sem, PR_A.at(p, "w"))
                    own(PR_D, p, "r", v.tensor_tensor(AR[:, p, 1, Q0:TP], AR[:, p, 1, Q0:TP], E1, ALU.mult))
                    dv.wait_ge(PR_A.sem, PR_A.at(p, "wx"))
                    own(PR_D, p, "at", v.scalar_tensor_tensor(out=AR[:, p, 0, Q0:TP], in0=KK, scalar=-1.0, in1=SG,
                                                              op0=ALU.mult, op1=ALU.mult))
            for job in JOBS:
                kind, j = job
                if kind == "lx" and j == 0:
                    conv(0)
                if kind == "gi":
                    lru(j)
                    if j < 3:
                        conv(j + 1)
                if kind in ("r", "k", "v", "z"):
                    shift(kind, j)
                    if job == ("z", 2):
                        for q, r in ((0, P), (1, 32)):
                            dv.wait_ge(s_zact, 2 + q)
                            v.tensor_scalar(ZG[0:r, q, :], ZG[0:r, q, :], 0.5, 0.5, ALU.mult, ALU.add).then_inc(s_zg, 1)
                if kind == "aa":
                    pair(j, 0)
                if kind == "ss":
                    pair(j, 1)
                if kind == "bon":
                    pair(j, 2)

            def masked(out_, in_, mask):
                return v.tensor_tensor(out_, in_, mask, ALU.mult)

            def pb(b0, lo, hi):
                return ps[:, b0, lo:hi]

            def st(m):
                return m.rearrange("p (o c) -> p o c", o=1).to_broadcast([P, PAIRS, HEAD])

            def bd(m):
                return m.rearrange("p (o h) c -> p o h c", o=1).to_broadcast([P, PAIRS, 2, HEAD])

            def dup(x4):
                return x4.rearrange("p a (o c) -> p a o c", o=1).to_broadcast([P, PAIRS, 2, HEAD])

            def quad(b0):
                return ps[:, b0, 0:512].rearrange("p (a h c) -> p a h c", h=2, c=HEAD)

            def solve_start(s, n):
                d, B, cd = slot[s], 4 * s, CD[s]
                dv.wait_ge(CM[s].sem, CM[s].at(n, "MB"))
                own(cd, n, "T0a", masked(d["Tb"], dup(quad(B)[:, :, 0, :]), bd(m_supT)))
                own(cd, n, "T0", v.tensor_tensor(d["Tb"], d["Tb"], bd(ident.rearrange("p (h c) -> p h c", c=HEAD)), ALU.add))
                own(cd, n, "Mb", masked(d["Mb"], dup(quad(B)[:, :, 0, :]), bd(m_strict)))
                own(cd, n, "Mr", masked(d["RB"][:, :, 0, :], quad(B)[:, :, 1, :], st(m_incl)))

            def k_masks(s, n):
                d, B, cd = slot[s], 4 * s, CD[s]
                dv.wait_ge(CM[s].sem, CM[s].at(n, "MK"))
                own(cd, n, "Nb", masked(d["Nb"], dup(quad(B + 1)[:, :, 0, :]), bd(m_strict)))
                own(cd, n, "Mk", masked(d["RK"][:, :, 0, :], quad(B + 1)[:, :, 1, :], st(m_incl)))

            def level_p(s, n, l):
                d, B, cd = slot[s], 4 * s, CD[s]
                dv.wait_ge(CE[s].sem, CE[s].at(n, f"P{l}"))
                own(cd, n, f"P{l}", masked(d["Pb"], quad(B), bd(m_sub[:, l, :, :])))

            def level_d(s, n, l):
                d, B, cd = slot[s], 4 * s, CD[s]
                if l < LV[-1]:
                    dv.wait_ge(CE[s].sem, CE[s].at(n, f"DP{l}"))
                    own(cd, n, f"D{l + 1}", v.tensor_tensor(d["Db"], d["Db"], quad(B + 1), ALU.add))
                else:
                    dv.wait_ge(CE[s].sem, CE[s].at(n, "PD"))
                    own(cd, n, f"T{l + 1}", v.tensor_tensor(d["Tb"], d["Tb"], quad(B + 1), ALU.add))

            def through(s, n, c):
                d, B, cd = slot[s], 4 * s, CD[s]
                dv.wait_ge(CE[s].sem, CE[s].at(n, "QG"))
                own(cd, n, "G", v.tensor_tensor(d["QG"][:, :, 1, :], quad(B + 1)[:, :, 1, :], st(ident2), ALU.add))
                own(cd, n, "Q", v.tensor_tensor(d["QG"][:, :, 0, :], quad(B + 1)[:, :, 0, :],
                                                AR[:, :, 1, bass.ds(c * CH, CH)], ALU.add))

            def state_t(s, n):
                dv.wait_ge(CE[s].sem, CE[s].at(n, "YS"))
                own(CD[s], n, "S", masked(slot[s]["Sb"], dup(quad(4 * s + 3)[:, :, 1, :]), bd(blk)))

            def state(s, n, c):
                dv.wait_ge(CE[s].sem, CE[s].at(n, "St"))
                own(CB[s], n, "SB", v.tensor_tensor(
                    SB[1 - s].rearrange("p a h c -> p a (h c)"), ps[:, 4 * s + 2, :].rearrange("p (a x) -> p a x", a=PAIRS),
                    wc[:, :, bass.ds(c, 1)].to_broadcast([P, PAIRS, P]), ALU.mult))

            def turn(slots_, n, c):
                if 1 in slots_:
                    solve_start(1, n)
                if not first(n):
                    state(1, n - 1, c - 1)
                if 1 in slots_:
                    k_masks(1, n)
                for l in LV:
                    for s in slots_:
                        level_p(s, n, l)
                    for s in slots_:
                        level_d(s, n, l)
                for k, s in enumerate(slots_):
                    through(s, n, c + k)
                if 1 in slots_:
                    state_t(0, n)
                    state(0, n, c)
                    solve_start(0, n + 1)
                    k_masks(0, n + 1)
                    state_t(1, n)

            solve_start(0, 0)
            k_masks(0, 0)
            turn((0, 1), 0, 0)
            with dv.Fori(1, (NCH - 1) // 2) as i:
                turn((0, 1), i, i * 2)
            turn((0,), (NCH - 1) // 2, NCH - 1)

            dv.wait_ge(CA[0].sem, CA[0].at((NCH - 1) // 2, "Y"))
            dv.wait_ge(CA[1].sem, CA[1].at((NCH - 1) // 2 - 1, "Y"))
            for n in range(2 * PAIRS):
                p, hf = n // 2, n % 2
                y = AR[:, p, 1, CH + hf * 512:CH + hf * 512 + 512]
                sd = gsd[n % 2]
                B = 4 * (n % 2)
                dv.wait_ge(GN_E.sem, GN_E.at(n, "mean"))
                own(GN_D, n, "c", v.scalar_tensor_tensor(out=y, in0=ps[:, B, :], scalar=-1.0 / HEAD, in1=y,
                                                         op0=ALU.mult, op1=ALU.add))
                dv.wait_ge(GN_A.sem, GN_A.at(n, "sd"))
                own(GN_D, n, "rec", v.reciprocal(sd, sd))
                own(GN_D, n, "n", v.tensor_tensor(y, y, sd, ALU.mult))
                own(GN_D, n, "aff", v.tensor_scalar(y, y, prm[:, P_GG, p:p + 1], prm[:, P_GB, p:p + 1], ALU.mult, ALU.add))
                own(GN_D, n, "bon", v.tensor_tensor(y, y, BON[:, p, XQ + hf * 512:XQ + hf * 512 + 512], ALU.add))
                dv.wait_ge(GN_E.sem, GN_E.at(n, "g"))
                own(GN_D, n, "g", v.tensor_tensor(y, y, ps[:, B + 2, :], ALU.mult))

            rt = [0]

            def r_(ins):
                rt[0] += 1
                ins.then_inc(s_rt, 1)
                dv.wait_ge(s_rt, rt[0])

            def route(ti):
                dv.wait_ge(F_E.sem, F_E.at(ti, "lg"))
                v.tensor_tensor(lg[:, ti, :], ps[:, 6, 0:NG + NE], br, ALU.add).then_inc(F_L, 1)
                dv.wait_ge(F_L, ti + 1)
                r_(v.tensor_copy(g8[:, 0:NG], lg[:, ti, 0:NG]))
                r_(v.max(gm8, g8))
                r_(v.max_index(gi8, gm8, g8))
                r_(v.tensor_copy(gi8f, gi8))
                r_(v.tensor_scalar(ohg, i4[:, 0:NG], gi8f[:, 0:1], None, ALU.is_equal))
                r_(v.tensor_tensor(esel, lg[:, ti, NG:NG + NE].rearrange("p (g e) -> p g e", e=EPG),
                                   ohg.rearrange("p (g o) -> p g o", o=1).to_broadcast([P, NG, EPG]), ALU.mult))
                r_(v.tensor_tensor(e8, esel[:, 0, :], esel[:, 1, :], ALU.add))
                r_(v.tensor_tensor(e8, e8, esel[:, 2, :], ALU.add))
                r_(v.tensor_tensor(e8, e8, esel[:, 3, :], ALU.add))
                r_(v.max(tm8, e8))
                r_(v.max_index(ti8, tm8, e8))
                r_(v.tensor_copy(ti8f, ti8))
                r_(v.tensor_scalar(sm[:, 0:1], gi8f[:, 0:1], float(EPG), None, ALU.mult))
                for k in range(2):
                    r_(v.tensor_tensor(eidf[:, k, ti:ti + 1], sm[:, 0:1], ti8f[:, k:k + 1], ALU.add))
                    r_(v.tensor_scalar(OH[k][:, ti, :], i4, eidf[:, k, ti:ti + 1], None, ALU.is_equal))
                r_(v.tensor_scalar(lg[:, ti, 0:NG], lg[:, ti, 0:NG], gm8[:, 0:1], None, ALU.subtract))
                arg = v.tensor_tensor(lg[:, ti, NG:NG + 1], tm8[:, 1:2], tm8[:, 0:1], ALU.subtract)
                if ti < NT - 1:
                    r_(arg)
                else:
                    arg.then_inc(s_rt_arg, 1)

            dv.wait_ge(s_rtc, 5)
            r_(v.memset(g8, -3.0e38))
            for ti in range(NT):
                b = ti % 2
                dv.wait_ge(s_hin[b], 16 * (ti // 2 + 1))
                for hf in range(2):
                    dv.wait_ge(F_O.sem, F_O.at(ti, f"o{hf}"))
                    cs = slice(hf * 512, (hf + 1) * 512)
                    own(F_D, ti, f"res{hf}", v.scalar_tensor_tensor(out=zb[b][:, cs], in0=hb[b][:, cs], scalar=ALPHA,
                                                                    in1=ps[:, 2 * b + hf, :], op0=ALU.mult, op1=ALU.add))
                for hf in range(2):
                    own(F_D, ti, f"st{hf}", v.bn_stats(out=st6[:, hf, :], in_=zb[b][:, hf * 512:(hf + 1) * 512]))
                v.bn_aggr(out=mv, in_=st6.rearrange("p a b -> p (a b)")).then_inc(F_D.sem, 1)
                dv.wait_ge(F_A, ti + 1)
                own(F_D, ti, "rstd", v.reciprocal(rstd[:, 1:2], rstd[:, 0:1]))
                if ti >= 2:
                    dv.wait_ge(s_h1st[b], 16 * (ti // 2))
                    dv.wait_ge(F_E.sem, F_E.at(ti - 2, "t1"))
                own(F_D, ti, "xhat", v.tensor_scalar(h1[b], zb[b], mv[:, 0:1], rstd[:, 1:2], ALU.subtract, ALU.mult))
                if ti:
                    route(ti - 1)
            route(NT - 1)


            r_(v.tensor_tensor(OS, OH[0], OH[1], ALU.add))
            r_(v.memset(OP[:, 0, :], 0.0))
            for ti in range(NT - 1):
                r_(v.tensor_tensor(OP[:, ti + 1, :], OP[:, ti, :], OS[:, ti, :], ALU.add))
            v.tensor_tensor(OP[:, NT, :], OP[:, NT - 1, :], OS[:, NT - 1, :], ALU.add).then_inc(s_rt_oh, 1)
            dv.wait_ge(s_rta, 1)
            r_(v.reduce_sum(s1t[:, 0, :], lg[:, :, 0:NG], axis=AXX))
            r_(v.tensor_scalar(s1t[:, 1, :], lg[:, :, NG], 1.0, None, ALU.add))
            r_(v.tensor_tensor(s1t[:, 0, :], s1t[:, 0, :], s1t[:, 1, :], ALU.mult))
            r_(v.reciprocal(gates[:, 0, :], s1t[:, 0, :]))
            r_(v.tensor_tensor(gates[:, 1, :], gates[:, 0, :], lg[:, :, NG], ALU.mult))
            dv.wait_ge(s_rte, 1)
            r_(v.tensor_copy(RK.rearrange("p a b -> p (a b)"), ps[:, 0, 0:NT * NE]))
            r_(v.tensor_copy(cnt, ps[:, 1, 0:NE]))
            r_(v.tensor_tensor(c7, cnt.rearrange("p (e o) -> p e o", o=1).to_broadcast([P, NE, 7]),
                               th7.rearrange("p (o m) -> p o m", o=1).to_broadcast([P, NE, 7]), ALU.is_gt))
            r_(v.reduce_sum(ovb, c7, axis=AXX))
            r_(v.tensor_tensor_scan(out=ovi, data0=ones[:, 0:NE], data1=ovb, initial=0.0, op0=ALU.mult, op1=ALU.add))
            r_(v.tensor_tensor(ove, ovi, ovb, ALU.subtract))
            for k in range(2):
                r_(v.tensor_tensor(t32, OH[k], RK, ALU.mult))
                r_(v.reduce_sum(rk[:, k, :], t32, axis=AXX))
                r_(v.tensor_tensor(t32, OH[k], ove.rearrange("p (o e) -> p o e", o=1).to_broadcast([P, NT, NE]), ALU.mult))
                r_(v.reduce_sum(ovs[:, k, :], t32, axis=AXX))
            rkf, qf = rk.rearrange("p k t -> p (k t)"), qk.rearrange("p k t -> p (k t)")
            ovf, ef = ovs.rearrange("p k t -> p (k t)"), eidf.rearrange("p k t -> p (k t)")
            r_(v.tensor_tensor(q7, rkf.rearrange("p (n o) -> p n o", o=1).to_broadcast([P, 2 * NT, 7]),
                               th7.rearrange("p (o m) -> p o m", o=1).to_broadcast([P, 2 * NT, 7]), ALU.is_ge))
            r_(v.reduce_sum(qf, q7, axis=AXX))
            r_(v.tensor_tensor(ovf, ovf, qf, ALU.add))
            r_(v.tensor_scalar(ovf, ovf, float(NE - 1), None, ALU.add))
            r_(v.tensor_tensor(ovf, ovf, ef, ALU.subtract))
            s1f = s1t.rearrange("p k t -> p (k t)")
            r_(v.tensor_scalar(s1f, qf, 0.0, None, ALU.is_gt))
            r_(v.tensor_tensor(ovf, ovf, s1f, ALU.mult))
            r_(v.tensor_tensor(ovf, ovf, ef, ALU.add))
            r_(v.tensor_tensor(ovf, ovf, qf, ALU.subtract))
            r_(v.scalar_tensor_tensor(out=ovf, in0=ovf, scalar=float(P), in1=rkf, op0=ALU.mult, op1=ALU.add))
            r_(v.tensor_copy(slots.rearrange("p k t -> p (k t)"), ovf))
            r_(v.tensor_tensor(o16, ovi.rearrange("p (o e) -> p o e", o=1).to_broadcast([P, OVER, NE]),
                               j16.rearrange("p (j o) -> p j o", o=1).to_broadcast([P, OVER, NE]), ALU.is_le))
            r_(v.reduce_sum(oef, o16, axis=AXX))
            r_(v.tensor_scalar(oef, oef, float(NE - 1), None, ALU.min))
            r_(v.tensor_copy(oei, oef))
            v.tensor_copy(novi, ovi[:, NE - 1:NE]).then_inc(s_rt_done, 1)

            def rest(s, n, k):
                dv.wait_ge(s_hi[k], n + 1)
                v.tensor_tensor(wsp[s][k][1], raw[k], wsp[s][k][0], ALU.subtract).then_inc(s_lo[k], 1)

            def rows_in(s, n):
                dv.wait_ge(A_X, n + 1)
                v.tensor_tensor(xT[s][1], ps[:, 0:2, :].rearrange("p b (k c) -> p (b k) c", c=P), xT[s][0],
                                ALU.subtract).then_inc(V_X, 1)

            def product(s, n):
                dv.wait_ge(A_S, n + 1)
                dv.wait_ge(E_U, n + 1)
                v.tensor_tensor(hd[s], hs[s], ps[:, 3, :], ALU.mult).then_inc(V_M, 1)

            def hidden(s, n):
                dv.wait_ge(A_H, n + 1)
                v.tensor_tensor(hTe[s][1], ps[:, 4, :].rearrange("p (k c) -> p k c", c=P), hTe[s][0],
                                ALU.subtract).then_inc(V_H, 1)

            def yout(s, n):
                dv.wait_ge(E_Y, n + 1)
                if not (isinstance(n, int) and n < 2):
                    dv.wait_ge(s_yo[s], (n - s) * 8)
                v.tensor_copy(yb[s][:, 512:1024], ps[:, 6, :]).then_inc(V_Y, 1)

            def turn(s, n, more=True):
                if more:
                    rest(1 - s, n + 1, 0)
                if not first(n):
                    hidden(1 - s, n - 1)
                if more:
                    rows_in(1 - s, n + 1)
                    rest(1 - s, n + 1, 1)
                product(s, n)
                if more:
                    rest(1 - s, n + 1, 2)
                if not first(n):
                    yout(1 - s, n - 1)

            for k in range(3):
                rest(0, 0, k)
            rows_in(0, 0)
            turn(0, 0)
            turn(1, 1)
            with dv.Fori(1, NE // 2 - 1) as i:
                turn(0, i * 2)
                turn(1, i * 2 + 1)
            turn(0, NE - 2)
            turn(1, NE - 1, False)
            hidden(1, NE - 1)
            yout(1, NE - 1)
            n_over = dv.value_load(novi[0:1, 0:1], min_val=0, max_val=OVER)
            for j in range(OVER):
                with dv.If(n_over > j):
                    s, n = j % 2, NE + j
                    rows_in(s, n)
                    for k in range(3):
                        rest(s, n, k)
                    product(s, n)
                    hidden(s, n)
                    yout(s, n)

            for ti in range(NT):
                b = ti % 2
                dv.wait_ge(s_y1[b], 16 * (ti // 2 + 1))
                dv.wait_ge(s_hr[b], 16 * (ti // 2 + 1))
                own(O_D, ti, "y1", v.tensor_scalar(y1[b], y1[b], gates[:, 0, ti:ti + 1], None, ALU.mult))
                dv.wait_ge(s_y2[b], 16 * (ti // 2 + 1))
                own(O_D, ti, "y2", v.scalar_tensor_tensor(out=y1[b], in0=y2[b], scalar=gates[:, 1, ti:ti + 1], in1=y1[b],
                                                          op0=ALU.mult, op1=ALU.add))
                own(O_D, ti, "res", v.scalar_tensor_tensor(out=hr[b], in0=hr[b], scalar=ALPHA, in1=y1[b], op0=ALU.mult, op1=ALU.add))
                for hf in range(2):
                    own(O_D, ti, f"st{hf}", v.bn_stats(out=st6[:, hf, :], in_=hr[b][:, hf * 512:(hf + 1) * 512]))
                v.bn_aggr(out=mv, in_=st6.rearrange("p a b -> p (a b)")).then_inc(O_D.sem, 1)
                dv.wait_ge(O_A, ti + 1)
                own(O_D, ti, "rstd", v.reciprocal(rstd[:, 1:2], rstd[:, 0:1]))
                if ti >= 2:
                    dv.wait_ge(s_out[b], 16 * (ti // 2))
                own(O_D, ti, "xhat", v.tensor_scalar(o_x[b], hr[b], mv[:, 0:1], rstd[:, 1:2], ALU.subtract, ALU.mult))

        @block.scalar
        def _(ac):
            f = nc.scalar.activation

            def copy_t(ti):
                r = rows(ti)
                c0 = 1 if ti == 0 else XQ + (ti - 1) * P
                for hf in range(2):
                    ac.wait_ge(s_tp, 2 * ti + hf + 1)
                    f(hT[:, 4 * hf:4 * hf + 4, c0:c0 + r],
                      ps[:, 2 * (ti % 2) + hf, :].rearrange("p (k c) -> p k c", c=P)[:, :, 0:r], ACT.Copy).then_inc(s_ht, 1)

            for ti in range(NT + 1):
                r = rows(ti)
                ac.wait_ge(s_ln.sem, s_ln.at(ti, "agg"))
                if ti == 0:
                    ac.wait_ge(s_const, 4)
                f(rstd[0:r, 0:1], mv[0:r, 1:2], ACT.Sqrt, bias=eps[0:r, 0:1]).then_inc(s_std, 1)
                if ti:
                    copy_t(ti - 1)
            copy_t(NT)
            ac.wait_ge(s_absl, 1)
            f(lamt[:, 1, :], lamt[:, 0, :], ACT.Exp).then_inc(s_expl, 1)

            nsh = [0]
            for job in JOBS:
                kind, j = job
                if kind in ("ss", "bon"):
                    continue
                ac.wait_ge(s_job, J[job] + 1)
                if kind == "gl":
                    f(seg3(GG[:, j, Q0:TP]), bank(job), ACT.Gelu_apprx_tanh).then_inc(s_gelu, 1)
                if kind == "lx":
                    if j == 0:
                        ac.wait_ge(s_const_done, 1)
                    if j:
                        ac.wait_ge(LRU_D.sem, LRU_D.at(j - 1, "c3"))
                    f(seg3(XL[:, 3:3 + TQ]), bank(job), ACT.Copy).then_inc(s_lx, 1)
                if kind == "gr":
                    if j:
                        ac.wait_ge(LRU_D.sem, LRU_D.at(j - 1, "scan"))
                    f(seg3(GR), bank(job), ACT.Tanh, bias=hprm[:, 2, j:j + 1], scale=0.5).then_inc(LRU_A.sem, 1)
                if kind == "gi":
                    f(seg3(GI), bank(job), ACT.Tanh, bias=hprm[:, 3, j:j + 1], scale=0.5).then_inc(LRU_A.sem, 1)
                    ac.wait_ge(LRU_D.sem, LRU_D.at(j, "gr"))
                    ac.wait_ge(s_c8, 1)
                    f(LA, GR, ACT.Exp, scale=c8[:, 0, j:j + 1]).then_inc(LRU_A.sem, 1)
                    f(GS, GR, ACT.Tanh, scale=c8[:, 1, j:j + 1]).then_inc(LRU_A.sem, 1)
                    ac.wait_ge(LRU_D.sem, LRU_D.at(j, "m2"))
                    f(GS, GS, ACT.Sqrt).then_inc(LRU_A.sem, 1)
                if kind in ("z", "r", "k", "v"):
                    n = nsh[0]
                    nsh[0] += 1
                    r = cols(kind, j)[1]
                    if n >= 2:
                        ac.wait_ge(s_ush, n - 1)
                    f(seg3(UB[0:r, n % 2, :]), bank(job, r), ACT.Copy).then_inc(s_uev, 1)
                    if kind == "z":
                        ac.wait_ge(s_ush, n + 1)
                        if j == 0:
                            ac.wait_ge(s_zcol, 2)
                            f(Z0[0:64, :], Z0[0:64, :], ACT.Tanh).then_inc(s_zact, 1)
                        if j == 1:
                            f(ZG[:, 0, :], ZG0[:, XQ:TQ], ACT.Tanh, scale=0.5).then_inc(s_zact, 1)
                        if j == 2:
                            f(ZG[0:32, 1, :], XC[0:32, XQ:TQ], ACT.Tanh, scale=0.5).then_inc(s_zact, 1)
                if kind == "dec":
                    if j:
                        ac.wait_ge(PR_D.sem, PR_D.at(j - 1, "at"))
                    f(seg3(SG), bank(job), ACT.Tanh, bias=hprm[:, 0, j:j + 1], scale=0.5).then_inc(PR_A.sem, 1)
                if kind == "aa":
                    f(seg3(AA), bank(job), ACT.Tanh, bias=hprm[:, 1, j:j + 1], scale=0.5).then_inc(PR_A.sem, 1)
                    ac.wait_ge(PR_D.sem, PR_D.at(j, "kk"))
                    f(T7, KK, ACT.Square).then_inc(PR_A.sem, 1)
                    f(E1, CS, ACT.Exp, scale=DECAY).then_inc(PR_A.sem, 1)
                nxt = JOBS[J[job] + 1] if J[job] + 1 < len(JOBS) else None
                while nxt and nxt[0] in ("ss", "bon"):
                    p = nxt[1]
                    if nxt[0] == "ss":
                        ac.wait_ge(PR_D.sem, PR_D.at(p, "ssm"))
                        f(T7, T7, ACT.Sqrt).then_inc(PR_A.sem, 1)
                    else:
                        f(wc[:, p, :], CS[:, HEAD - 1 - Q0:TQ:CH], ACT.Exp, scale=-DECAY).then_inc(PR_A.sem, 1)
                        f(SG, SG, ACT.Exp, scale=-DECAY).then_inc(PR_A.sem, 1)
                        ac.wait_ge(PR_D.sem, PR_D.at(p, "k"))
                        f(E1, CS, ACT.Exp, scale=-DECAY).then_inc(PR_A.sem, 1)
                    nxt = JOBS[J[nxt] + 1] if J[nxt] + 1 < len(JOBS) else None

            def quad(b0):
                return ps[:, b0, :].rearrange("p (a h c) -> p a h c", h=2, c=HEAD)

            def turn(slots_, n, c):
                def take(s, step, dst, src, when=None):
                    ac.wait_ge(CE[s].sem, CE[s].at(n, when or step))
                    f(dst, src, ACT.Copy).then_inc(CA[s].sem, 1)

                def blocks(s, step, dst_of, src_of, when=None):
                    ac.wait_ge(CE[s].sem, CE[s].at(n, when or step))
                    for h in range(2):
                        rws = slice(h * HEAD, (h + 1) * HEAD)
                        last = f(dst_of(rws, h), src_of(rws, h), ACT.Copy)
                    last.then_inc(CA[s].sem, 1)

                def diagonal(m):
                    return lambda rws, h: m[rws, :, h, :]

                def column(m, k):
                    return lambda rws, h: m[rws, :, k, :]

                for s in slots_:
                    take(s, "D0", slot[s]["Db"], quad(4 * s + 3))
                for l in LV:
                    if l:
                        for s in slots_:
                            take(s, f"T{l}", slot[s]["Tb"], quad(4 * s + 2))
                    for s in slots_:
                        d, from_ = slot[s], quad(4 * s + 3)
                        if l == 0:
                            take(s, "Vt", d["Vtb"], from_)
                        else:
                            name, to = (None, ("Bt", column(d["RB"], 1)), ("NV", column(d["AN"], 1)),
                                        ("Kt", column(d["RK"], 1)), ("At", column(d["AN"], 0)))[l]
                            blocks(s, name, to, diagonal(from_))
                for s in slots_:
                    blocks(s, "X", diagonal(slot[s]["Xb"]), column(quad(4 * s), 0), "XZ")
                    blocks(s, "Z", diagonal(slot[s]["Zb"]), column(quad(4 * s), 1), "XZ")
                for k, s in enumerate(slots_):
                    if 1 in slots_:
                        ac.wait_ge(CD[s].sem, CD[s].at(n, "S"))
                    take(s, "Y", AR[:, :, 1, bass.ds((c + k) * CH, CH)], quad(4 * s + 3)[:, :, 0, :], "YS")

            ac.wait_ge(s_z0, 10)
            turn((0, 1), 0, 0)
            with ac.Fori(1, (NCH - 1) // 2) as i:
                turn((0, 1), i, i * 2)
            turn((0,), (NCH - 1) // 2, NCH - 1)

            for n in range(2 * PAIRS):
                p, hf = n // 2, n % 2
                y = AR[:, p, 1, CH + hf * 512:CH + hf * 512 + 512]
                ac.wait_ge(GN_D.sem, GN_D.at(n, "c"))
                f(gsq[n % 2], y, ACT.Square).then_inc(GN_A.sem, 1)
                ac.wait_ge(GN_E.sem, GN_E.at(n, "var"))
                f(gsd[n % 2], ps[:, 4 * (n % 2) + 1, :], ACT.Sqrt, scale=1.0 / HEAD, bias=eps[:, 1:2]).then_inc(GN_A.sem, 1)

            def copy_h(ti):
                for hf in range(2):
                    ac.wait_ge(F_E.sem, F_E.at(ti, f"t{hf}"))
                    f(h1T[ti % 2][:, 4 * hf:4 * hf + 4, :], ps[:, 4 + hf, :].rearrange("p (k c) -> p k c", c=P),
                      ACT.Copy).then_inc(F_C.sem, 1)

            for ti in range(NT):
                if ti:
                    copy_h(ti - 1)
                ac.wait_ge(F_D.sem, F_D.at(ti, "agg"))
                f(rstd[:, 0:1], mv[:, 1:2], ACT.Sqrt, bias=eps[:, 0:1]).then_inc(F_A, 1)
            copy_h(NT - 1)
            ac.wait_ge(s_rt_arg, 1)
            f(lg[:, :, 0:NG + 1], lg[:, :, 0:NG + 1], ACT.Exp).then_inc(s_rta, 1)

            def head(s, n, k):
                ac.wait_ge(s_we[k], n * 16 + 16)
                if not (isinstance(n, int) and n < 2):
                    ac.wait_ge((E_G, E_U, E_Y)[k], n - 1)
                f(wsp[s][k][0], raw[k], ACT.Copy).then_inc(s_hi[k], 1)

            def rows_in(s, n):
                ac.wait_ge(E_X, n + 1)
                f(xT[s][0], ps[:, 0:2, :].rearrange("p b (k c) -> p (b k) c", c=P), ACT.Copy).then_inc(A_X, 1)

            def silu(s, n):
                ac.wait_ge(E_G, n + 1)
                f(hs[s], ps[:, 2, :], ACT.Silu).then_inc(A_S, 1)

            def hidden(s, n):
                ac.wait_ge(E_H, n + 1)
                f(hTe[s][0], ps[:, 4, :].rearrange("p (k c) -> p k c", c=P), ACT.Copy).then_inc(A_H, 1)

            def yout(s, n):
                ac.wait_ge(E_Y, n + 1)
                if not (isinstance(n, int) and n < 2):
                    ac.wait_ge(s_yo[s], (n - s) * 8)
                f(yb[s][:, 0:512], ps[:, 5, :], ACT.Copy).then_inc(A_Y, 1)

            def turn(s, n, more=True):
                if more:
                    head(1 - s, n + 1, 0)
                silu(s, n)
                if not first(n):
                    hidden(1 - s, n - 1)
                if more:
                    rows_in(1 - s, n + 1)
                    head(1 - s, n + 1, 1)
                    head(1 - s, n + 1, 2)
                if not first(n):
                    yout(1 - s, n - 1)

            ac.wait_ge(F_L, NT)
            for b in range(2):
                ac.wait_ge(s_h1st[b], 16 * 4)
            for k in range(3):
                head(0, 0, k)
            rows_in(0, 0)
            turn(0, 0)
            turn(1, 1)
            with ac.Fori(1, NE // 2 - 1) as i:
                turn(0, i * 2)
                turn(1, i * 2 + 1)
            turn(0, NE - 2)
            turn(1, NE - 1, False)
            hidden(1, NE - 1)
            yout(1, NE - 1)
            n_over = ac.value_load(novi[0:1, 0:1], min_val=0, max_val=OVER)
            for j in range(OVER):
                with ac.If(n_over > j):
                    s, n = j % 2, NE + j
                    rows_in(s, n)
                    for k in range(3):
                        head(s, n, k)
                    silu(s, n)
                    hidden(s, n)
                    yout(s, n)

            for ti in range(NT):
                ac.wait_ge(O_D.sem, O_D.at(ti, "agg"))
                f(rstd[:, 0:1], mv[:, 1:2], ACT.Sqrt, bias=eps[:, 0:1]).then_inc(O_A, 1)

        @block.tensor
        def _(pe):
            mm, tr = nc.tensor.matmul, nc.tensor.transpose

            pe.wait_ge(s_const, 2)
            for ti in range(NT + 1):
                b, r = ti % 2, rows(ti)
                pe.wait_ge(s_h.sem, s_h.at(ti, "bias"))
                if ti >= 2:
                    pe.wait_ge(s_ht, 2 * (ti - 1))
                for hf in range(2):
                    for k in range(4):
                        last = tr(ps[:, 2 * b + hf, k * P:k * P + r], xh[b][0:r, (4 * hf + k) * P:(4 * hf + k + 1) * P],
                                  ident[0:r, 0:r])
                    last.then_inc(s_tp, 1)

            def emptied(job):
                kind, j = job
                if kind == "gl":
                    pe.wait_ge(s_gelu, j + 1)
                elif kind == "lx":
                    pe.wait_ge(s_lx, j + 1)
                elif kind in ("gr", "gi"):
                    pe.wait_ge(LRU_A.sem, LRU_A.at(j, kind))
                elif kind in ("z", "r", "k", "v"):
                    pe.wait_ge(s_uev, SHIFTED.index(job) + 1)
                elif kind == "dec":
                    pe.wait_ge(PR_A.sem, PR_A.at(j, "sg"))
                elif kind == "aa":
                    pe.wait_ge(PR_A.sem, PR_A.at(j, "a"))
                elif kind == "ss":
                    pe.wait_ge(PR_D.sem, PR_D.at(j, "ssm"))
                else:
                    pe.wait_ge(PR_D.sem, PR_D.at(j, "bon"))

            pe.wait_ge(s_ht, 2 * (NT + 1))
            pe.wait_ge(s_zcol, 1)
            for n, job in enumerate(JOBS):
                kind, j = job
                if n >= 2:
                    emptied(JOBS[n - 2])
                if job in WTILES:
                    w = WTILES.index(job)
                    width = cols(kind, j)[1]
                    pe.wait_ge(s_w[w % 2], 16 * (w // 2 + 1))
                    for k in range(KD):
                        for q in range(3):
                            last = mm(bank(job, width)[:, q, :], wbuf[w % 2][:, k, 0:width], hT[:, k, q * SEG:(q + 1) * SEG],
                                      start=k == 0, stop=k == KD - 1)
                else:
                    if kind in ("gr", "gi"):
                        pe.wait_ge(s_gate_w, 64)
                        pe.wait_ge(LRU_D.sem, LRU_D.at(j, "c3"))
                        lhs, rhs = (wrg if kind == "gr" else wig)[:, j, :], XC
                    elif kind in ("dec", "aa"):
                        pe.wait_ge(s_zact, 1)
                        pe.wait_ge(s_prm, 16 * 15)
                        h = slice(0, 64) if kind == "dec" else slice(64, 128)
                        lhs, rhs = wlr[h, j * P:(j + 1) * P], Z0[h, :]
                    elif kind == "ss":
                        pe.wait_ge(PR_A.sem, PR_A.at(j, "sq"))
                        pe.wait_ge(s_const_done, 1)
                        lhs, rhs = blk.rearrange("p h c -> p (h c)"), T7
                    else:
                        pe.wait_ge(PR_D.sem, PR_D.at(j, "q"))
                        lhs, rhs = blk.rearrange("p h c -> p (h c)"), T7
                    for q in range(3):
                        last = mm(bank(job)[:, q, :], lhs, rhs[:, q * SEG:(q + 1) * SEG], start=True, stop=True)
                last.then_inc(s_job, 1)

            def pair(m, p):
                return m[:, p, :, :].rearrange("p h c -> p (h c)")

            def products(s, k, lefts_rights):
                for p in range(PAIRS):
                    for q, (lh, rh) in enumerate(lefts_rights):
                        last = mm(ps[:, 4 * s + k, p * P:(p + 1) * P], pair(lh, p), pair(rh, p),
                                  start=q == 0, stop=q == len(lefts_rights) - 1)
                last.then_inc(CE[s].sem, 1)

            def transposes(s, k, m):
                for p in range(PAIRS):
                    last = tr(ps[:, 4 * s + k, p * P:(p + 1) * P], pair(m, p), ident)
                last.then_inc(CE[s].sem, 1)

            def scores(s, k, n, c):
                name = "BK"[k]
                pe.wait_ge(CP[s].sem, CP[s].at(n, name))
                for p in range(PAIRS):
                    last = mm(ps[:, 4 * s + k, p * P:(p + 1) * P], pair(slot[s][name + "b"], p),
                              AR[:, p, :, bass.ds(c * CH, CH)], start=True, stop=True)
                last.then_inc(CM[s].sem, 1)

            def turn(slots_, n, c):
                def W(st_, name, m=None):
                    pe.wait_ge(st_.sem, st_.at(n if m is None else m, name))

                if 1 in slots_:
                    scores(1, 0, n, c + 1)
                    scores(1, 1, n, c + 1)
                for s in slots_:
                    W(CD[s], "T0")
                    if not first(n):
                        W(CA[s], "Y", n - 1)
                    transposes(s, 3, slot[s]["Tb"])
                    if s == 0 and not first(n):
                        W(CD[1], "S", n - 1)
                        transposes(1, 2, slot[1]["Sb"])
                for l in LV:
                    for s in slots_:
                        if l == 0:
                            W(CD[s], "Mr")
                            W(CA[s], "D0")
                        else:
                            W(CD[s], f"D{l}")
                        products(s, 0, [(slot[s]["Mb"], slot[s]["Db"])])
                    if l:
                        for s in slots_:
                            if l == 1 and not first(n):
                                W(CB[s], "SB", n - 1)
                            transposes(s, 2, slot[s]["Db"])
                    for s in slots_:
                        if l:
                            W(CA[s], ("Vt", "Bt", "NV", "Kt")[l - 1])
                        if l == 2:
                            W(CD[s], "Nb")
                            products(s, 3, [(slot[s]["Nb"], slot[s]["Vtb"])])
                        else:
                            name = ("V", "B", None, "K", "A")[l]
                            W(CP[s], name)
                            transposes(s, 3, slot[s][name + "b"])
                    for s in slots_:
                        if l == 0:
                            W(CD[s], "Mk")
                        W(CD[s], f"P{l}")
                        if l:
                            W(CA[s], f"T{l}")
                        if l < LV[-1]:
                            products(s, 1, [(slot[s]["Tb"], slot[s]["Pb"])])
                        else:
                            products(s, 1, [(slot[s]["Pb"], slot[s]["Tb"])])
                for s in slots_:
                    W(CD[s], "T5")
                    W(CA[s], "At")
                    products(s, 0, [(slot[s]["Tb"], slot[s]["AN"])])
                for s in slots_:
                    W(CA[s], "X")
                    products(s, 1, [(slot[s]["Xb"], slot[s]["RB"])])
                for s in slots_:
                    if s == 1:
                        scores(0, 0, n + 1, c + 2)
                        W(CD[0], "S")
                        transposes(0, 2, slot[0]["Sb"])
                        scores(0, 1, n + 1, c + 2)
                        W(CB[0], "SB")
                    elif not first(n):
                        W(CB[1], "SB", n - 1)
                    W(CA[s], "Z")
                    W(CD[s], "Q")
                    products(s, 3, [(slot[s]["Zb"], slot[s]["RB"]), (slot[s]["Vtb"], slot[s]["RK"]),
                                    (SB[s], slot[s]["QG"])])

            pe.wait_ge(s_z0, 10)
            pe.wait_ge(PR_D.sem, PR_D.at(PAIRS - 1, "at"))
            scores(0, 0, 0, 0)
            scores(0, 1, 0, 0)
            turn((0, 1), 0, 0)
            with pe.Fori(1, (NCH - 1) // 2) as i:
                turn((0, 1), i, i * 2)
            turn((0,), (NCH - 1) // 2, NCH - 1)

            pe.wait_ge(s_wgu, 32)
            pe.wait_ge(s_zg, 2)
            for s in range(2):
                pe.wait_ge(CA[s].sem, CA[s].at((NCH - 1) // 2 - s, "Y"))
            sums = blk.rearrange("p h c -> p (h c)")
            for n in range(2 * PAIRS):
                p, hf = n // 2, n % 2
                B = 4 * (n % 2)
                cs = slice(hf * 512, hf * 512 + 512)
                if n >= 2:
                    pe.wait_ge(GN_D.sem, GN_D.at(n - 2, "g"))
                mm(ps[:, B, :], sums, AR[:, p, 1, CH + hf * 512:CH + hf * 512 + 512], start=True, stop=True).then_inc(GN_E.sem, 1)
                mm(ps[:, B + 2, :], wgu[:, 0, p * P:(p + 1) * P], ZG[:, 0, cs], start=True, stop=False)
                mm(ps[:, B + 2, :], wgu[0:32, 1, p * P:(p + 1) * P], ZG[0:32, 1, cs], start=False, stop=True).then_inc(GN_E.sem, 1)
                pe.wait_ge(GN_A.sem, GN_A.at(n, "sq"))
                mm(ps[:, B + 1, :], sums, gsq[n % 2], start=True, stop=True).then_inc(GN_E.sem, 1)

            def router(ti):
                b = ti % 2
                pe.wait_ge(F_P.sem, F_P.at(ti, "bias"))
                if ti:
                    pe.wait_ge(F_C.sem, F_C.at(ti - 1, "t1"))
                    pe.wait_ge(F_L, ti)
                for hf in range(2):
                    for k in range(4):
                        last = tr(ps[:, 4 + hf, k * P:(k + 1) * P], h1[b][:, (4 * hf + k) * P:(4 * hf + k + 1) * P], ident)
                    last.then_inc(F_E.sem, 1)
                pe.wait_ge(F_C.sem, F_C.at(ti, "t1"))
                for k in range(KD):
                    last = mm(ps[:, 6, 0:NG + NE], h1T[b][:, k, :], wr[:, k, :], start=k == 0, stop=k == KD - 1)
                last.then_inc(F_E.sem, 1)

            pe.wait_ge(GN_D.sem, GN_D.at(2 * PAIRS - 1, "g"))
            pe.wait_ge(s_wo, 16)
            pe.wait_ge(s_yl, 16)
            pe.wait_ge(s_wr, 64)
            for ti in range(NT):
                b = ti % 2
                if ti >= 2:
                    pe.wait_ge(F_D.sem, F_D.at(ti - 2, "res1"))
                for hf in range(2):
                    for k in range(KD):
                        y = AR[:, k, 1, CH + ti * P:CH + (ti + 1) * P] if k < PAIRS else yl[:, k - PAIRS, ti * P:(ti + 1) * P]
                        last = mm(ps[:, 2 * b + hf, :], y, wo[:, k, hf * 512:(hf + 1) * 512], start=k == 0, stop=k == KD - 1)
                    last.then_inc(F_O.sem, 1)
                if ti:
                    router(ti - 1)
            router(NT - 1)
            pe.wait_ge(s_rt_oh, 1)
            mm(ps[:, 0, 0:NT * NE], ltri, OS.rearrange("p a b -> p (a b)"), start=True, stop=False)
            mm(ps[:, 0, 0:NT * NE], ones, OP[:, 0:NT, :].rearrange("p a b -> p (a b)"), start=False, stop=True)
            mm(ps[:, 1, 0:NE], ones, OP[:, NT, :], start=True, stop=True).then_inc(s_rte, 1)

            def rows_in(s, n):
                pe.wait_ge(s_xg[s], (n - s) * 8 + 16)
                if not first(n):
                    pe.wait_ge(V_X, n)
                xv = xg[s].rearrange("p (c k) -> p k c", k=KD)
                for k in range(KD):
                    last = tr(ps[:, k // 4, (k % 4) * P:(k % 4 + 1) * P], xv[:, k, :], ident)
                last.then_inc(E_X, 1)

            def split_product(out_, x, w, kk, cs):
                for k in range(kk):
                    mm(out_, x[0][:, k, :], w[0][:, k, cs], start=k == 0, stop=False)
                    mm(out_, x[0][:, k, :], w[1][:, k, cs], start=False, stop=False)
                for k in range(kk):
                    last = mm(out_, x[1][:, k, :], w[0][:, k, cs], start=False, stop=k == kk - 1)
                return last

            def gate(s, n):
                pe.wait_ge(V_X, n + 1)
                pe.wait_ge(s_lo[0], n + 1)
                if not first(n):
                    pe.wait_ge(A_S, n)
                split_product(ps[:, 2, :], xT[s], wsp[s][0], KD, slice(0, FE)).then_inc(E_G, 1)

            def up(s, n):
                pe.wait_ge(s_lo[1], n + 1)
                if not first(n):
                    pe.wait_ge(V_M, n)
                split_product(ps[:, 3, :], xT[s], wsp[s][1], KD, slice(0, FE)).then_inc(E_U, 1)

            def turned(s, n):
                pe.wait_ge(V_M, n + 1)
                if not first(n):
                    pe.wait_ge(V_H, n)
                hv = hd[s].rearrange("p (c k) -> p k c", k=KF)
                for k in range(KF):
                    last = tr(ps[:, 4, k * P:(k + 1) * P], hv[:, k, :], ident)
                last.then_inc(E_H, 1)

            def down(s, n):
                pe.wait_ge(V_H, n + 1)
                pe.wait_ge(s_lo[2], n + 1)
                if not first(n):
                    pe.wait_ge(A_Y, n)
                    pe.wait_ge(V_Y, n)
                for hf in range(2):
                    last = split_product(ps[:, 5 + hf, :], hTe[s], wsp[s][2], KF, slice(hf * 512, (hf + 1) * 512))
                last.then_inc(E_Y, 1)

            def turn(s, n, more=True):
                gate(s, n)
                if not first(n):
                    turned(1 - s, n - 1)
                if more:
                    rows_in(1 - s, n + 1)
                up(s, n)
                if not first(n):
                    down(1 - s, n - 1)

            rows_in(0, 0)
            turn(0, 0)
            turn(1, 1)
            with pe.Fori(1, NE // 2 - 1) as i:
                turn(0, i * 2)
                turn(1, i * 2 + 1)
            turn(0, NE - 2)
            turn(1, NE - 1, False)
            turned(1, NE - 1)
            down(1, NE - 1)
            n_over = pe.value_load(novi[0:1, 0:1], min_val=0, max_val=OVER)
            for j in range(OVER):
                with pe.If(n_over > j):
                    s, n = j % 2, NE + j
                    rows_in(s, n)
                    gate(s, n)
                    up(s, n)
                    turned(s, n)
                    down(s, n)


_INS = ["x", "meta", "ln0_g", "ln0_b", "w_in", "mu_shift", "w0", "w_decay_up", "a0", "w_a_up", "w_g_up", "k_k", "k_a", "r_k",
        "gn_g", "gn_b", "conv_w", "conv_b", "w_rg", "b_rg", "w_ig", "b_ig", "lru_lambda", "w_out", "ln1_g", "ln1_b",
        "w_router_grp", "b_router_grp", "w_router_exp", "b_router_exp", "w_exp_gate", "w_exp_up", "w_exp_down",
        "ln2_g", "ln2_b"]


def kernel(**inputs):
    import numpy as _np
    import concourse.bacc as _bacc
    from concourse import mybir as _mybir
    from concourse.bass_utils import run_bass_kernel_spmd as _run

    nc = _bacc.Bacc("TRN2", target_bir_lowering=False, num_devices=1)
    f32, i32 = _mybir.dt.float32, _mybir.dt.int32
    arrays, args = {}, {}
    for name in _INS:
        v = _np.ascontiguousarray(inputs[name])
        arrays[f"in_{name}_dram"] = v
        args[name] = nc.dram_tensor(f"in_{name}_dram", v.shape, _mybir.dt.from_np(v.dtype), kind="ExternalInput").ap()
    out = nc.dram_tensor("out_dram", (1, SEQ, D), f32, kind="ExternalOutput").ap()
    scratch = {
        "h": nc.dram_tensor("scr_h", (SEQ, D), f32).ap(),
        "ylru": nc.dram_tensor("scr_ylru", (4 * P, SEQ), f32).ap(),
        "h1": nc.dram_tensor("scr_h1", (SEQ, D), f32).ap(),
        "tok": nc.dram_tensor("scr_tok", (NBLK * CAP, 1), i32).ap(),
        "y": nc.dram_tensor("scr_y", (NBLK * CAP, D), f32).ap(),
    }
    build(nc, args, out, scratch)
    r = _run(nc, [arrays], core_ids=[0])
    return r.results[0]["out_dram"]
```

```python
from contextlib import ExitStack

import concourse.bass as bass
from concourse import mybir

F32 = mybir.dt.float32
BF16 = mybir.dt.bfloat16
F16 = mybir.dt.float16
I32 = mybir.dt.int32
U32 = mybir.dt.uint32
ALU = mybir.AluOpType
ACT = mybir.ActivationFunctionType
AXX = mybir.AxisListType.X

D = 1024
SEQ = 1024
META = 16
P = 128
KD = D // P
NT = SEQ // P
HEAD = 64
PAIRS = 4
CH = 64
NCH = 17
TP = NCH * CH
PAD = TP - SEQ - META
TQ = SEQ + META + 1
Q0 = PAD - 1
SEG = TQ // 3
XQ = META + 1
DECAY = 0.6065306597126334
N_RWKV = 1824
GATE = 160
NG, EPG = 4, 8
NE = NG * EPG
FE = 512
KF = FE // P
CAP = P
OVER = 16
NBLK = NE + OVER
ALPHA = 2.0 ** 0.25
W_UP = 64.0
LN_EPS, GN_EPS = 1e-5, 64e-5


class Steps:

    def __init__(self, sem, names):
        self.sem, self.names = sem, list(names)

    def at(self, turn, name):
        return turn * len(self.names) + (self.names.index(name) + 1)


def build(nc, a, out, scratch):
    ctx = ExitStack()
    with ctx:
        def sem(name):
            return ctx.enter_context(nc.semaphore(name))

        WORDS = 53000
        big = ctx.enter_context(nc.sbuf_tensor("big", [P, WORDS], F32))
        ps = ctx.enter_context(nc.psum_tensor("ps", [P, 8, 512], F32))

        class Region:
            def __init__(self, at):
                self.at = at

            def take(self, *shape):
                n = 1
                for s in shape:
                    n *= s
                v = big[:, self.at:self.at + n]
                self.at += n
                assert self.at <= WORDS, self.at
                if len(shape) == 2:
                    v = v.rearrange("p (a b) -> p a b", b=shape[1])
                elif len(shape) == 3:
                    v = v.rearrange("p (a b c) -> p a b c", b=shape[1], c=shape[2])
                return v

        R = Region(0)
        ident = R.take(P)
        blk = R.take(2, HEAD)
        ident2 = R.take(HEAD)
        m_strict = R.take(2, HEAD)
        m_incl = R.take(HEAD)
        m_sub = R.take(5, 2 * HEAD).rearrange("p l (h c) -> p l h c", c=HEAD)
        m_supT = R.take(2, HEAD)
        ones = R.take(P)
        ltri = R.take(P)
        lng = R.take(D)
        lnb = R.take(D)
        mu = R.take(15)
        prm = R.take(12, 4)
        ln0c = R.take(2, KD)
        (P_W0, P_A0, P_KK, P_KA, P_RK, P_GG, P_GB, P_CB, P_BR, P_BI, P_LAM, P_K1) = range(12)
        cw = R.take(4, 4)
        c8 = R.take(2, 4)
        lamt = R.take(6, 4)
        hprm = R.take(4, 4)
        eps = R.take(2)
        st6 = R.take(2, 6)
        mv = R.take(2)
        rstd = R.take(2)
        wc = R.take(PAIRS, NCH)
        wlr = R.take(512)
        BASE = R.at

        AR = R.take(PAIRS, 2, TP)
        BT = R.take(PAIRS, TP)
        KT = R.take(PAIRS, TP)
        VT = R.take(PAIRS, TP)
        BON = R.take(PAIRS, TQ)
        ZG = R.take(2, SEQ)
        AFTER = R.at

        def halves(region, *shape, dt=BF16):
            n = 1
            for x in shape:
                n *= x
            return [region.take(n // 2).bitcast(dt).rearrange("p (a b) -> p a b", b=shape[1]) for _ in range(2)]

        hT = halves(R, KD, TQ, dt=F16)
        wbuf = [halves(R, KD, P, dt=F16) for _ in range(2)]
        wraw = [x.rearrange("p (k c) -> p k c", c=P) for x in (lng, lnb)]
        rst = R.take(TQ // 2 + 1)
        reset = rst.bitcast(BF16)[:, 0:TQ]
        UB = R.take(2, TQ)
        Z0 = R.take(TQ)
        TM = [R.take(TQ) for _ in range(6)]
        SG, CS, E1, AA, KK, T7 = TM
        ZG0, XC, GR, GI, GS, LD = TM

        RA = Region(AFTER + KD * TQ + 2 * KD * P + TQ // 2 + 1)
        xb = [RA.take(D) for _ in range(2)]
        xh = [RA.take(D) for _ in range(2)]
        ht32 = [RA.take(KD, P) for _ in range(2)]

        GG = BT
        wrg = VT[:, 0, 0:512].rearrange("p (j c) -> p j c", c=P)
        wig = VT[:, 0, 512:1024].rearrange("p (j c) -> p j c", c=P)
        LA = VT[:, 1, 0:TQ]
        YL = VT[:, 2, 0:SEQ]
        YZ = KT[:, 0, 0:D]
        XL = VT[:, 3, 0:1044]

        (meta_d, x_d) = (a["meta"], a["x"])
        h_dram, ylru_dram, h1_dram, tok_dram, y_dram = (
            scratch[n] for n in ("h", "ylru", "h1", "tok", "y"))

        s_const = sem("s_const")
        s_prm = sem("s_prm")
        s_gate_w = sem("s_gate_w")
        s_const_done = sem("s_const_done")
        s_lnp = sem("s_lnp")
        s_xin = [sem(f"s_xin{i}") for i in range(2)]
        s_ln = Steps(sem("s_ln"), ["st0", "st1", "agg", "rstd", "xhat"])
        s_std = sem("s_std")
        s_hf = sem("s_hf")
        s_tp = sem("s_tp")
        s_ht, s_hl = sem("s_ht"), sem("s_hl")
        s_whi, s_wlo = sem("s_whi"), sem("s_wlo")
        s_hst = [sem(f"s_hst{i}") for i in range(2)]
        s_yz, s_yzd = sem("s_yz"), sem("s_yzd")
        s_zcol = sem("s_zcol")
        s_setup = sem("s_setup")
        s_absl, s_expl, s_c8 = sem("s_absl"), sem("s_expl"), sem("s_c8")

        def cols(kind, j):
            base = {"r": 0, "k": 512, "v": 1024, "lx": N_RWKV, "gl": N_RWKV + 512}
            if kind == "z":
                return (1536 + P * j, P if j < 2 else 32)
            return base[kind] + P * j, P

        JOBS = [("gl", 0), ("lx", 0), ("gl", 1), ("lx", 1), ("gr", 0), ("gi", 0), ("gl", 2), ("lx", 2), ("gr", 1), ("gi", 1),
                ("gl", 3), ("lx", 3), ("gr", 2), ("gi", 2), ("z", 0), ("z", 1), ("gr", 3), ("gi", 3), ("z", 2),
                ("r", 0), ("k", 0)]
        for p in range(PAIRS):
            nxt = [("r", p + 1), ("k", p + 1)] if p + 1 < PAIRS else []
            JOBS += [("dec", p), ("aa", p), ("v", p), ("ss", p)] + nxt[0:1] + [("bon", p)] + nxt[1:2]
        J = {j: n for n, j in enumerate(JOBS)}
        WTILES = [j for j in JOBS if j[0] in ("gl", "lx", "z", "r", "k", "v")]
        s_w = [sem(f"s_w{i}") for i in range(2)]
        s_job = sem("s_job")
        SHIFTED = [j for j in JOBS if j[0] in ("z", "r", "k", "v")]

        def bank(job, rows=P):
            s = J[job] % 2
            return ps[0:rows, 3 * s:3 * s + 3, 0:SEG]

        def seg3(v):
            return v.rearrange("p (s c) -> p s c", c=SEG)

        s_gelu = sem("s_gelu")
        s_uev = sem("s_uev")
        s_udif = sem("s_udif")
        s_ush = sem("s_ush")
        s_zact = sem("s_zact")
        s_zg = sem("s_zg")
        LRU_D = Steps(sem("s_lrud"), ["c0", "c1", "c2", "c3", "gr", "m2", "gi", "ga", "gb", "scan", "y"])
        s_lx = sem("s_lx")
        LRU_A = Steps(sem("s_lrua"), ["gr", "gi", "la", "gs", "ln", "rc", "sq"])
        s_yst = sem("s_yst")
        PR_D = Steps(sem("s_prd"), ["sg", "cs", "csx", "a", "kk", "ssm", "kkn", "kc", "k2", "q", "bon",
                                    "b0", "b", "k", "r", "at"])
        PR_A = Steps(sem("s_pra"), ["sg", "a", "sq", "iw", "ln", "rt", "w63", "wx", "w"])
        s_z0 = sem("s_z0")

        RC = Region(AFTER)
        slot = []
        for s in range(2):
            d = {n: RC.take(PAIRS, 2, HEAD) for n in
                 ("Ab", "Bb", "Kb", "Vb",
                  "Mb", "Nb",
                  "Db", "Tb", "Pb",
                  "Vtb", "Xb", "Zb",
                  "AN",
                  "RB", "RK",
                  "QG",
                  "Sb")}
            slot.append(d)
        SB = [RC.take(PAIRS, 2, HEAD) for _ in range(2)]

        LV = range(5)
        CP = [Steps(sem(f"s_cp{s}"), ["B", "K", "V", "A"]) for s in range(2)]
        CM = [Steps(sem(f"s_cs{s}"), ["MB", "MK"]) for s in range(2)]
        CE = [Steps(sem(f"s_ce{s}"), ["D0", "P0", "Vt", "DP0", "P1", "T1", "Bt", "DP1", "P2", "T2", "NV", "DP2", "P3",
                                      "T3", "Kt", "DP3", "P4", "T4", "At", "PD", "XZ", "QG", "YS", "St"])
              for s in range(2)]
        CD = [Steps(sem(f"s_cd{s}"), ["T0a", "T0", "Mb", "Mr", "Nb", "Mk", "P0", "D1", "P1", "D2", "P2", "D3", "P3",
                                      "D4", "P4", "T5", "G", "Q", "S"]) for s in range(2)]
        CB = [Steps(sem(f"s_cb{s}"), ["SB"]) for s in range(2)]
        CA = [Steps(sem(f"s_ca{s}"), ["D0", "Vt", "T1", "Bt", "T2", "NV", "T3", "Kt", "T4", "At", "X", "Z", "Y"])
              for s in range(2)]

        RE = Region(AFTER)
        yl = RE.take(4, SEQ)
        wo = RE.take(KD, D)
        gsq = [RE.take(512) for _ in range(2)]
        gsd = [RE.take(512) for _ in range(2)]
        wgu = RE.take(2, 512)
        GN_C = sem("s_gnc")
        GN_D = Steps(sem("s_gnd"), ["n", "aff", "bon", "g"])
        GN_A = Steps(sem("s_gna"), ["ln", "rs"])
        GN_S = sem("s_gns")
        GN_M, GN_V, GN_G = sem("s_gnm"), sem("s_gnv"), sem("s_gng")
        s_wo, s_yl, s_wgu = sem("s_wo"), sem("s_yl"), sem("s_wgu")

        RF = Region(BASE + PAIRS * 2 * TP)
        hb = [RF.take(D) for _ in range(2)]
        zb = [RF.take(D) for _ in range(2)]
        h1 = [RF.take(D) for _ in range(2)]
        h1T = [RF.take(KD, P) for _ in range(2)]
        ln0g, ln0b = RF.take(D), RF.take(D)
        RF = Region(BASE + 6 * KD * FE)
        wr = RF.take(KD, NG + NE)
        br = RF.take(NG + NE)
        lg = RF.take(NT, NG + NE)
        F_D = Steps(sem("s_fd"), ["res0", "res1", "st0", "st1", "agg", "rstd", "xhat"])
        F_L = sem("s_fl")
        F_P = Steps(sem("s_fp"), ["gain", "bias"])
        F_H = Steps(sem("s_fh"), ["gain", "bias"])
        s_ln0 = sem("s_ln0")
        F_A = sem("s_fa")
        F_C = Steps(sem("s_fc"), ["t0", "t1"])
        F_O = Steps(sem("s_fo"), ["o0", "o1"])
        F_E = Steps(sem("s_fe"), ["t0", "t1", "lg"])
        s_hin = [sem(f"s_hin{i}") for i in range(2)]
        s_h1st = [sem(f"s_h1st{i}") for i in range(2)]
        s_wr, s_ln1 = sem("s_wr"), sem("s_ln1")

        g8 = RF.take(8)
        i4 = RF.take(NE)
        e8 = RF.take(EPG)
        gm8, gi8f = RF.take(8), RF.take(8)
        gi8 = RF.take(8).bitcast(U32)
        ti8 = RF.take(8).bitcast(U32)
        ti8f = RF.take(8)
        ohg = RF.take(NG)
        esel = RF.take(NG, EPG)
        tm8 = RF.take(8)
        sm = RF.take(16)
        oh_at = RF.at
        OH = [RF.take(NT, NE) for _ in range(2)]
        OS = RF.take(NT, NE)
        OP = RF.take(NT + 1, NE)
        RK = RF.take(NT, NE)
        t32 = RF.take(NT, NE)
        eidf = RF.take(2, NT)
        rk = RF.take(2, NT)
        ovs = RF.take(2, NT)
        qk = RF.take(2, NT)
        q7 = RF.take(2 * NT, 7)
        th7 = RF.take(7)
        cnt = RF.take(NE)
        c7 = RF.take(NE, 7)
        ovb, ovi, ove = RF.take(NE), RF.take(NE), RF.take(NE)
        j16 = RF.take(OVER)
        o16 = big[:, oh_at:oh_at + OVER * NE].rearrange("p (j e) -> p j e", e=NE)
        oef = RF.take(OVER)
        s1t = RF.take(2, NT)
        ztab = RF.take(NBLK * CAP // P)
        assert RF.at <= AFTER, RF.at
        KEEP = 52800
        RK2 = Region(KEEP)
        gates = RK2.take(2, NT)
        slots = RK2.take(2, NT).bitcast(I32)
        oei = RK2.take(OVER).bitcast(I32)
        novi = RK2.take(1).bitcast(I32)
        tokid = RK2.take(NT).bitcast(I32)
        idx = RK2.take(NBLK).bitcast(I32)
        s_rt = sem("s_rt")
        s_rt_arg, s_rt_oh, s_rt_done = sem("s_rt_arg"), sem("s_rt_oh"), sem("s_rt_done")
        s_rta = sem("s_rta")
        s_rte = sem("s_rte")
        s_rtc = sem("s_rtc")
        s_zt, s_sc, s_idx = sem("s_zt"), sem("s_sc"), sem("s_idx")

        RM = Region(BASE)

        raw = [RM.take(KD, FE), RM.take(KD, FE), RM.take(KF, D)]
        wsp = [[halves(RM, KD, FE), halves(RM, KD, FE), halves(RM, KF, D)] for _ in range(2)]
        xg = [RM.take(D) for _ in range(2)]
        xT = [halves(RM, KD, P) for _ in range(2)]
        hs = [RM.take(FE) for _ in range(2)]
        hd = [RM.take(FE) for _ in range(2)]
        hTe = [halves(RM, KF, P) for _ in range(2)]
        yb = [RM.take(D) for _ in range(2)]
        assert RM.at <= KEEP, RM.at
        s_we = [sem(f"s_we{k}") for k in range(3)]
        s_hi = [sem(f"s_hi{k}") for k in range(3)]
        s_lo = [sem(f"s_lo{k}") for k in range(3)]
        s_xg = [sem(f"s_xg{i}") for i in range(2)]
        E_X, E_G, E_U, E_H, E_Y = (sem(f"s_e{n}") for n in "xguhy")
        A_X, A_S, A_H, A_Y = (sem(f"s_a{n}") for n in "xshy")
        V_X, V_M, V_H, V_Y = (sem(f"s_v{n}") for n in "xmhy")
        s_yo = [sem(f"s_yo{i}") for i in range(2)]

        RO = Region(BASE)
        AHEAD = 4
        y1 = [RO.take(D) for _ in range(AHEAD)]
        y2 = [RO.take(D) for _ in range(AHEAD)]
        hr = [RO.take(D) for _ in range(AHEAD)]
        o_x = [RO.take(D) for _ in range(2)]
        s_y1 = [sem(f"s_y1{i}") for i in range(AHEAD)]
        s_y2 = [sem(f"s_y2{i}") for i in range(AHEAD)]
        s_hr = [sem(f"s_hr{i}") for i in range(AHEAD)]
        s_ln2 = sem("s_ln2")
        O_S = sem("s_os")
        O_D = Steps(sem("s_od"), ["y2", "res", "st0", "st1", "agg", "rstd", "xhat"])
        O_A = sem("s_oa")
        O_P = Steps(sem("s_op"), ["gain", "bias"])
        s_out = [sem(f"s_out{i}") for i in range(2)]

        block = ctx.enter_context(nc.Block())

        def rows(ti):
            return META if ti == 0 else P

        def first(n):
            return isinstance(n, int) and n == 0

        def shifted(kind, j):
            if kind == "r":
                return AR[:, j, 1, PAD:TP]
            if kind == "k":
                return KT[:, j, PAD:TP]
            if kind == "v":
                return VT[:, j, PAD:TP]
            return (Z0[:, 1:TQ], TM[0][:, 1:TQ], TM[1][0:32, 1:TQ])[j]

        def finish(pl, g, ti):
            b = ti % 2
            pl.wait_ge(O_D.sem, O_D.at(ti, "xhat"))
            g.tensor_tensor(o_x[b], o_x[b], lng, ALU.mult).then_inc(O_P.sem, 1)
            pl.wait_ge(O_P.sem, O_P.at(ti, "gain"))
            g.tensor_tensor(o_x[b], o_x[b], lnb, ALU.add).then_inc(O_P.sem, 1)

        @block.sync
        def _(sp):
            for ti in range(NT + 1):
                b = ti % 2
                if ti >= 2:
                    sp.wait_ge(s_ln.sem, s_ln.at(ti - 2, "xhat"))
                src = meta_d if ti == 0 else x_d[0, (ti - 1) * P:ti * P, :]
                sp.dma_start(xb[b][0:rows(ti), :], src).then_inc(s_xin[b], 16)
                if ti == 1:
                    for n, j in enumerate(WTILES[0:2]):
                        c0, w = cols(*j)
                        sp.dma_start(wraw[n][:, :, 0:w],
                                     a["w_in"][0, :, c0:c0 + w].rearrange("(k p) c -> p k c", p=P)).then_inc(s_w[n], 16)
            names = ["w0", "a0", "k_k", "k_a", None, "gn_g", "gn_b", "conv_b", "b_rg", "b_ig", "lru_lambda"]
            with nc.allow_non_contiguous_dma(reason="parameters to columns"):
                for n, name in enumerate(names):
                    src = a["r_k"].rearrange("o h n -> o (h n)") if name is None else a[name]
                    sp.dma_start(prm[:, n, :], src[0].rearrange("(j p) -> p j", p=P)).then_inc(s_prm, 16)
                sp.dma_start(cw, a["conv_w"][0].rearrange("w (j p) -> p w j", p=P)).then_inc(s_prm, 16)
                sp.dma_start(mu[:, 0:14], a["mu_shift"][0, 0:14 * P].rearrange("(j p) -> p j", p=P)).then_inc(s_prm, 16)
                sp.dma_start(mu[0:32, 14:15], a["mu_shift"][0, 14 * P:N_RWKV].rearrange("(p j) -> p j", j=1)).then_inc(s_prm, 16)
            sp.dma_start(wlr[0:64, :], a["w_decay_up"][0]).then_inc(s_prm, 16)
            sp.dma_start(wlr[64:128, :], a["w_a_up"][0]).then_inc(s_prm, 16)
            for n, j in enumerate(WTILES[2:], 2):
                sp.wait_ge(s_wlo, n - 1)
                c0, w = cols(*j)
                sp.dma_start(wraw[n % 2][:, :, 0:w],
                             a["w_in"][0, :, c0:c0 + w].rearrange("(k p) c -> p k c", p=P)).then_inc(s_w[n % 2], 16)
            sp.wait_ge(s_wlo, len(WTILES))
            sp.dma_start(lng, a["ln1_g"].to_broadcast([P, D])).then_inc(s_ln1, 16)
            sp.dma_start(lnb, a["ln1_b"].to_broadcast([P, D])).then_inc(s_ln1, 16)
            for s in range(2):
                last = (NCH - 1 - s) // 2
                sp.wait_ge(CE[s].sem, CE[s].at(last, "YS"))
                sp.wait_ge(CA[s].sem, CA[s].at(last, "Y"))
            sp.wait_ge(CD[0].sem, CD[0].at((NCH - 1) // 2, "Q"))
            sp.wait_ge(CB[1].sem, CB[1].at((NCH - 1) // 2 - 1, "SB"))
            sp.wait_ge(s_yst, 16 * 4)
            sp.dma_start(wgu[:, 0, :], a["w_g_up"][0, 0:P, :]).then_inc(s_wgu, 16)
            sp.dma_start(wgu[0:32, 1, :], a["w_g_up"][0, P:GATE, :]).then_inc(s_wgu, 16)
            sp.dma_start(yl, ylru_dram.rearrange("(j p) t -> p j t", p=P)).then_inc(s_yl, 16)
            sp.dma_start(wo, a["w_out"][0].rearrange("(k p) n -> p k n", p=P)).then_inc(s_wo, 16)
            sp.wait_ge(GN_D.sem, GN_D.at(2 * PAIRS - 1, "g"))
            sp.dma_start(wr[:, :, 0:NG], a["w_router_grp"][0].rearrange("(k p) n -> p k n", p=P)).then_inc(s_wr, 16)
            sp.dma_start(wr[:, :, NG:NG + NE], a["w_router_exp"][0].rearrange("(k p) n -> p k n", p=P)).then_inc(s_wr, 16)
            sp.dma_start(br[:, 0:NG], a["b_router_grp"].to_broadcast([P, NG])).then_inc(s_wr, 16)
            sp.dma_start(br[:, NG:NG + NE], a["b_router_exp"].to_broadcast([P, NE])).then_inc(s_wr, 16)
            for row, name in ((ln0g, "ln0_g"), (ln0b, "ln0_b")):
                sp.dma_start(row, a[name].rearrange("(o n) -> o n", o=1).to_broadcast([P, D])).then_inc(s_ln0, 16)
            for b in range(2):
                sp.wait_ge(s_hst[b], 16 * 4)
            for ti in range(NT):
                b = ti % 2
                if ti >= 2:
                    sp.wait_ge(F_D.sem, F_D.at(ti - 2, "res1"))
                sp.dma_start(hb[b], h_dram[ti * P:(ti + 1) * P, :]).then_inc(s_hin[b], 16)

            def weights(n, e):
                srcs = (("w_exp_gate", KD), ("w_exp_up", KD), ("w_exp_down", KF))
                for k, (name, kk) in enumerate(srcs):
                    if first(n):
                        sp.wait_ge(*((F_O.sem, F_O.at(NT - 1, "o1")) if k < 2 else (F_D.sem, F_D.at(NT - 1, "xhat"))))
                    else:
                        sp.wait_ge(s_hi[k], n)
                        sp.wait_ge(s_lo[k], n)
                    sp.dma_start(raw[k], a[name][0, bass.ds(e, 1)].rearrange("o (p k) n -> p (o k) n", k=kk)).then_inc(s_we[k], 16)

            weights(0, 0)
            with sp.Fori(1, NE) as i:
                weights(i, i)
            n_over = sp.value_load(novi[0:1, 0:1], min_val=0, max_val=OVER)
            for j in range(OVER):
                with sp.If(n_over > j):
                    e = sp.value_load(oei[0:1, j:j + 1], min_val=0, max_val=NE - 1)
                    weights(NE + j, e)
            for s in range(2):
                sp.wait_ge(s_yo[s], 16 * (NE // 2))
            for j in range(OVER):
                with sp.If(n_over > j):
                    sp.wait_ge(s_yo[j % 2], 16 * (NE // 2 + j // 2 + 1))
            def rows_back(ti):
                b = ti % AHEAD
                sp.dma_start(hr[b], h1_dram[ti * P:(ti + 1) * P, :]).then_inc(s_hr[b], 16)

            for ti in range(AHEAD):
                rows_back(ti)
            for ti in range(NT):
                sp.wait_ge(O_P.sem, O_P.at(ti, "bias"))
                sp.dma_start(out[0, ti * P:(ti + 1) * P, :], o_x[ti % 2]).then_inc(s_out[ti % 2], 16)
                if ti + AHEAD < NT:
                    sp.wait_ge(O_D.sem, O_D.at(ti, "xhat"))
                    rows_back(ti + AHEAD)
            for b in range(2):
                sp.wait_ge(s_out[b], 16 * (NT // 2))

        @block.gpsimd
        def _(pl):
            g = nc.gpsimd
            count = [0]

            def const(ins):
                count[0] += 1
                ins.then_inc(s_const, 1)
                pl.wait_ge(s_const, count[0])

            with nc.allow_non_contiguous_dma(reason="parameters to columns"):
                for n, name in enumerate(("ln0_g", "ln0_b")):
                    pl.dma_start(ln0c[:, n, :], a[name].rearrange("(k p) -> p k", p=P)).then_inc(s_lnp, 16)
            const(g.memset(ident, 0.0))
            const(g.affine_select(out=ident, in_=ident, compare_op=ALU.not_equal, fill=1.0, base=0,
                                  pattern=[[-1, P]], channel_multiplier=1))
            const(g.memset(eps[:, 0:1], LN_EPS))
            const(g.memset(eps[:, 1:2], GN_EPS))
            def masks():
                const(g.memset(ones, 1.0))
                const(g.affine_select(out=ltri, in_=ones, compare_op=ALU.is_gt, fill=0.0, base=0,
                                      pattern=[[1, P]], channel_multiplier=-1))
                const(g.memset(XL[:, 0:3], 0.0))
                const(g.memset(reset, 1.0))
                const(g.memset(reset[:, CH - Q0:CH - Q0 + CH * (NCH - 2) + 1:CH], 0.0))
                for m in (blk, m_strict, m_supT, ident2, m_sub):
                    const(g.memset(m, 0.0))
                for h in range(2):
                    rws = slice(h * HEAD, (h + 1) * HEAD)
                    const(g.memset(blk[rws, h, :], 1.0))
                    const(g.affine_select(out=m_incl[rws, :], in_=ones[rws, 0:HEAD], compare_op=ALU.is_ge, fill=0.0,
                                          base=0, pattern=[[1, HEAD]], channel_multiplier=-1))
                    const(g.affine_select(out=m_strict[rws, h, :], in_=ones[rws, 0:HEAD], compare_op=ALU.is_gt, fill=0.0,
                                          base=0, pattern=[[1, HEAD]], channel_multiplier=-1))
                    const(g.affine_select(out=ident2[rws, :], in_=ident2[rws, :], compare_op=ALU.not_equal, fill=1.0,
                                          base=0, pattern=[[-1, HEAD]], channel_multiplier=1))
                    odd = m_supT[rws, h, :].rearrange("p (a b) -> p a b", b=2)[:, :, 1]
                    const(g.affine_select(out=odd, in_=odd, compare_op=ALU.not_equal, fill=1.0,
                                          base=0, pattern=[[-2, HEAD // 2]], channel_multiplier=1))
                for l in LV:
                    w = 2 << l
                    n = HEAD // (2 * w)
                    for h in range(2):
                        rws = slice(h * HEAD, (h + 1) * HEAD)
                        even = m_sub[rws, l, h, :].rearrange("p (a b c) -> p a b c", b=2, c=w)[:, :, 0, :]
                        const(g.memset(even, 1.0))
                        const(g.affine_select(out=even, in_=even, compare_op=ALU.is_ge, fill=0.0, base=-w,
                                              pattern=[[-2 * w, n], [0, w]], channel_multiplier=1))
                        const(g.affine_select(out=even, in_=even, compare_op=ALU.is_ge, fill=0.0, base=2 * w - 1,
                                              pattern=[[2 * w, n], [0, w]], channel_multiplier=-1))
                g.memset(lamt[:, 4, :], 1.0 / 19).then_inc(s_const_done, 1)

            def rest(ti):
                r = rows(ti)
                c0 = 1 if ti == 0 else XQ + (ti - 1) * P
                pl.wait_ge(s_ht, ti + 1)
                g.tensor_tensor(hT[1][:, :, c0:c0 + r], ht32[ti % 2][:, :, 0:r], hT[0][:, :, c0:c0 + r],
                                ALU.subtract).then_inc(s_hl, 1)

            for ti in range(NT + 1):
                if ti:
                    pl.wait_ge(s_ln.sem, s_ln.at(ti, "xhat"))
                    pl.dma_start(h_dram[(ti - 1) * P:ti * P, :], xh[ti % 2]).then_inc(s_hst[ti % 2], 16)
                    rest(ti - 1)
            rest(NT)
            const(g.memset(VT[:, 0, 0:1024], 0.0))
            for dst, name in ((wrg, "w_rg"), (wig, "w_ig")):
                for h in range(2):
                    pl.dma_start(dst[h * HEAD:(h + 1) * HEAD, :, h * HEAD:(h + 1) * HEAD],
                                 a[name][0].rearrange("(j h) i c -> h i j c", h=2)[h]).then_inc(s_gate_w, 16)
            masks()

            def lru_store(j):
                pl.wait_ge(LRU_D.sem, LRU_D.at(j, "y"))
                pl.dma_start(ylru_dram[j * P:(j + 1) * P, :], YL).then_inc(s_yst, 16)

            g.memset(YZ, 0.0).then_inc(s_yz, 1)
            pl.wait_ge(s_yz, 1)
            pl.dma_start(y_dram[NE * P:NBLK * P, :].rearrange("(b p) n -> p b n", p=P),
                         YZ.rearrange("p (o n) -> p o n", o=1).to_broadcast([P, OVER, D])).then_inc(s_yzd, 16)
            for j in range(3):
                lru_store(j)
            for n, (kind, j) in enumerate(SHIFTED):
                pl.wait_ge(s_uev, n + 1)
                r = cols(kind, j)[1]
                if (kind, j) == ("z", 2):
                    lru_store(3)
                if (kind, j) == ("r", 0):
                    pl.wait_ge(s_yst, 16 * 4)
                    pl.wait_ge(s_yzd, 16)
                    for arr in (AR[:, :, 0, 0:PAD], AR[:, :, 1, 0:PAD], BT[:, :, 0:PAD], KT[:, :, 0:PAD], VT[:, :, 0:PAD]):
                        g.memset(arr, 0.0).then_inc(s_z0, 1)
                dst = shifted(kind, j)
                g.tensor_tensor(dst, UB[0:r, n % 2, 0:TQ - 1], UB[0:r, n % 2, 1:TQ], ALU.subtract).then_inc(s_udif, 1)

            def blocks(dst, src):
                return g.tensor_tensor(dst, src.rearrange("p a (o c) -> p a o c", o=1).to_broadcast([P, PAIRS, 2, HEAD]),
                                       blk.rearrange("p (o h) c -> p o h c", o=1).to_broadcast([P, PAIRS, 2, HEAD]), ALU.mult)

            def prep(s, n, c):
                d = slot[s]
                if not first(n):
                    pl.wait_ge(CE[s].sem, CE[s].at(n - 1, "At"))
                for name, src in (("B", BT), ("K", KT), ("V", VT), ("A", AR[:, :, 0, :])):
                    blocks(d[name + "b"], src[:, :, bass.ds(c * CH, CH)]).then_inc(CP[s].sem, 1)

            def zeros():
                for m in (SB[0], slot[0]["Xb"], slot[0]["Zb"], slot[1]["Xb"], slot[1]["Zb"]):
                    g.memset(m, 0.0).then_inc(s_z0, 1)

            def turn(slots_, n, c):
                for k, s in enumerate(slots_):
                    prep(s, n, c + k)
                    if s == 0 and first(n):
                        zeros()

            pl.wait_ge(PR_D.sem, PR_D.at(PAIRS - 1, "at"))
            turn((0, 1), 0, 0)
            with pl.Fori(1, (NCH - 1) // 2) as i:
                turn((0, 1), i, i * 2)
            turn((0,), (NCH - 1) // 2, NCH - 1)

            pl.wait_ge(GN_D.sem, GN_D.at(2 * PAIRS - 1, "g"))
            g.iota(i4, pattern=[[1, NE]], base=0, channel_multiplier=0, allow_small_or_imprecise_dtypes=True).then_inc(s_rtc, 1)
            g.iota(th7, pattern=[[P, 7]], base=P, channel_multiplier=0, allow_small_or_imprecise_dtypes=True).then_inc(s_rtc, 1)
            g.iota(j16, pattern=[[1, OVER]], base=0, channel_multiplier=0, allow_small_or_imprecise_dtypes=True).then_inc(s_rtc, 1)
            g.iota(tokid, pattern=[[P, NT]], base=0, channel_multiplier=1).then_inc(s_rtc, 1)
            g.memset(ztab, 0.0).then_inc(s_rtc, 1)
            pl.wait_ge(s_rtc, 5)
            pl.dma_start(tok_dram.rearrange("(p b) o -> p (b o)", p=P), ztab.bitcast(I32)).then_inc(s_zt, 16)
            pl.wait_ge(s_ln1, 32)
            pl.wait_ge(s_ln0, 32)

            def residual(ti):
                b = ti % 2
                pl.wait_ge(s_hin[b], 16 * (ti // 2 + 1))
                g.tensor_tensor(hb[b], hb[b], ln0g, ALU.mult).then_inc(F_H.sem, 1)
                pl.wait_ge(F_H.sem, F_H.at(ti, "gain"))
                g.tensor_tensor(hb[b], hb[b], ln0b, ALU.add).then_inc(F_H.sem, 1)

            residual(0)
            for ti in range(NT):
                b = ti % 2
                if ti + 1 < NT:
                    residual(ti + 1)
                pl.wait_ge(F_D.sem, F_D.at(ti, "xhat"))
                g.tensor_tensor(h1[b], h1[b], lng, ALU.mult).then_inc(F_P.sem, 1)
                pl.wait_ge(F_P.sem, F_P.at(ti, "gain"))
                g.tensor_tensor(h1[b], h1[b], lnb, ALU.add).then_inc(F_P.sem, 1)
                pl.wait_ge(F_P.sem, F_P.at(ti, "bias"))
                pl.dma_start(h1_dram[ti * P:(ti + 1) * P, :], h1[b]).then_inc(s_h1st[b], 16)
            pl.wait_ge(s_rt_done, 1)
            pl.wait_ge(s_zt, 16)
            for k in range(2):
                for ti in range(NT):
                    g.indirect_dma_start(out=tok_dram, out_offset=bass.IndirectOffsetOnAxis(ap=slots[:, k, ti:ti + 1], axis=0),
                                         in_=tokid[:, ti:ti + 1], in_offset=None).then_inc(s_sc, 16)
            pl.wait_ge(s_sc, 16 * 2 * NT)
            with nc.allow_non_contiguous_dma(reason="slot table to columns"):
                pl.dma_start(idx, tok_dram.rearrange("(b p) o -> p (b o)", p=P)).then_inc(s_idx, 16)
            pl.wait_ge(s_idx, 16)
            for b in range(2):
                pl.wait_ge(s_h1st[b], 16 * 4)

            def gather(s, n):
                if n >= 2:
                    pl.wait_ge(E_X, n - 1)
                g.indirect_dma_start(out=xg[s], out_offset=None, in_=h1_dram,
                                     in_offset=bass.IndirectOffsetOnAxis(ap=idx[:, n:n + 1], axis=0)).then_inc(s_xg[s], 16)

            def store(s, n):
                pl.wait_ge(V_Y, n + 1)
                pl.wait_ge(A_Y, n + 1)
                pl.dma_start(y_dram[n * P:(n + 1) * P, :], yb[s]).then_inc(s_yo[s], 16)

            for n in range(NE):
                gather(n % 2, n)
                if n == 2:
                    pl.dma_start(lng, a["ln2_g"].to_broadcast([P, D])).then_inc(s_ln2, 16)
                    pl.dma_start(lnb, a["ln2_b"].to_broadcast([P, D])).then_inc(s_ln2, 16)
                if n >= 3:
                    store((n - 3) % 2, n - 3)
            for n in range(NE - 3, NE):
                store(n % 2, n)
            n_over = pl.value_load(novi[0:1, 0:1], min_val=0, max_val=OVER)
            for j in range(OVER):
                with pl.If(n_over > j):
                    gather(j % 2, NE + j)
                    store(j % 2, NE + j)
            for s in range(2):
                pl.wait_ge(s_yo[s], 16 * (NE // 2))
            for j in range(OVER):
                with pl.If(n_over > j):
                    pl.wait_ge(s_yo[j % 2], 16 * (NE // 2 + j // 2 + 1))
            pl.wait_ge(s_ln2, 32)
            def fetch(ti):
                b = ti % AHEAD
                for k, (y, arrived) in enumerate(((y1, s_y1), (y2, s_y2))):
                    g.indirect_dma_start(out=y[b], out_offset=None, in_=y_dram,
                                         in_offset=bass.IndirectOffsetOnAxis(ap=slots[:, k, ti:ti + 1], axis=0)).then_inc(arrived[b], 16)

            for ti in range(AHEAD):
                fetch(ti)
            for ti in range(NT):
                if ti + AHEAD < NT:
                    pl.wait_ge(O_D.sem, O_D.at(ti, "res"))
                    fetch(ti + AHEAD)
                finish(pl, g, ti)

        @block.vector
        def _(dv):
            v = nc.vector

            def own(st, n, name, ins):
                ins.then_inc(st.sem, 1)
                dv.wait_ge(st.sem, st.at(n, name))

            for part in hT:
                v.memset(part[:, :, 0:1], 0.0).then_inc(s_zcol, 1)
            setup = [0]

            def once(ins):
                setup[0] += 1
                ins.then_inc(s_setup, 1)
                dv.wait_ge(s_setup, setup[0])

            for ti in range(NT + 1):
                b, r = ti % 2, rows(ti)
                dv.wait_ge(s_xin[b], 16 * (ti // 2 + 1))
                for hf in range(2):
                    own(s_ln, ti, f"st{hf}", v.bn_stats(out=st6[0:r, hf, :], in_=xb[b][0:r, hf * 512:(hf + 1) * 512]))
                v.bn_aggr(out=mv[0:r, :], in_=st6[0:r, :, :].rearrange("p a b -> p (a b)")).then_inc(s_ln.sem, 1)
                dv.wait_ge(s_std, ti + 1)
                own(s_ln, ti, "rstd", v.reciprocal(rstd[0:r, 1:2], rstd[0:r, 0:1]))
                if ti >= 2:
                    dv.wait_ge(s_tp, 2 * (ti - 1))
                    if ti >= 3:
                        dv.wait_ge(s_hst[b], 16 * ((ti - 1) // 2))
                own(s_ln, ti, "xhat", v.tensor_scalar(xh[b][0:r, :], xb[b][0:r, :], mv[0:r, 0:1], rstd[0:r, 1:2],
                                                      ALU.subtract, ALU.mult))

            def split(n):
                w = cols(*WTILES[n])[1]
                dv.wait_ge(s_whi, n + 1)
                v.scalar_tensor_tensor(out=wbuf[n % 2][1][:, :, 0:w], in0=wraw[n % 2][:, :, 0:w], scalar=W_UP,
                                       in1=wbuf[n % 2][0][:, :, 0:w], op0=ALU.mult, op1=ALU.subtract).then_inc(s_wlo, 1)

            split(0)
            split(1)
            dv.wait_ge(s_tp, 2 * (NT + 1))
            for b in range(2):
                dv.wait_ge(s_hst[b], 16 * (NT // 2))
            v.memset(Z0[:, 0:1], 0.0).then_inc(s_zcol, 1)
            dv.wait_ge(s_prm, 16 * 16)
            dv.wait_ge(s_const_done, 1)
            for q, n in enumerate((P_W0, P_A0, P_BR, P_BI)):
                once(v.tensor_scalar(hprm[:, q, :], prm[:, n, :], 0.5, None, ALU.mult))
            once(v.tensor_scalar(prm[:, P_K1, :], prm[:, P_KA, :], -1.0, 1.0, ALU.mult, ALU.add))
            once(v.tensor_scalar(lamt[:, 0, :], prm[:, P_LAM, :], -1.0, None, ALU.mult))
            once(v.tensor_tensor(lamt[:, 0, :], lamt[:, 0, :], prm[:, P_LAM, :], ALU.min))
            v.tensor_scalar(lamt[:, 5, :], prm[:, P_LAM, :], 0.0, None, ALU.min).then_inc(s_absl, 1)
            dv.wait_ge(s_absl, 1)
            dv.wait_ge(s_expl, 1)
            once(v.tensor_scalar(lamt[:, 2, :], lamt[:, 1, :], 2.0, None, ALU.add))
            once(v.reciprocal(lamt[:, 3, :], lamt[:, 2, :]))
            once(v.tensor_tensor(lamt[:, 2, :], lamt[:, 1, :], lamt[:, 3, :], ALU.mult))
            once(v.tensor_tensor(lamt[:, 3, :], lamt[:, 2, :], lamt[:, 2, :], ALU.mult))
            for q in range(8, -1, -1):
                once(v.tensor_tensor(lamt[:, 4, :], lamt[:, 4, :], lamt[:, 3, :], ALU.mult))
                once(v.tensor_scalar(lamt[:, 4, :], lamt[:, 4, :], 1.0 / (2 * q + 1), None, ALU.add))
            once(v.tensor_tensor(lamt[:, 4, :], lamt[:, 4, :], lamt[:, 2, :], ALU.mult))
            once(v.tensor_scalar(lamt[:, 4, :], lamt[:, 4, :], -2.0, None, ALU.mult))
            once(v.tensor_tensor(lamt[:, 4, :], lamt[:, 4, :], lamt[:, 5, :], ALU.add))
            once(v.tensor_scalar(c8[:, 0, :], lamt[:, 4, :], 8.0, None, ALU.mult))
            v.tensor_scalar(c8[:, 1, :], lamt[:, 4, :], -8.0, None, ALU.mult).then_inc(s_c8, 1)

            def conv(j):
                dv.wait_ge(s_lx, j + 1)
                own(LRU_D, j, "c0", v.tensor_scalar(XC, XL[:, 0:TQ], cw[:, 0, j:j + 1], prm[:, P_CB, j:j + 1], ALU.mult, ALU.add))
                for w in range(1, 4):
                    own(LRU_D, j, f"c{w}", v.scalar_tensor_tensor(out=XC, in0=XL[:, w:w + TQ], scalar=cw[:, w, j:j + 1], in1=XC,
                                                                  op0=ALU.mult, op1=ALU.add))

            def lru(j):
                dv.wait_ge(LRU_A.sem, LRU_A.at(j, "gr"))
                own(LRU_D, j, "gr", v.tensor_scalar(GR, GR, 0.5, 0.5, ALU.mult, ALU.add))
                dv.wait_ge(LRU_A.sem, LRU_A.at(j, "rc"))
                own(LRU_D, j, "m2", v.scalar_tensor_tensor(out=GS, in0=GS, scalar=2.0, in1=LD, op0=ALU.mult, op1=ALU.mult))
                own(LRU_D, j, "gi", v.tensor_scalar(GI, GI, 0.5, 0.5, ALU.mult, ALU.add))
                own(LRU_D, j, "ga", v.tensor_tensor(GI, GI, XC, ALU.mult))
                dv.wait_ge(LRU_A.sem, LRU_A.at(j, "sq"))
                own(LRU_D, j, "gb", v.tensor_tensor(GI, GI, GS, ALU.mult))
                own(LRU_D, j, "scan", v.tensor_tensor_scan(out=LD[:, 1:TQ], data0=LA[:, 1:TQ], data1=GI[:, 1:TQ], initial=0.0,
                                                           op0=ALU.mult, op1=ALU.add))
                if j:
                    dv.wait_ge(s_yst, 16 * j)
                own(LRU_D, j, "y", v.tensor_tensor(YL, LD[:, XQ:TQ], GG[:, j, 64:TP], ALU.mult))

            nsh = [0]

            def shift(kind, j):
                n = nsh[0]
                nsh[0] += 1
                r = cols(kind, j)[1]
                q = {"r": j, "k": 4 + j, "v": 8 + j, "z": 12 + j}[kind]
                dv.wait_ge(s_udif, n + 1)
                dst = shifted(kind, j)
                v.scalar_tensor_tensor(out=dst, in0=dst, scalar=mu[0:r, q:q + 1], in1=UB[0:r, n % 2, 1:TQ],
                                       op0=ALU.mult, op1=ALU.add).then_inc(s_ush, 1)
                dv.wait_ge(s_ush, n + 1)

            def pair(p, part):
                jb = J
                kt = KT[:, p, Q0:TP]
                if part == 0:
                    dv.wait_ge(PR_A.sem, PR_A.at(p, "sg"))
                    own(PR_D, p, "sg", v.tensor_scalar(SG, SG, 0.5, 0.5, ALU.mult, ALU.add))
                    own(PR_D, p, "cs", v.tensor_tensor_scan(out=CS, data0=reset, data1=SG, initial=0.0, op0=ALU.mult, op1=ALU.add))
                    own(PR_D, p, "csx", v.tensor_tensor(SG, CS, SG, ALU.subtract))
                    dv.wait_ge(PR_A.sem, PR_A.at(p, "a"))
                    own(PR_D, p, "a", v.tensor_scalar(AA, AA, 0.5, 0.5, ALU.mult, ALU.add))
                    dv.wait_ge(s_z0, 5)
                    own(PR_D, p, "kk", v.tensor_scalar(KK, kt, prm[:, P_KK, p:p + 1], None, ALU.mult))
                if part == 1:
                    dv.wait_ge(s_job, jb[("ss", p)] + 1)
                    own(PR_D, p, "ssm", v.tensor_scalar(seg3(T7), bank(("ss", p)), 1e-24, None, ALU.max))
                    dv.wait_ge(PR_A.sem, PR_A.at(p, "rt"))
                    own(PR_D, p, "kkn", v.tensor_tensor(KK, KK, T7, ALU.mult))
                    own(PR_D, p, "kc", v.tensor_scalar(T7, AA, prm[:, P_KA, p:p + 1], prm[:, P_K1, p:p + 1], ALU.mult, ALU.add))
                    own(PR_D, p, "k2", v.tensor_tensor(kt, kt, T7, ALU.mult))
                    own(PR_D, p, "q", v.scalar_tensor_tensor(out=T7, in0=AR[:, p, 1, Q0:TP], scalar=prm[:, P_RK, p:p + 1], in1=kt,
                                                             op0=ALU.mult, op1=ALU.mult))
                if part == 2:
                    dv.wait_ge(s_job, jb[("bon", p)] + 1)
                    own(PR_D, p, "bon", v.tensor_tensor(seg3(BON[:, p, :]), bank(("bon", p)), seg3(VT[:, p, Q0:TP]), ALU.mult))
                    own(PR_D, p, "b0", v.tensor_tensor(AA, AA, KK, ALU.mult))
                    dv.wait_ge(PR_A.sem, PR_A.at(p, "iw"))
                    own(PR_D, p, "b", v.tensor_tensor(BT[:, p, Q0:TP], AA, E1, ALU.mult))
                    own(PR_D, p, "k", v.tensor_tensor(kt, kt, E1, ALU.mult))
                    dv.wait_ge(PR_A.sem, PR_A.at(p, "w"))
                    own(PR_D, p, "r", v.tensor_tensor(AR[:, p, 1, Q0:TP], AR[:, p, 1, Q0:TP], E1, ALU.mult))
                    dv.wait_ge(PR_A.sem, PR_A.at(p, "wx"))
                    own(PR_D, p, "at", v.scalar_tensor_tensor(out=AR[:, p, 0, Q0:TP], in0=KK, scalar=-1.0, in1=SG,
                                                              op0=ALU.mult, op1=ALU.mult))
            for job in JOBS:
                kind, j = job
                if job in WTILES and WTILES.index(job) + 2 < len(WTILES):
                    split(WTILES.index(job) + 2)
                if kind == "lx" and j == 0:
                    conv(0)
                if kind == "gi":
                    lru(j)
                    if j < 3:
                        conv(j + 1)
                if kind in ("r", "k", "v", "z"):
                    shift(kind, j)
                    if job == ("z", 2):
                        for q, r in ((0, P), (1, 32)):
                            dv.wait_ge(s_zact, 2 + q)
                            v.tensor_scalar(ZG[0:r, q, :], ZG[0:r, q, :], 0.5, 0.5, ALU.mult, ALU.add).then_inc(s_zg, 1)
                if kind == "aa":
                    pair(j, 0)
                if kind == "ss":
                    pair(j, 1)
                if kind == "bon":
                    pair(j, 2)

            def masked(out_, in_, mask):
                return v.tensor_tensor(out_, in_, mask, ALU.mult)

            def st(m):
                return m.rearrange("p (o c) -> p o c", o=1).to_broadcast([P, PAIRS, HEAD])

            def bd(m):
                return m.rearrange("p (o h) c -> p o h c", o=1).to_broadcast([P, PAIRS, 2, HEAD])

            def dup(x4):
                return x4.rearrange("p a (o c) -> p a o c", o=1).to_broadcast([P, PAIRS, 2, HEAD])

            def quad(b0):
                return ps[:, b0, 0:512].rearrange("p (a h c) -> p a h c", h=2, c=HEAD)

            def solve_start(s, n):
                d, B, cd = slot[s], 4 * s, CD[s]
                dv.wait_ge(CM[s].sem, CM[s].at(n, "MB"))
                own(cd, n, "T0a", masked(d["Tb"], dup(quad(B)[:, :, 0, :]), bd(m_supT)))
                own(cd, n, "T0", v.tensor_tensor(d["Tb"], d["Tb"], bd(ident.rearrange("p (h c) -> p h c", c=HEAD)), ALU.add))
                own(cd, n, "Mb", masked(d["Mb"], dup(quad(B)[:, :, 0, :]), bd(m_strict)))
                own(cd, n, "Mr", masked(d["RB"][:, :, 0, :], quad(B)[:, :, 1, :], st(m_incl)))

            def k_masks(s, n):
                d, B, cd = slot[s], 4 * s, CD[s]
                dv.wait_ge(CM[s].sem, CM[s].at(n, "MK"))
                own(cd, n, "Nb", masked(d["Nb"], dup(quad(B + 1)[:, :, 0, :]), bd(m_strict)))
                own(cd, n, "Mk", masked(d["RK"][:, :, 0, :], quad(B + 1)[:, :, 1, :], st(m_incl)))

            def level_p(s, n, l):
                d, B, cd = slot[s], 4 * s, CD[s]
                dv.wait_ge(CE[s].sem, CE[s].at(n, f"P{l}"))
                own(cd, n, f"P{l}", masked(d["Pb"], quad(B), bd(m_sub[:, l, :, :])))

            def level_d(s, n, l):
                d, B, cd = slot[s], 4 * s, CD[s]
                if l < LV[-1]:
                    dv.wait_ge(CE[s].sem, CE[s].at(n, f"DP{l}"))
                    own(cd, n, f"D{l + 1}", v.tensor_tensor(d["Db"], d["Db"], quad(B + 1), ALU.add))
                else:
                    dv.wait_ge(CE[s].sem, CE[s].at(n, "PD"))
                    own(cd, n, f"T{l + 1}", v.tensor_tensor(d["Tb"], d["Tb"], quad(B + 1), ALU.add))

            def through(s, n, c):
                d, B, cd = slot[s], 4 * s, CD[s]
                dv.wait_ge(CE[s].sem, CE[s].at(n, "QG"))
                own(cd, n, "G", v.tensor_tensor(d["QG"][:, :, 1, :], quad(B + 1)[:, :, 1, :], st(ident2), ALU.add))
                own(cd, n, "Q", v.tensor_tensor(d["QG"][:, :, 0, :], quad(B + 1)[:, :, 0, :],
                                                AR[:, :, 1, bass.ds(c * CH, CH)], ALU.add))

            def state_t(s, n):
                dv.wait_ge(CE[s].sem, CE[s].at(n, "YS"))
                own(CD[s], n, "S", masked(slot[s]["Sb"], dup(quad(4 * s + 3)[:, :, 1, :]), bd(blk)))

            def state(s, n, c):
                dv.wait_ge(CE[s].sem, CE[s].at(n, "St"))
                own(CB[s], n, "SB", v.tensor_tensor(
                    SB[1 - s].rearrange("p a h c -> p a (h c)"), ps[:, 4 * s + 2, :].rearrange("p (a x) -> p a x", a=PAIRS),
                    wc[:, :, bass.ds(c, 1)].to_broadcast([P, PAIRS, P]), ALU.mult))

            def turn(slots_, n, c):
                if 1 in slots_:
                    solve_start(1, n)
                if not first(n):
                    state(1, n - 1, c - 1)
                if 1 in slots_:
                    k_masks(1, n)
                for l in LV:
                    for s in slots_:
                        level_p(s, n, l)
                    for s in slots_:
                        level_d(s, n, l)
                for k, s in enumerate(slots_):
                    through(s, n, c + k)
                if 1 in slots_:
                    state_t(0, n)
                    state(0, n, c)
                    solve_start(0, n + 1)
                    k_masks(0, n + 1)
                    state_t(1, n)

            solve_start(0, 0)
            k_masks(0, 0)
            turn((0, 1), 0, 0)
            with dv.Fori(1, (NCH - 1) // 2) as i:
                turn((0, 1), i, i * 2)
            turn((0,), (NCH - 1) // 2, NCH - 1)

            dv.wait_ge(CA[0].sem, CA[0].at((NCH - 1) // 2, "Y"))
            dv.wait_ge(CA[1].sem, CA[1].at((NCH - 1) // 2 - 1, "Y"))
            def half_pair(n):
                return AR[:, n // 2, 1, CH + (n % 2) * 512:CH + (n % 2) * 512 + 512]

            def centre(n):
                dv.wait_ge(GN_M, n + 1)
                y = half_pair(n)
                v.scalar_tensor_tensor(out=y, in0=ps[:, 4 * (n % 2), :], scalar=-1.0 / HEAD, in1=y,
                                       op0=ALU.mult, op1=ALU.add).then_inc(GN_C, 1)
                dv.wait_ge(GN_C, n + 1)

            centre(0)
            for n in range(2 * PAIRS):
                if n + 1 < 2 * PAIRS:
                    centre(n + 1)
                p, hf = n // 2, n % 2
                y = half_pair(n)
                dv.wait_ge(GN_A.sem, GN_A.at(n, "rs"))
                own(GN_D, n, "n", v.tensor_tensor(y, y, gsd[n % 2], ALU.mult))
                own(GN_D, n, "aff", v.tensor_scalar(y, y, prm[:, P_GG, p:p + 1], prm[:, P_GB, p:p + 1], ALU.mult, ALU.add))
                own(GN_D, n, "bon", v.tensor_tensor(y, y, BON[:, p, XQ + hf * 512:XQ + hf * 512 + 512], ALU.add))
                dv.wait_ge(GN_G, n + 1)
                own(GN_D, n, "g", v.tensor_tensor(y, y, ps[:, 4 * (n % 2) + 2, :], ALU.mult))

            rt = [0]

            def r_(ins):
                rt[0] += 1
                ins.then_inc(s_rt, 1)
                dv.wait_ge(s_rt, rt[0])

            def route(ti):
                dv.wait_ge(F_E.sem, F_E.at(ti, "lg"))
                v.tensor_tensor(lg[:, ti, :], ps[:, 6, 0:NG + NE], br, ALU.add).then_inc(F_L, 1)
                dv.wait_ge(F_L, ti + 1)
                r_(v.tensor_copy(g8[:, 0:NG], lg[:, ti, 0:NG]))
                r_(v.max(gm8, g8))
                r_(v.max_index(gi8, gm8, g8))
                r_(v.tensor_copy(gi8f, gi8))
                r_(v.tensor_scalar(ohg, i4[:, 0:NG], gi8f[:, 0:1], None, ALU.is_equal))
                r_(v.tensor_tensor(esel, lg[:, ti, NG:NG + NE].rearrange("p (g e) -> p g e", e=EPG),
                                   ohg.rearrange("p (g o) -> p g o", o=1).to_broadcast([P, NG, EPG]), ALU.mult))
                r_(v.tensor_tensor(e8, esel[:, 0, :], esel[:, 1, :], ALU.add))
                r_(v.tensor_tensor(e8, e8, esel[:, 2, :], ALU.add))
                r_(v.tensor_tensor(e8, e8, esel[:, 3, :], ALU.add))
                r_(v.max(tm8, e8))
                r_(v.max_index(ti8, tm8, e8))
                r_(v.tensor_copy(ti8f, ti8))
                r_(v.tensor_scalar(sm[:, 0:1], gi8f[:, 0:1], float(EPG), None, ALU.mult))
                for k in range(2):
                    r_(v.tensor_tensor(eidf[:, k, ti:ti + 1], sm[:, 0:1], ti8f[:, k:k + 1], ALU.add))
                    r_(v.tensor_scalar(OH[k][:, ti, :], i4, eidf[:, k, ti:ti + 1], None, ALU.is_equal))
                r_(v.tensor_scalar(lg[:, ti, 0:NG], lg[:, ti, 0:NG], gm8[:, 0:1], None, ALU.subtract))
                arg = v.tensor_tensor(lg[:, ti, NG:NG + 1], tm8[:, 1:2], tm8[:, 0:1], ALU.subtract)
                if ti < NT - 1:
                    r_(arg)
                else:
                    arg.then_inc(s_rt_arg, 1)

            dv.wait_ge(s_rtc, 5)
            r_(v.memset(g8, -3.0e38))
            for ti in range(NT):
                b = ti % 2
                dv.wait_ge(F_H.sem, F_H.at(ti, "bias"))
                for hf in range(2):
                    dv.wait_ge(F_O.sem, F_O.at(ti, f"o{hf}"))
                    cs = slice(hf * 512, (hf + 1) * 512)
                    own(F_D, ti, f"res{hf}", v.scalar_tensor_tensor(out=zb[b][:, cs], in0=hb[b][:, cs], scalar=ALPHA,
                                                                    in1=ps[:, 2 * b + hf, :], op0=ALU.mult, op1=ALU.add))
                for hf in range(2):
                    own(F_D, ti, f"st{hf}", v.bn_stats(out=st6[:, hf, :], in_=zb[b][:, hf * 512:(hf + 1) * 512]))
                v.bn_aggr(out=mv, in_=st6.rearrange("p a b -> p (a b)")).then_inc(F_D.sem, 1)
                dv.wait_ge(F_A, ti + 1)
                own(F_D, ti, "rstd", v.reciprocal(rstd[:, 1:2], rstd[:, 0:1]))
                if ti >= 2:
                    dv.wait_ge(s_h1st[b], 16 * (ti // 2))
                    dv.wait_ge(F_E.sem, F_E.at(ti - 2, "t1"))
                own(F_D, ti, "xhat", v.tensor_scalar(h1[b], zb[b], mv[:, 0:1], rstd[:, 1:2], ALU.subtract, ALU.mult))
                if ti:
                    route(ti - 1)
            route(NT - 1)


            r_(v.tensor_tensor(OS, OH[0], OH[1], ALU.add))
            r_(v.memset(OP[:, 0, :], 0.0))
            for ti in range(NT - 1):
                r_(v.tensor_tensor(OP[:, ti + 1, :], OP[:, ti, :], OS[:, ti, :], ALU.add))
            v.tensor_tensor(OP[:, NT, :], OP[:, NT - 1, :], OS[:, NT - 1, :], ALU.add).then_inc(s_rt_oh, 1)
            dv.wait_ge(s_rta, 1)
            r_(v.reduce_sum(s1t[:, 0, :], lg[:, :, 0:NG], axis=AXX))
            r_(v.tensor_scalar(s1t[:, 1, :], lg[:, :, NG], 1.0, None, ALU.add))
            r_(v.tensor_tensor(s1t[:, 0, :], s1t[:, 0, :], s1t[:, 1, :], ALU.mult))
            r_(v.reciprocal(gates[:, 0, :], s1t[:, 0, :]))
            r_(v.tensor_tensor(gates[:, 1, :], gates[:, 0, :], lg[:, :, NG], ALU.mult))
            dv.wait_ge(s_rte, 1)
            r_(v.tensor_copy(RK.rearrange("p a b -> p (a b)"), ps[:, 0, 0:NT * NE]))
            r_(v.tensor_copy(cnt, ps[:, 1, 0:NE]))
            r_(v.tensor_tensor(c7, cnt.rearrange("p (e o) -> p e o", o=1).to_broadcast([P, NE, 7]),
                               th7.rearrange("p (o m) -> p o m", o=1).to_broadcast([P, NE, 7]), ALU.is_gt))
            r_(v.reduce_sum(ovb, c7, axis=AXX))
            r_(v.tensor_tensor_scan(out=ovi, data0=ones[:, 0:NE], data1=ovb, initial=0.0, op0=ALU.mult, op1=ALU.add))
            r_(v.tensor_tensor(ove, ovi, ovb, ALU.subtract))
            for k in range(2):
                r_(v.tensor_tensor(t32, OH[k], RK, ALU.mult))
                r_(v.reduce_sum(rk[:, k, :], t32, axis=AXX))
                r_(v.tensor_tensor(t32, OH[k], ove.rearrange("p (o e) -> p o e", o=1).to_broadcast([P, NT, NE]), ALU.mult))
                r_(v.reduce_sum(ovs[:, k, :], t32, axis=AXX))
            rkf, qf = rk.rearrange("p k t -> p (k t)"), qk.rearrange("p k t -> p (k t)")
            ovf, ef = ovs.rearrange("p k t -> p (k t)"), eidf.rearrange("p k t -> p (k t)")
            r_(v.tensor_tensor(q7, rkf.rearrange("p (n o) -> p n o", o=1).to_broadcast([P, 2 * NT, 7]),
                               th7.rearrange("p (o m) -> p o m", o=1).to_broadcast([P, 2 * NT, 7]), ALU.is_ge))
            r_(v.reduce_sum(qf, q7, axis=AXX))
            r_(v.tensor_tensor(ovf, ovf, qf, ALU.add))
            r_(v.tensor_scalar(ovf, ovf, float(NE - 1), None, ALU.add))
            r_(v.tensor_tensor(ovf, ovf, ef, ALU.subtract))
            s1f = s1t.rearrange("p k t -> p (k t)")
            r_(v.tensor_scalar(s1f, qf, 0.0, None, ALU.is_gt))
            r_(v.tensor_tensor(ovf, ovf, s1f, ALU.mult))
            r_(v.tensor_tensor(ovf, ovf, ef, ALU.add))
            r_(v.tensor_tensor(ovf, ovf, qf, ALU.subtract))
            r_(v.scalar_tensor_tensor(out=ovf, in0=ovf, scalar=float(P), in1=rkf, op0=ALU.mult, op1=ALU.add))
            r_(v.tensor_copy(slots.rearrange("p k t -> p (k t)"), ovf))
            r_(v.tensor_tensor(o16, ovi.rearrange("p (o e) -> p o e", o=1).to_broadcast([P, OVER, NE]),
                               j16.rearrange("p (j o) -> p j o", o=1).to_broadcast([P, OVER, NE]), ALU.is_le))
            r_(v.reduce_sum(oef, o16, axis=AXX))
            r_(v.tensor_scalar(oef, oef, float(NE - 1), None, ALU.min))
            r_(v.tensor_copy(oei, oef))
            v.tensor_copy(novi, ovi[:, NE - 1:NE]).then_inc(s_rt_done, 1)

            def rest(s, n, k):
                dv.wait_ge(s_hi[k], n + 1)
                v.tensor_tensor(wsp[s][k][1], raw[k], wsp[s][k][0], ALU.subtract).then_inc(s_lo[k], 1)

            def rows_in(s, n):
                dv.wait_ge(A_X, n + 1)
                v.tensor_tensor(xT[s][1], ps[:, 0:2, :].rearrange("p b (k c) -> p (b k) c", c=P), xT[s][0],
                                ALU.subtract).then_inc(V_X, 1)

            def product(s, n):
                dv.wait_ge(A_S, n + 1)
                dv.wait_ge(E_U, n + 1)
                v.tensor_tensor(hd[s], hs[s], ps[:, 3, :], ALU.mult).then_inc(V_M, 1)

            def hidden(s, n):
                dv.wait_ge(A_H, n + 1)
                v.tensor_tensor(hTe[s][1], ps[:, 4, :].rearrange("p (k c) -> p k c", c=P), hTe[s][0],
                                ALU.subtract).then_inc(V_H, 1)

            def yout(s, n):
                dv.wait_ge(E_Y, n + 1)
                if not (isinstance(n, int) and n < 2):
                    dv.wait_ge(s_yo[s], (n - s) * 8)
                v.tensor_copy(yb[s][:, 512:1024], ps[:, 6, :]).then_inc(V_Y, 1)

            def turn(s, n, more=True):
                if more:
                    rest(1 - s, n + 1, 0)
                if not first(n):
                    hidden(1 - s, n - 1)
                if more:
                    rows_in(1 - s, n + 1)
                    rest(1 - s, n + 1, 1)
                product(s, n)
                if more:
                    rest(1 - s, n + 1, 2)
                if not first(n):
                    yout(1 - s, n - 1)

            for k in range(3):
                rest(0, 0, k)
            rows_in(0, 0)
            turn(0, 0)
            turn(1, 1)
            with dv.Fori(1, NE // 2 - 1) as i:
                turn(0, i * 2)
                turn(1, i * 2 + 1)
            turn(0, NE - 2)
            turn(1, NE - 1, False)
            hidden(1, NE - 1)
            yout(1, NE - 1)
            n_over = dv.value_load(novi[0:1, 0:1], min_val=0, max_val=OVER)
            for j in range(OVER):
                with dv.If(n_over > j):
                    s, n = j % 2, NE + j
                    rows_in(s, n)
                    for k in range(3):
                        rest(s, n, k)
                    product(s, n)
                    hidden(s, n)
                    yout(s, n)

            for ti in range(NT):
                b = ti % 2
                q = ti % AHEAD
                dv.wait_ge(O_S, ti + 1)
                dv.wait_ge(s_y2[q], 16 * (ti // AHEAD + 1))
                own(O_D, ti, "y2", v.scalar_tensor_tensor(out=y1[q], in0=y2[q], scalar=gates[:, 1, ti:ti + 1], in1=y1[q],
                                                          op0=ALU.mult, op1=ALU.add))
                dv.wait_ge(s_hr[q], 16 * (ti // AHEAD + 1))
                own(O_D, ti, "res", v.scalar_tensor_tensor(out=hr[q], in0=hr[q], scalar=ALPHA, in1=y1[q], op0=ALU.mult, op1=ALU.add))
                for hf in range(2):
                    own(O_D, ti, f"st{hf}", v.bn_stats(out=st6[:, hf, :], in_=hr[q][:, hf * 512:(hf + 1) * 512]))
                v.bn_aggr(out=mv, in_=st6.rearrange("p a b -> p (a b)")).then_inc(O_D.sem, 1)
                dv.wait_ge(O_A, ti + 1)
                own(O_D, ti, "rstd", v.reciprocal(rstd[:, 1:2], rstd[:, 0:1]))
                if ti >= 2:
                    dv.wait_ge(s_out[b], 16 * (ti // 2))
                own(O_D, ti, "xhat", v.tensor_scalar(o_x[b], hr[q], mv[:, 0:1], rstd[:, 1:2], ALU.subtract, ALU.mult))

        @block.scalar
        def _(ac):
            f = nc.scalar.activation

            def copy_t(ti):
                b, r = ti % 2, rows(ti)
                c0 = 1 if ti == 0 else XQ + (ti - 1) * P
                if ti == 0:
                    ac.wait_ge(s_lnp, 32)
                if ti >= 2:
                    ac.wait_ge(s_hl, ti - 1)
                for k in range(KD):
                    if k % 4 == 0:
                        ac.wait_ge(s_tp, 2 * ti + k // 4 + 1)
                    f(ht32[b][:, k, 0:r], ps[:, 2 * b + k // 4, (k % 4) * P:(k % 4) * P + r], ACT.Identity,
                      scale=ln0c[:, 0, k:k + 1], bias=ln0c[:, 1, k:k + 1]).then_inc(s_hf, 1)
                ac.wait_ge(s_hf, KD * (ti + 1))
                f(hT[0][:, :, c0:c0 + r], ht32[b][:, :, 0:r], ACT.Copy).then_inc(s_ht, 1)

            def split(n):
                w = cols(*WTILES[n])[1]
                ac.wait_ge(s_w[n % 2], 16 * (n // 2 + 1))
                if n >= 2:
                    ac.wait_ge(s_job, J[WTILES[n - 2]] + 1)
                f(wbuf[n % 2][0][:, :, 0:w], wraw[n % 2][:, :, 0:w], ACT.Copy, scale=W_UP).then_inc(s_whi, 1)

            for ti in range(NT + 1):
                r = rows(ti)
                ac.wait_ge(s_ln.sem, s_ln.at(ti, "agg"))
                if ti == 0:
                    ac.wait_ge(s_const, 4)
                f(rstd[0:r, 0:1], mv[0:r, 1:2], ACT.Sqrt, bias=eps[0:r, 0:1]).then_inc(s_std, 1)
                if ti:
                    copy_t(ti - 1)
            copy_t(NT)
            split(0)
            split(1)
            ac.wait_ge(s_absl, 1)
            f(lamt[:, 1, :], lamt[:, 0, :], ACT.Exp).then_inc(s_expl, 1)

            nsh = [0]
            for job in JOBS:
                kind, j = job
                if kind in ("ss", "bon"):
                    continue
                ac.wait_ge(s_job, J[job] + 1)
                if job in WTILES and WTILES.index(job) + 2 < len(WTILES):
                    split(WTILES.index(job) + 2)
                if kind == "gl":
                    f(seg3(GG[:, j, Q0:TP]), bank(job), ACT.Gelu_apprx_tanh, scale=1 / W_UP).then_inc(s_gelu, 1)
                if kind == "lx":
                    if j == 0:
                        ac.wait_ge(s_const_done, 1)
                    if j:
                        ac.wait_ge(LRU_D.sem, LRU_D.at(j - 1, "c3"))
                    f(seg3(XL[:, 3:3 + TQ]), bank(job), ACT.Copy, scale=1 / W_UP).then_inc(s_lx, 1)
                if kind == "gr":
                    if j:
                        ac.wait_ge(LRU_D.sem, LRU_D.at(j - 1, "scan"))
                    f(seg3(GR), bank(job), ACT.Tanh, bias=hprm[:, 2, j:j + 1], scale=0.5).then_inc(LRU_A.sem, 1)
                if kind == "gi":
                    f(seg3(GI), bank(job), ACT.Tanh, bias=hprm[:, 3, j:j + 1], scale=0.5).then_inc(LRU_A.sem, 1)
                    ac.wait_ge(LRU_D.sem, LRU_D.at(j, "gr"))
                    ac.wait_ge(s_c8, 1)
                    f(LA, GR, ACT.Exp, scale=c8[:, 0, j:j + 1]).then_inc(LRU_A.sem, 1)
                    f(GS, GR, ACT.Tanh, scale=c8[:, 1, j:j + 1]).then_inc(LRU_A.sem, 1)
                    ac.wait_ge(LRU_A.sem, LRU_A.at(j, "gs"))
                    f(LD, GS, ACT.Ln, bias=ones[:, 0:1]).then_inc(LRU_A.sem, 1)
                    ac.wait_ge(LRU_A.sem, LRU_A.at(j, "ln"))
                    f(LD, LD, ACT.Exp, scale=-1.0).then_inc(LRU_A.sem, 1)
                    ac.wait_ge(LRU_D.sem, LRU_D.at(j, "m2"))
                    f(GS, GS, ACT.Sqrt).then_inc(LRU_A.sem, 1)
                if kind in ("z", "r", "k", "v"):
                    n = nsh[0]
                    nsh[0] += 1
                    r = cols(kind, j)[1]
                    if n >= 2:
                        ac.wait_ge(s_ush, n - 1)
                    f(seg3(UB[0:r, n % 2, :]), bank(job, r), ACT.Copy, scale=1 / W_UP).then_inc(s_uev, 1)
                    if kind == "z":
                        ac.wait_ge(s_ush, n + 1)
                        if j == 0:
                            ac.wait_ge(s_zcol, 3)
                            f(Z0[0:64, :], Z0[0:64, :], ACT.Tanh).then_inc(s_zact, 1)
                        if j == 1:
                            f(ZG[:, 0, :], ZG0[:, XQ:TQ], ACT.Tanh, scale=0.5).then_inc(s_zact, 1)
                        if j == 2:
                            f(ZG[0:32, 1, :], XC[0:32, XQ:TQ], ACT.Tanh, scale=0.5).then_inc(s_zact, 1)
                if kind == "dec":
                    if j:
                        ac.wait_ge(PR_D.sem, PR_D.at(j - 1, "at"))
                    f(seg3(SG), bank(job), ACT.Tanh, bias=hprm[:, 0, j:j + 1], scale=0.5).then_inc(PR_A.sem, 1)
                if kind == "aa":
                    f(seg3(AA), bank(job), ACT.Tanh, bias=hprm[:, 1, j:j + 1], scale=0.5).then_inc(PR_A.sem, 1)
                    ac.wait_ge(PR_D.sem, PR_D.at(j, "kk"))
                    f(T7, KK, ACT.Square).then_inc(PR_A.sem, 1)
                    f(E1, CS, ACT.Exp, scale=DECAY).then_inc(PR_A.sem, 1)
                nxt = JOBS[J[job] + 1] if J[job] + 1 < len(JOBS) else None
                while nxt and nxt[0] in ("ss", "bon"):
                    p = nxt[1]
                    if nxt[0] == "ss":
                        ac.wait_ge(PR_D.sem, PR_D.at(p, "ssm"))
                        f(T7, T7, ACT.Ln).then_inc(PR_A.sem, 1)
                        ac.wait_ge(PR_A.sem, PR_A.at(p, "ln"))
                        f(T7, T7, ACT.Exp, scale=-0.5).then_inc(PR_A.sem, 1)
                    else:
                        f(wc[:, p, :], CS[:, HEAD - 1 - Q0:TQ:CH], ACT.Exp, scale=-DECAY).then_inc(PR_A.sem, 1)
                        f(SG, SG, ACT.Exp, scale=-DECAY).then_inc(PR_A.sem, 1)
                        ac.wait_ge(PR_D.sem, PR_D.at(p, "k"))
                        f(E1, CS, ACT.Exp, scale=-DECAY).then_inc(PR_A.sem, 1)
                    nxt = JOBS[J[nxt] + 1] if J[nxt] + 1 < len(JOBS) else None

            def quad(b0):
                return ps[:, b0, :].rearrange("p (a h c) -> p a h c", h=2, c=HEAD)

            def turn(slots_, n, c):
                def take(s, step, dst, src, when=None):
                    ac.wait_ge(CE[s].sem, CE[s].at(n, when or step))
                    f(dst, src, ACT.Copy).then_inc(CA[s].sem, 1)

                def blocks(s, step, dst_of, src_of, when=None):
                    ac.wait_ge(CE[s].sem, CE[s].at(n, when or step))
                    for h in range(2):
                        rws = slice(h * HEAD, (h + 1) * HEAD)
                        last = f(dst_of(rws, h), src_of(rws, h), ACT.Copy)
                    last.then_inc(CA[s].sem, 1)

                def diagonal(m):
                    return lambda rws, h: m[rws, :, h, :]

                def column(m, k):
                    return lambda rws, h: m[rws, :, k, :]

                for s in slots_:
                    take(s, "D0", slot[s]["Db"], quad(4 * s + 3))
                for l in LV:
                    if l:
                        for s in slots_:
                            take(s, f"T{l}", slot[s]["Tb"], quad(4 * s + 2))
                    for s in slots_:
                        d, from_ = slot[s], quad(4 * s + 3)
                        if l == 0:
                            take(s, "Vt", d["Vtb"], from_)
                        else:
                            name, to = (None, ("Bt", column(d["RB"], 1)), ("NV", column(d["AN"], 1)),
                                        ("Kt", column(d["RK"], 1)), ("At", column(d["AN"], 0)))[l]
                            blocks(s, name, to, diagonal(from_))
                if first(n):
                    ac.wait_ge(s_z0, 10)
                for s in slots_:
                    blocks(s, "X", diagonal(slot[s]["Xb"]), column(quad(4 * s), 0), "XZ")
                    blocks(s, "Z", diagonal(slot[s]["Zb"]), column(quad(4 * s), 1), "XZ")
                for k, s in enumerate(slots_):
                    if 1 in slots_:
                        ac.wait_ge(CD[s].sem, CD[s].at(n, "S"))
                    take(s, "Y", AR[:, :, 1, bass.ds((c + k) * CH, CH)], quad(4 * s + 3)[:, :, 0, :], "YS")

            turn((0, 1), 0, 0)
            with ac.Fori(1, (NCH - 1) // 2) as i:
                turn((0, 1), i, i * 2)
            turn((0,), (NCH - 1) // 2, NCH - 1)

            def squares(n):
                ac.wait_ge(GN_C, n + 1)
                f(gsq[n % 2], AR[:, n // 2, 1, CH + (n % 2) * 512:CH + (n % 2) * 512 + 512], ACT.Square).then_inc(GN_S, 1)

            squares(0)
            for n in range(2 * PAIRS):
                if n + 1 < 2 * PAIRS:
                    squares(n + 1)
                ac.wait_ge(GN_V, n + 1)
                if n >= 2:
                    ac.wait_ge(GN_D.sem, GN_D.at(n - 2, "n"))
                f(gsd[n % 2], ps[:, 4 * (n % 2) + 1, :], ACT.Ln, scale=1.0 / HEAD, bias=eps[:, 1:2]).then_inc(GN_A.sem, 1)
                ac.wait_ge(GN_A.sem, GN_A.at(n, "ln"))
                f(gsd[n % 2], gsd[n % 2], ACT.Exp, scale=-0.5).then_inc(GN_A.sem, 1)

            def copy_h(ti):
                for hf in range(2):
                    ac.wait_ge(F_E.sem, F_E.at(ti, f"t{hf}"))
                    f(h1T[ti % 2][:, 4 * hf:4 * hf + 4, :], ps[:, 4 + hf, :].rearrange("p (k c) -> p k c", c=P),
                      ACT.Copy).then_inc(F_C.sem, 1)

            for ti in range(NT):
                if ti:
                    copy_h(ti - 1)
                ac.wait_ge(F_D.sem, F_D.at(ti, "agg"))
                f(rstd[:, 0:1], mv[:, 1:2], ACT.Sqrt, bias=eps[:, 0:1]).then_inc(F_A, 1)
            copy_h(NT - 1)
            ac.wait_ge(s_rt_arg, 1)
            f(lg[:, :, 0:NG + 1], lg[:, :, 0:NG + 1], ACT.Exp).then_inc(s_rta, 1)

            def head(s, n, k):
                ac.wait_ge(s_we[k], n * 16 + 16)
                if not (isinstance(n, int) and n < 2):
                    ac.wait_ge((E_G, E_U, E_Y)[k], n - 1)
                f(wsp[s][k][0], raw[k], ACT.Copy).then_inc(s_hi[k], 1)

            def rows_in(s, n):
                ac.wait_ge(E_X, n + 1)
                f(xT[s][0], ps[:, 0:2, :].rearrange("p b (k c) -> p (b k) c", c=P), ACT.Copy).then_inc(A_X, 1)

            def silu(s, n):
                ac.wait_ge(E_G, n + 1)
                f(hs[s], ps[:, 2, :], ACT.Silu).then_inc(A_S, 1)

            def hidden(s, n):
                ac.wait_ge(E_H, n + 1)
                f(hTe[s][0], ps[:, 4, :].rearrange("p (k c) -> p k c", c=P), ACT.Copy).then_inc(A_H, 1)

            def yout(s, n):
                ac.wait_ge(E_Y, n + 1)
                if not (isinstance(n, int) and n < 2):
                    ac.wait_ge(s_yo[s], (n - s) * 8)
                f(yb[s][:, 0:512], ps[:, 5, :], ACT.Copy).then_inc(A_Y, 1)

            def turn(s, n, more=True):
                if more:
                    head(1 - s, n + 1, 0)
                silu(s, n)
                if not first(n):
                    hidden(1 - s, n - 1)
                if more:
                    rows_in(1 - s, n + 1)
                    head(1 - s, n + 1, 1)
                    head(1 - s, n + 1, 2)
                if not first(n):
                    yout(1 - s, n - 1)

            ac.wait_ge(F_L, NT)
            for b in range(2):
                ac.wait_ge(s_h1st[b], 16 * 4)
            for k in range(3):
                head(0, 0, k)
            rows_in(0, 0)
            turn(0, 0)
            turn(1, 1)
            with ac.Fori(1, NE // 2 - 1) as i:
                turn(0, i * 2)
                turn(1, i * 2 + 1)
            turn(0, NE - 2)
            turn(1, NE - 1, False)
            hidden(1, NE - 1)
            yout(1, NE - 1)
            n_over = ac.value_load(novi[0:1, 0:1], min_val=0, max_val=OVER)
            for j in range(OVER):
                with ac.If(n_over > j):
                    s, n = j % 2, NE + j
                    rows_in(s, n)
                    for k in range(3):
                        head(s, n, k)
                    silu(s, n)
                    hidden(s, n)
                    yout(s, n)

            def gated(ti):
                q = ti % AHEAD
                ac.wait_ge(s_y1[q], 16 * (ti // AHEAD + 1))
                f(y1[q], y1[q], ACT.Copy, scale=gates[:, 0, ti:ti + 1]).then_inc(O_S, 1)

            gated(0)
            for ti in range(NT):
                if ti + 1 < NT:
                    gated(ti + 1)
                ac.wait_ge(O_D.sem, O_D.at(ti, "agg"))
                f(rstd[:, 0:1], mv[:, 1:2], ACT.Sqrt, bias=eps[:, 0:1]).then_inc(O_A, 1)

        @block.tensor
        def _(pe):
            mm, tr = nc.tensor.matmul, nc.tensor.transpose

            pe.wait_ge(s_const, 2)
            for ti in range(NT + 1):
                b, r = ti % 2, rows(ti)
                pe.wait_ge(s_ln.sem, s_ln.at(ti, "xhat"))
                if ti >= 2:
                    pe.wait_ge(s_hf, KD * (ti - 1))
                for hf in range(2):
                    for k in range(4):
                        last = tr(ps[:, 2 * b + hf, k * P:k * P + r], xh[b][0:r, (4 * hf + k) * P:(4 * hf + k + 1) * P],
                                  ident[0:r, 0:r])
                    last.then_inc(s_tp, 1)

            def emptied(job):
                kind, j = job
                if kind == "gl":
                    pe.wait_ge(s_gelu, j + 1)
                elif kind == "lx":
                    pe.wait_ge(s_lx, j + 1)
                elif kind in ("gr", "gi"):
                    pe.wait_ge(LRU_A.sem, LRU_A.at(j, kind))
                elif kind in ("z", "r", "k", "v"):
                    pe.wait_ge(s_uev, SHIFTED.index(job) + 1)
                elif kind == "dec":
                    pe.wait_ge(PR_A.sem, PR_A.at(j, "sg"))
                elif kind == "aa":
                    pe.wait_ge(PR_A.sem, PR_A.at(j, "a"))
                elif kind == "ss":
                    pe.wait_ge(PR_D.sem, PR_D.at(j, "ssm"))
                else:
                    pe.wait_ge(PR_D.sem, PR_D.at(j, "bon"))

            pe.wait_ge(s_hl, NT + 1)
            pe.wait_ge(s_zcol, 2)
            for n, job in enumerate(JOBS):
                kind, j = job
                if n >= 2:
                    emptied(JOBS[n - 2])
                if job in WTILES:
                    w = WTILES.index(job)
                    width = cols(kind, j)[1]
                    pe.wait_ge(s_wlo, w + 1)
                    wt = wbuf[w % 2]
                    for k in range(KD):
                        for a_, b_ in ((0, 0), (0, 1), (1, 0)):
                            for q in range(3):
                                last = mm(bank(job, width)[:, q, :], wt[a_][:, k, 0:width], hT[b_][:, k, q * SEG:(q + 1) * SEG],
                                          start=k == 0 and a_ == b_, stop=k == KD - 1 and a_ == 1)
                else:
                    if kind in ("gr", "gi"):
                        pe.wait_ge(s_gate_w, 64)
                        pe.wait_ge(LRU_D.sem, LRU_D.at(j, "c3"))
                        lhs, rhs = (wrg if kind == "gr" else wig)[:, j, :], XC
                    elif kind in ("dec", "aa"):
                        pe.wait_ge(s_zact, 1)
                        pe.wait_ge(s_prm, 16 * 16)
                        h = slice(0, 64) if kind == "dec" else slice(64, 128)
                        lhs, rhs = wlr[h, j * P:(j + 1) * P], Z0[h, :]
                    elif kind == "ss":
                        pe.wait_ge(PR_A.sem, PR_A.at(j, "sq"))
                        pe.wait_ge(s_const_done, 1)
                        lhs, rhs = blk.rearrange("p h c -> p (h c)"), T7
                    else:
                        pe.wait_ge(PR_D.sem, PR_D.at(j, "q"))
                        lhs, rhs = blk.rearrange("p h c -> p (h c)"), T7
                    for q in range(3):
                        last = mm(bank(job)[:, q, :], lhs, rhs[:, q * SEG:(q + 1) * SEG], start=True, stop=True)
                last.then_inc(s_job, 1)

            def pair(m, p):
                return m[:, p, :, :].rearrange("p h c -> p (h c)")

            def products(s, k, lefts_rights):
                for p in range(PAIRS):
                    for q, (lh, rh) in enumerate(lefts_rights):
                        last = mm(ps[:, 4 * s + k, p * P:(p + 1) * P], pair(lh, p), pair(rh, p),
                                  start=q == 0, stop=q == len(lefts_rights) - 1)
                last.then_inc(CE[s].sem, 1)

            def transposes(s, k, m):
                for p in range(PAIRS):
                    last = tr(ps[:, 4 * s + k, p * P:(p + 1) * P], pair(m, p), ident)
                last.then_inc(CE[s].sem, 1)

            def scores(s, k, n, c):
                name = "BK"[k]
                pe.wait_ge(CP[s].sem, CP[s].at(n, name))
                for p in range(PAIRS):
                    last = mm(ps[:, 4 * s + k, p * P:(p + 1) * P], pair(slot[s][name + "b"], p),
                              AR[:, p, :, bass.ds(c * CH, CH)], start=True, stop=True)
                last.then_inc(CM[s].sem, 1)

            def turn(slots_, n, c):
                def W(st_, name, m=None):
                    pe.wait_ge(st_.sem, st_.at(n if m is None else m, name))

                if 1 in slots_:
                    scores(1, 0, n, c + 1)
                    scores(1, 1, n, c + 1)
                for s in slots_:
                    W(CD[s], "T0")
                    if not first(n):
                        W(CA[s], "Y", n - 1)
                    transposes(s, 3, slot[s]["Tb"])
                    if s == 0 and not first(n):
                        W(CD[1], "S", n - 1)
                        transposes(1, 2, slot[1]["Sb"])
                for l in LV:
                    for s in slots_:
                        if l == 0:
                            W(CD[s], "Mr")
                            W(CA[s], "D0")
                        else:
                            W(CD[s], f"D{l}")
                        products(s, 0, [(slot[s]["Mb"], slot[s]["Db"])])
                    if l:
                        for s in slots_:
                            if l == 1 and not first(n):
                                W(CB[s], "SB", n - 1)
                            transposes(s, 2, slot[s]["Db"])
                    for s in slots_:
                        if l:
                            W(CA[s], ("Vt", "Bt", "NV", "Kt")[l - 1])
                        if l == 2:
                            W(CD[s], "Nb")
                            products(s, 3, [(slot[s]["Nb"], slot[s]["Vtb"])])
                        else:
                            name = ("V", "B", None, "K", "A")[l]
                            W(CP[s], name)
                            transposes(s, 3, slot[s][name + "b"])
                    for s in slots_:
                        if l == 0:
                            W(CD[s], "Mk")
                        W(CD[s], f"P{l}")
                        if l:
                            W(CA[s], f"T{l}")
                        if l < LV[-1]:
                            products(s, 1, [(slot[s]["Tb"], slot[s]["Pb"])])
                        else:
                            products(s, 1, [(slot[s]["Pb"], slot[s]["Tb"])])
                for s in slots_:
                    W(CD[s], "T5")
                    W(CA[s], "At")
                    products(s, 0, [(slot[s]["Tb"], slot[s]["AN"])])
                for s in slots_:
                    W(CA[s], "X")
                    products(s, 1, [(slot[s]["Xb"], slot[s]["RB"])])
                for s in slots_:
                    if s == 1:
                        scores(0, 0, n + 1, c + 2)
                        W(CD[0], "S")
                        transposes(0, 2, slot[0]["Sb"])
                        scores(0, 1, n + 1, c + 2)
                        W(CB[0], "SB")
                    elif first(n):
                        pe.wait_ge(s_z0, 10)
                    else:
                        W(CB[1], "SB", n - 1)
                    W(CA[s], "Z")
                    W(CD[s], "Q")
                    products(s, 3, [(slot[s]["Zb"], slot[s]["RB"]), (slot[s]["Vtb"], slot[s]["RK"]),
                                    (SB[s], slot[s]["QG"])])

            pe.wait_ge(PR_D.sem, PR_D.at(PAIRS - 1, "at"))
            scores(0, 0, 0, 0)
            scores(0, 1, 0, 0)
            turn((0, 1), 0, 0)
            with pe.Fori(1, (NCH - 1) // 2) as i:
                turn((0, 1), i, i * 2)
            turn((0,), (NCH - 1) // 2, NCH - 1)

            pe.wait_ge(s_wgu, 32)
            pe.wait_ge(s_zg, 2)
            for s in range(2):
                pe.wait_ge(CA[s].sem, CA[s].at((NCH - 1) // 2 - s, "Y"))
            sums = blk.rearrange("p h c -> p (h c)")
            def mean(n):
                if n >= 2:
                    pe.wait_ge(GN_C, n - 1)
                mm(ps[:, 4 * (n % 2), :], sums, AR[:, n // 2, 1, CH + (n % 2) * 512:CH + (n % 2) * 512 + 512],
                   start=True, stop=True).then_inc(GN_M, 1)

            def variance(n):
                pe.wait_ge(GN_S, n + 1)
                if n >= 2:
                    pe.wait_ge(GN_A.sem, GN_A.at(n - 2, "ln"))
                mm(ps[:, 4 * (n % 2) + 1, :], sums, gsq[n % 2], start=True, stop=True).then_inc(GN_V, 1)

            def gates_(n):
                p, B = n // 2, 4 * (n % 2)
                cs = slice((n % 2) * 512, (n % 2) * 512 + 512)
                if n >= 2:
                    pe.wait_ge(GN_D.sem, GN_D.at(n - 2, "g"))
                mm(ps[:, B + 2, :], wgu[:, 0, p * P:(p + 1) * P], ZG[:, 0, cs], start=True, stop=False)
                mm(ps[:, B + 2, :], wgu[0:32, 1, p * P:(p + 1) * P], ZG[0:32, 1, cs], start=False, stop=True).then_inc(GN_G, 1)

            mean(0)
            gates_(0)
            for n in range(1, 2 * PAIRS):
                mean(n)
                variance(n - 1)
                gates_(n)
            variance(2 * PAIRS - 1)

            def router(ti):
                b = ti % 2
                if ti == 0:
                    pe.wait_ge(s_wr, 64)
                pe.wait_ge(F_P.sem, F_P.at(ti, "bias"))
                if ti:
                    pe.wait_ge(F_C.sem, F_C.at(ti - 1, "t1"))
                    pe.wait_ge(F_L, ti)
                for hf in range(2):
                    for k in range(4):
                        last = tr(ps[:, 4 + hf, k * P:(k + 1) * P], h1[b][:, (4 * hf + k) * P:(4 * hf + k + 1) * P], ident)
                    last.then_inc(F_E.sem, 1)
                pe.wait_ge(F_C.sem, F_C.at(ti, "t1"))
                for k in range(KD):
                    last = mm(ps[:, 6, 0:NG + NE], h1T[b][:, k, :], wr[:, k, :], start=k == 0, stop=k == KD - 1)
                last.then_inc(F_E.sem, 1)

            pe.wait_ge(GN_D.sem, GN_D.at(2 * PAIRS - 1, "g"))
            pe.wait_ge(s_wo, 16)
            pe.wait_ge(s_yl, 16)
            for ti in range(NT):
                b = ti % 2
                if ti >= 2:
                    pe.wait_ge(F_D.sem, F_D.at(ti - 2, "res1"))
                for hf in range(2):
                    for k in range(KD):
                        y = AR[:, k, 1, CH + ti * P:CH + (ti + 1) * P] if k < PAIRS else yl[:, k - PAIRS, ti * P:(ti + 1) * P]
                        last = mm(ps[:, 2 * b + hf, :], y, wo[:, k, hf * 512:(hf + 1) * 512], start=k == 0, stop=k == KD - 1)
                    last.then_inc(F_O.sem, 1)
                if ti:
                    router(ti - 1)
            router(NT - 1)
            pe.wait_ge(s_rt_oh, 1)
            mm(ps[:, 0, 0:NT * NE], ltri, OS.rearrange("p a b -> p (a b)"), start=True, stop=False)
            mm(ps[:, 0, 0:NT * NE], ones, OP[:, 0:NT, :].rearrange("p a b -> p (a b)"), start=False, stop=True)
            mm(ps[:, 1, 0:NE], ones, OP[:, NT, :], start=True, stop=True).then_inc(s_rte, 1)

            def rows_in(s, n):
                pe.wait_ge(s_xg[s], (n - s) * 8 + 16)
                if not first(n):
                    pe.wait_ge(V_X, n)
                xv = xg[s].rearrange("p (c k) -> p k c", k=KD)
                for k in range(KD):
                    last = tr(ps[:, k // 4, (k % 4) * P:(k % 4 + 1) * P], xv[:, k, :], ident)
                last.then_inc(E_X, 1)

            def split_product(out_, x, w, kk, cs):
                for k in range(kk):
                    mm(out_, x[0][:, k, :], w[0][:, k, cs], start=k == 0, stop=False)
                    mm(out_, x[0][:, k, :], w[1][:, k, cs], start=False, stop=False)
                for k in range(kk):
                    last = mm(out_, x[1][:, k, :], w[0][:, k, cs], start=False, stop=k == kk - 1)
                return last

            def gate(s, n):
                pe.wait_ge(V_X, n + 1)
                pe.wait_ge(s_lo[0], n + 1)
                if not first(n):
                    pe.wait_ge(A_S, n)
                split_product(ps[:, 2, :], xT[s], wsp[s][0], KD, slice(0, FE)).then_inc(E_G, 1)

            def up(s, n):
                pe.wait_ge(s_lo[1], n + 1)
                if not first(n):
                    pe.wait_ge(V_M, n)
                split_product(ps[:, 3, :], xT[s], wsp[s][1], KD, slice(0, FE)).then_inc(E_U, 1)

            def turned(s, n):
                pe.wait_ge(V_M, n + 1)
                if not first(n):
                    pe.wait_ge(V_H, n)
                hv = hd[s].rearrange("p (c k) -> p k c", k=KF)
                for k in range(KF):
                    last = tr(ps[:, 4, k * P:(k + 1) * P], hv[:, k, :], ident)
                last.then_inc(E_H, 1)

            def down(s, n):
                pe.wait_ge(V_H, n + 1)
                pe.wait_ge(s_lo[2], n + 1)
                if not first(n):
                    pe.wait_ge(A_Y, n)
                    pe.wait_ge(V_Y, n)
                for hf in range(2):
                    last = split_product(ps[:, 5 + hf, :], hTe[s], wsp[s][2], KF, slice(hf * 512, (hf + 1) * 512))
                last.then_inc(E_Y, 1)

            def turn(s, n, more=True):
                gate(s, n)
                if not first(n):
                    turned(1 - s, n - 1)
                if more:
                    rows_in(1 - s, n + 1)
                up(s, n)
                if not first(n):
                    down(1 - s, n - 1)

            rows_in(0, 0)
            turn(0, 0)
            turn(1, 1)
            with pe.Fori(1, NE // 2 - 1) as i:
                turn(0, i * 2)
                turn(1, i * 2 + 1)
            turn(0, NE - 2)
            turn(1, NE - 1, False)
            turned(1, NE - 1)
            down(1, NE - 1)
            n_over = pe.value_load(novi[0:1, 0:1], min_val=0, max_val=OVER)
            for j in range(OVER):
                with pe.If(n_over > j):
                    s, n = j % 2, NE + j
                    rows_in(s, n)
                    gate(s, n)
                    up(s, n)
                    turned(s, n)
                    down(s, n)


_INS = ["x", "meta", "ln0_g", "ln0_b", "w_in", "mu_shift", "w0", "w_decay_up", "a0", "w_a_up", "w_g_up", "k_k", "k_a", "r_k",
        "gn_g", "gn_b", "conv_w", "conv_b", "w_rg", "b_rg", "w_ig", "b_ig", "lru_lambda", "w_out", "ln1_g", "ln1_b",
        "w_router_grp", "b_router_grp", "w_router_exp", "b_router_exp", "w_exp_gate", "w_exp_up", "w_exp_down",
        "ln2_g", "ln2_b"]


def kernel(**inputs):
    import numpy as _np
    import concourse.bacc as _bacc
    from concourse import mybir as _mybir
    from concourse.bass_utils import run_bass_kernel_spmd as _run

    nc = _bacc.Bacc("TRN2", target_bir_lowering=False, num_devices=1)
    f32, i32 = _mybir.dt.float32, _mybir.dt.int32
    arrays, args = {}, {}
    for name in _INS:
        v = _np.ascontiguousarray(inputs[name])
        arrays[f"in_{name}_dram"] = v
        args[name] = nc.dram_tensor(f"in_{name}_dram", v.shape, _mybir.dt.from_np(v.dtype), kind="ExternalInput").ap()
    out = nc.dram_tensor("out_dram", (1, SEQ, D), f32, kind="ExternalOutput").ap()
    scratch = {
        "h": nc.dram_tensor("scr_h", (SEQ, D), f32).ap(),
        "ylru": nc.dram_tensor("scr_ylru", (4 * P, SEQ), f32).ap(),
        "h1": nc.dram_tensor("scr_h1", (SEQ, D), f32).ap(),
        "tok": nc.dram_tensor("scr_tok", (NBLK * CAP, 1), i32).ap(),
        "y": nc.dram_tensor("scr_y", (NBLK * CAP, D), f32).ap(),
    }
    build(nc, args, out, scratch)
    r = _run(nc, [arrays], core_ids=[0])
    return r.results[0]["out_dram"]
```
